# Optimizing a Trainium2 kernel written in Bass

```python
import math
import jax, jax.numpy as jnp
from jax import lax
import numpy as np

D_MODEL = 1024
BATCH = 1
SEQ = 512
DEPTH = 1
DEC_BATCH = 1
DEC_SEQ = 512
PAST_LEN = 128

CONV_WIDTH = D_MODEL // 2
HYENA_WIDTH = D_MODEL // 2
CONV_KERNEL = 31
SHORT_KERNEL = 3
POS_EMB_DIM = 33
POS_BANDS = (POS_EMB_DIM - 1) // 2
FILTER_FFN = 64
FAST_DECAY_PCT = 0.3
SLOW_DECAY_PCT = 1.5
DECAY_TARGET = 1e-2
N_EXPERTS = 16
EXPERT_D_FF = 1408
CAPACITY_FACTOR = 2
PROJ_COLS = 2 * CONV_WIDTH + 3 * HYENA_WIDTH + 2 * D_MODEL
NORM_EPS = 1e-6
LN_EPS = 1e-5

kernel_name = 'hybrid_conformer_hyena_ec_moe_encoder'

def rmsnorm(x, g):
    xf = x.astype(jnp.float32)
    y = xf * lax.rsqrt(jnp.mean(xf * xf, axis=-1, keepdims=True) + NORM_EPS)
    return (y * g.astype(jnp.float32)).astype(x.dtype)

def layernorm(x, g, b):
    xf = x.astype(jnp.float32)
    mu = jnp.mean(xf, axis=-1, keepdims=True)
    var = jnp.mean(jnp.square(xf - mu), axis=-1, keepdims=True)
    y = (xf - mu) * lax.rsqrt(var + LN_EPS)
    return (y * g.astype(jnp.float32) + b.astype(jnp.float32)).astype(x.dtype)

def depthwise_conv(x, w, b):
    k = w.shape[0]
    y = lax.conv_general_dilated(
        x, w[:, None, :].astype(x.dtype), window_strides=(1,),
        padding=[(k // 2, k // 2)],
        dimension_numbers=('NWC', 'WIO', 'NWC'),
        feature_group_count=x.shape[-1])
    return y + b

def hyena_pos_features(L):
    t = jnp.linspace(0.0, 1.0, L, dtype=jnp.float32)[:, None]
    w = 2.0 * math.pi * jnp.arange(L, dtype=jnp.float32)[:, None] / L
    bands = jnp.linspace(1e-4, POS_BANDS - 1, POS_BANDS, dtype=jnp.float32)[None, :]
    return jnp.concatenate([t, jnp.cos(bands * w), -jnp.sin(bands * w)], axis=-1)

def hyena_filter_spectrum(L, w1, b1, w2, b2, w3, b3, w4, freq):
    z = hyena_pos_features(L)
    f32 = lambda a: a.astype(jnp.float32)
    fr = f32(freq)
    h = jnp.sin(fr * (z @ f32(w1) + f32(b1)))
    h = jnp.sin(fr * (h @ f32(w2) + f32(b2)))
    h = jnp.sin(fr * (h @ f32(w3) + f32(b3)))
    h = (h @ f32(w4)).reshape(L, 2, HYENA_WIDTH)
    t = jnp.linspace(0.0, 1.0, L, dtype=jnp.float32)[:, None]
    max_decay = math.log(DECAY_TARGET) / FAST_DECAY_PCT
    min_decay = math.log(DECAY_TARGET) / SLOW_DECAY_PCT
    deltas = jnp.linspace(min_decay, max_decay, HYENA_WIDTH, dtype=jnp.float32)
    decay = jnp.exp(-t * jnp.abs(deltas)[None, :])
    h = h * decay[:, None, :]
    h = h / jnp.sum(jnp.abs(h), axis=(0, 1), keepdims=True)
    h_fwd, h_bwd = h[:, 0], h[:, 1]
    kern = jnp.concatenate([h_fwd, jnp.zeros((1, HYENA_WIDTH), jnp.float32), h_bwd[:L - 1][::-1]], axis=0)
    return jnp.fft.rfft(kern, n=2 * L, axis=0)

def long_conv(u, k_fft):
    L = u.shape[1]
    u_f = jnp.fft.rfft(u.astype(jnp.float32), n=2 * L, axis=1)
    y = jnp.fft.irfft(u_f * k_fft[None], n=2 * L, axis=1)[:, :L]
    return y.astype(u.dtype)

def expert_choice_moe(h, router_w, w_gate, w_up, w_down):
    B, L, D = h.shape
    T = B * L
    tok = h.reshape(T, D)
    logits = (tok @ router_w).astype(jnp.float32)
    aff = jax.nn.softmax(logits, axis=-1)
    cap = max(1, min(T, CAPACITY_FACTOR * T // N_EXPERTS))
    gate, idx = lax.top_k(aff.T, cap)
    xs = tok[idx]
    hid = jax.nn.silu(jnp.einsum('ecd,edf->ecf', xs, w_gate)) * jnp.einsum('ecd,edf->ecf', xs, w_up)
    ye = jnp.einsum('ecf,efd->ecd', hid, w_down) * gate[..., None].astype(h.dtype)
    out = jnp.zeros_like(tok).at[idx.reshape(-1)].add(ye.reshape(-1, D))
    return out.reshape(B, L, D)

def hybrid_layer(x, norm1_g, w_in, b_in, conv_dw_w, conv_dw_b, conv_ln_g, conv_ln_b,
                 conv_w_out, conv_b_out, hy_short_w, hy_short_b, hy_f_w1, hy_f_b1,
                 hy_f_w2, hy_f_b2, hy_f_w3, hy_f_b3, hy_f_w4, hy_f_freq, hy_skip,
                 hy_w_out, hy_b_out, w_o, norm2_g, router_w, exp_w_gate, exp_w_up, exp_w_down):
    L = x.shape[1]
    h = rmsnorm(x, norm1_g)
    z = jnp.einsum('bld,dc->blc', h, w_in) + b_in
    a_in, hy_in, g_in = jnp.split(z, [2 * CONV_WIDTH, 2 * CONV_WIDTH + 3 * HYENA_WIDTH], axis=-1)
    a = a_in[..., :CONV_WIDTH] * jax.nn.sigmoid(a_in[..., CONV_WIDTH:])
    a = depthwise_conv(a, conv_dw_w, conv_dw_b)
    a = jax.nn.silu(layernorm(a, conv_ln_g, conv_ln_b))
    y_a = a @ conv_w_out + conv_b_out
    u = depthwise_conv(hy_in, hy_short_w, hy_short_b)
    x0, x1, v = jnp.split(u, 3, axis=-1)
    k_fft = hyena_filter_spectrum(L, hy_f_w1, hy_f_b1, hy_f_w2, hy_f_b2, hy_f_w3, hy_f_b3, hy_f_w4, hy_f_freq)
    v = x1 * v
    v = long_conv(v, k_fft) + hy_skip * v
    y_b = (x0 * v) @ hy_w_out + hy_b_out
    g_a, g_b = jnp.split(jax.nn.sigmoid(g_in), 2, axis=-1)
    x = x + (g_a * y_a + g_b * y_b) @ w_o
    x = x + expert_choice_moe(rmsnorm(x, norm2_g), router_w, exp_w_gate, exp_w_up, exp_w_down)
    return x

def setup_inputs(seed: int = 0) -> dict:
    key = jax.random.key(seed)
    ks = iter(jax.random.split(key, 40))
    D, Da, Db, E, F = D_MODEL, CONV_WIDTH, HYENA_WIDTH, N_EXPERTS, EXPERT_D_FF

    def nrm(shape, scale):
        return jax.random.normal(next(ks), shape, jnp.float32) * scale

    return {
        'x_prompt': nrm((BATCH, SEQ, D), 1.0),
        'x_sample': nrm((DEC_BATCH, DEC_SEQ, D), 1.0),
        'norm1_g': 1.0 + nrm((DEPTH, D), 0.02),
        'w_in': nrm((DEPTH, D, PROJ_COLS), D ** -0.5),
        'b_in': nrm((DEPTH, PROJ_COLS), 0.01),
        'conv_dw_w': nrm((DEPTH, CONV_KERNEL, Da), CONV_KERNEL ** -0.5),
        'conv_dw_b': nrm((DEPTH, Da), 0.01),
        'conv_ln_g': 1.0 + nrm((DEPTH, Da), 0.02),
        'conv_ln_b': nrm((DEPTH, Da), 0.01),
        'conv_w_out': nrm((DEPTH, Da, D), Da ** -0.5),
        'conv_b_out': nrm((DEPTH, D), 0.01),
        'hy_short_w': nrm((DEPTH, SHORT_KERNEL, 3 * Db), SHORT_KERNEL ** -0.5),
        'hy_short_b': nrm((DEPTH, 3 * Db), 0.01),
        'hy_f_w1': nrm((DEPTH, POS_EMB_DIM, FILTER_FFN), POS_EMB_DIM ** -0.5),
        'hy_f_b1': nrm((DEPTH, FILTER_FFN), 0.1),
        'hy_f_w2': nrm((DEPTH, FILTER_FFN, FILTER_FFN), FILTER_FFN ** -0.5),
        'hy_f_b2': nrm((DEPTH, FILTER_FFN), 0.1),
        'hy_f_w3': nrm((DEPTH, FILTER_FFN, FILTER_FFN), FILTER_FFN ** -0.5),
        'hy_f_b3': nrm((DEPTH, FILTER_FFN), 0.1),
        'hy_f_w4': nrm((DEPTH, FILTER_FFN, 2 * Db), FILTER_FFN ** -0.5),
        'hy_f_freq': 1.0 + nrm((DEPTH, FILTER_FFN), 0.05),
        'hy_skip': nrm((DEPTH, Db), 1.0),
        'hy_w_out': nrm((DEPTH, Db, D), Db ** -0.5),
        'hy_b_out': nrm((DEPTH, D), 0.01),
        'w_o': nrm((DEPTH, D, D), D ** -0.5),
        'norm2_g': 1.0 + nrm((DEPTH, D), 0.02),
        'router_w': nrm((DEPTH, D, E), D ** -0.5),
        'exp_w_gate': nrm((DEPTH, E, D, F), D ** -0.5),
        'exp_w_up': nrm((DEPTH, E, D, F), D ** -0.5),
        'exp_w_down': nrm((DEPTH, E, F, D), F ** -0.5),
        'norm_f_g': 1.0 + nrm((D,), 0.02),
    }

def reference(x_prompt, x_sample, norm1_g, w_in, b_in, conv_dw_w, conv_dw_b, conv_ln_g,
              conv_ln_b, conv_w_out, conv_b_out, hy_short_w, hy_short_b, hy_f_w1, hy_f_b1,
              hy_f_w2, hy_f_b2, hy_f_w3, hy_f_b3, hy_f_w4, hy_f_freq, hy_skip, hy_w_out,
              hy_b_out, w_o, norm2_g, router_w, exp_w_gate, exp_w_up, exp_w_down, norm_f_g):
    def trunk(x):
        for i in range(DEPTH):
            x = hybrid_layer(
                x, norm1_g[i], w_in[i], b_in[i], conv_dw_w[i], conv_dw_b[i], conv_ln_g[i],
                conv_ln_b[i], conv_w_out[i], conv_b_out[i], hy_short_w[i], hy_short_b[i],
                hy_f_w1[i], hy_f_b1[i], hy_f_w2[i], hy_f_b2[i], hy_f_w3[i], hy_f_b3[i],
                hy_f_w4[i], hy_f_freq[i], hy_skip[i], hy_w_out[i], hy_b_out[i], w_o[i],
                norm2_g[i], router_w[i], exp_w_gate[i], exp_w_up[i], exp_w_down[i])
        return rmsnorm(x, norm_f_g)

    y_prompt = trunk(x_prompt)
    y_sample = trunk(x_sample)
    return (y_prompt, y_sample)


_drawn_inputs = setup_inputs


def setup_inputs(seed=0):
    import zlib

    import numpy as np

    out = dict(_drawn_inputs(seed))
    spreads = {}
    factors = {'norm1_g': 2.69,
     'b_in': 4.506,
     'conv_dw_b': 17.976,
     'conv_ln_g': 16.257,
     'conv_ln_b': 39.128,
     'conv_b_out': 34.919,
     'hy_short_b': 4.666,
     'hy_f_b1': 4.821,
     'hy_f_b2': 4.577,
     'hy_f_b3': 4.121,
     'hy_f_freq': 7.501,
     'hy_b_out': 33.261,
     'norm2_g': 3.578,
     'norm_f_g': 7.625}
    for name, (base, spread) in spreads.items():
        noise = np.random.default_rng([zlib.crc32(name.encode()), seed]).standard_normal(out[name].shape)
        drawn = base * np.exp(spread * noise) if base else spread * noise
        out[name] = __import__('jax').numpy.asarray(drawn.astype(out[name].dtype))
    for name, factor in factors.items():
        out[name] = (out[name] * factor).astype(out[name].dtype)
    return out
```

```python
from contextlib import ExitStack
import math

import concourse.bass as bass
from concourse import mybir

P = 128
F32 = mybir.dt.float32
F32R = mybir.dt.float32r
U32 = mybir.dt.uint32
ALU = mybir.AluOpType
ACT = mybir.ActivationFunctionType
AX_X = mybir.AxisListType.X
KB = 1024
SBUF_BASE = 16 * KB + 128

TWO_PI_HEAD = 6.28125
TWO_PI_TAIL = 2.0 * math.pi - TWO_PI_HEAD
ROUNDER = 1.5 * 2.0 ** 23


def small_columns(D, DC, PROJ, TAPS, SHORT, E):
    widths = [
        ("b_in", PROJ // P), ("dw_w", DC // P * TAPS), ("dw_b", DC // P), ("ln_g", DC // P), ("ln_b", DC // P),
        ("conv_b", D // P), ("short_w", 3 * DC // P * SHORT), ("short_b", 3 * DC // P), ("hy_b", D // P),
        ("norm1", D // P), ("cos_half", DC // P), ("sin_half", DC // P), ("router", D // P * E), ("ident", P),
    ]
    at, where = 0, {}
    for name, width in widths:
        where[name] = (at, width)
        at += width
    return where, at


def hybrid_encoder_kernel(
    nc: bass.Bass,
    x_prompt: bass.AP,
    x_sample: bass.AP,
    small: bass.AP,
    ffn: bass.AP,
    ffn_w4: bass.AP,
    zpos: bass.AP,
    decay: bass.AP,
    cosine: bass.AP,
    sine: bass.AP,
    w_in: bass.AP,
    conv_w_out: bass.AP,
    hy_w_out: bass.AP,
    w_o: bass.AP,
    hy_skip: bass.AP,
    norm2_g: bass.AP,
    norm_f_g: bass.AP,
    w_gate: bass.AP,
    w_up: bass.AP,
    w_down: bass.AP,
    y_prompt: bass.AP,
    y_sample: bass.AP,
):
    L, D = x_prompt.shape
    PROJ = w_in.shape[1]
    DC = conv_w_out.shape[0]
    E, _, F = w_gate.shape
    FFN = ffn.shape[0]
    TAPS, SHORT = 31, 3
    PAD = TAPS // 2
    CAP = 2 * L // E
    KD, KC, LT = D // P, DC // P, L // P
    TT = 2 * LT
    where, small_n = small_columns(D, DC, PROJ, TAPS, SHORT, E)
    assert L == 512 and D == 1024 and DC == 512 and 2 * CAP == P and E == 16

    x0_dram = nc.dram_tensor("x0_spill", [KC, P, 2 * L], F32, kind="Internal").ap()
    gate_dram = nc.dram_tensor("gate_spill", [2 * KD, P, 2 * L], F32, kind="Internal").ap()
    tok_dram = nc.dram_tensor("tok_rows", [2 * L, D], F32, kind="Internal").ap()
    acc_dram = nc.dram_tensor("acc_rows", [2 * L, D], F32, kind="Internal").ap()

    ctx = ExitStack()
    with ctx:
        def at(name, kib, shape, dt=F32):
            return nc.alloc_sbuf_tensor_at(name, shape, dt, offset=SBUF_BASE + int(kib * KB))

        SM = at("small_params", 0, [P, small_n])
        IDENT = SM[:, where["ident"][0]:where["ident"][0] + P]
        ONES = at("ones", 2.5, [P, P])
        ONES_R = at("ones_r", 3.0, [P, P], F32R)
        SUMSQ = at("sum_squares", 3.5, [P, TT])
        RSTD = at("rstd", 3.5625, [P, TT])
        SUMSQ2 = at("sum_squares2", 3.625, [P, TT, 2])
        RSTD2 = at("rstd2", 3.75, [P, TT])
        SUMSQF = at("sum_squares_f", 3.8125, [P, TT])
        RSTDF = at("rstd_f", 3.875, [P, TT])
        AFF = at("affinity", 4.0, [P, TT, E])
        RSUM = at("softmax_sum", 4.5, [P, TT])
        RMAX = at("softmax_max", 4.5625, [P, TT])
        TOPV = at("top_values", 4.625, [48, CAP])
        TOPI = at("top_index", 4.875, [48, CAP], U32)
        TOPF = at("top_index_float", 5.125, [48, CAP])
        PAIR = at("slots_of_experts", 5.375, [E, 2, P])
        GATES = at("slot_gates", 6.375, [P, E])
        SLOTS = at("slot_rows", 6.4375, [P, E], U32)
        NEXT_ROWS = at("rows_to_gather", 6.5, [P, 1], U32)
        DONE_ROWS = at("rows_to_scatter", 6.53125, [P, 1], U32)
        CUR_GATE = at("gate_of_slot", 6.5625, [P, 1])
        EPS = at("eps", 6.59375, [P, 2])

        HT = (at("hT_hi", 8, [P, KD, 2 * L], F32R), at("hT_lo", 40, [P, KD, 2 * L], F32R))
        X = at("x_rows", 120, [P, TT, D])
        RAW = [at(f"w_raw{j}", 72 + 4 * j, [P, KD, P]) for j in range(4)]
        SPLIT = [(at(f"w_hi{j}", 88 + 8 * j, [P, KD, P], F32R), at(f"w_lo{j}", 92 + 8 * j, [P, KD, P], F32R))
                 for j in range(4)]
        VT = (at("v_rows_hi", 120, [P, TT, DC], F32R), at("v_rows_lo", 136, [P, TT, DC], F32R))
        APAD = at("a_padded", 152, [P, KC, 2, L + 2 * PAD])
        CONV = at("conv_sum", 169, [P, KC, 2, L])
        FF = at("ffn_params", 185, [FFN, ffn.shape[1]])
        ZP = at("zpos", 190.5, [zpos.shape[0], L])
        FARG = at("sin_argument", 192.5, [FFN, L])
        FK = at("sin_turns", 194.5, [FFN, L])
        FH = [at("filter_h1", 196.5, [FFN, L]), at("filter_h2", 198.5, [FFN, L]), at("filter_h3", 205.5, [FFN, L])]
        SQJUNK = [at(f"square_out{i}", 185 - 16 + 4 * i, [P, D]) for i in range(2)]
        SIG = [at(f"sigmoid{i}", 197.5 + 4 * i, [P, 2, L]) for i in range(2)]
        ZPAD = [at(f"z_padded{j}", 185 + 4.0625 * j, [P, 2, L + 2]) for j in range(3)]
        SHORTS = [at(f"short_conv{i}", 197.25 + 4 * i, [P, 2, L]) for i in range(2)]
        GSTAGE = [at(f"gate_stage{j}", 185 + 4 * j, [P, 2, L]) for j in range(4)]
        COS = (at("cos_hi", 8, [P, LT, L], F32R), at("cos_lo", 16, [P, LT, L], F32R))
        SIN = (at("sin_hi", 24, [P, LT, L], F32R), at("sin_lo", 32, [P, LT, L], F32R))
        TABLE_RAW = [at("cos_raw", 40, [P, LT, L]), at("sin_raw", 48, [P, LT, L])]
        DECAY = at("decay", 56, [P, LT, DC])
        W4 = at("w4", 64, [FFN, 2 * DC])
        HF = at("filter_taps", 68, [P, 2 * DC])
        HABS = at("filter_abs", 72, [P, 2 * DC])
        HSUM = at("filter_even_odd", 76, [P, 2 * DC])
        NORM = at("filter_norm", 80, [P, DC])
        SKIP = at("skip", 82, [P, DC])
        EO = (at("even_odd_hi", 88, [P, LT, 2, DC], F32R), at("even_odd_lo", 104, [P, LT, 2, DC], F32R))
        KR = at("filter_re", 40, [P, LT, DC])
        KI = at("filter_im", 48, [P, LT, DC])
        KTMP = [at(f"spectrum_tmp{i}", 84 + 2 * i, [P, DC]) for i in range(2)]
        YRE = (at("y_re_hi", 88, [P, LT, DC], F32R), at("y_re_lo", 96, [P, LT, DC], F32R))
        YIM = (at("y_im_hi", 104, [P, LT, DC], F32R), at("y_im_lo", 112, [P, LT, DC], F32R))
        YT = [at(f"product{i}", 185 + 2 * i, [P, DC]) for i in range(4)]
        X0 = at("x0", 193, [P, KC, L])
        UY = [at(f"x0_times_y{i}", 201 + 2 * i, [P, L]) for i in range(2)]
        UB = (at("hyena_out_hi", 56, [P, KC, 2, L], F32R), at("hyena_out_lo", 72, [P, KC, 2, L], F32R))
        LNSQ = at("ln_square", 185, [P, 2, L])
        LNRS = at("ln_rstd", 189, [P, 2, L])
        LNSR = at("ln_square_r", 193, [P, 2, 2, L], F32R)
        AT = (at("conv_out_hi", 152, [P, KC, 2, L], F32R), at("conv_out_lo", 169, [P, KC, 2, L], F32R))
        OUT_RAW = [at(f"wout_raw{j}", 120 + 2 * j, [P, KC, P]) for j in range(4)]
        OUT_SPLIT = [(at(f"wout_hi{j}", 128 + 4 * j, [P, KC, P], F32R), at(f"wout_lo{j}", 130 + 4 * j, [P, KC, P], F32R))
                     for j in range(4)]
        GIN = [at(f"gate_in{j}", 185 + 4 * j, [P, 2, L]) for j in range(4)]
        MT = (at("mixed_hi", 8, [P, KD, 2, L], F32R), at("mixed_lo", 88, [P, KD, 2, L], F32R))
        WO_RAW = [at(f"wo_raw{j}", 120 + 2 * j, [P, L]) for j in range(4)]
        WO_SPLIT = [(at(f"wo_hi{j}", 128 + 4 * j, [P, L], F32R), at(f"wo_lo{j}", 130 + 4 * j, [P, L], F32R))
                    for j in range(4)]
        X2 = at("x2_rows", 40, [P, TT, D])
        XRES = [at(f"x_again{i}", 144 + 2 * i, [P, 512]) for i in range(4)]
        TOK = [at(f"tok_rows{i}", 152 + 4 * i, [P, D]) for i in range(2)]
        TOKT = [at(f"tok_T{i}", 160 + 4 * i, [P, KD, P]) for i in range(2)]
        NG2 = at("norm2_g_all", 168, [P, D])
        JUNK2 = [at(f"square2_out{i}", 172 + 2 * i, [P, 512]) for i in range(1)]
        ROWS = [at(f"affinity_rows{i}", 144 + 2 * i, [48, L]) for i in range(3)]
        raw_at = [72, 80, 174, 182, 190, 198, 8, 16, 24]
        RAWS = len(raw_at)
        EW = [at(f"expert_raw{j}", k, [P, 4, 512]) for j, k in enumerate(raw_at)]
        SPLITS = 3
        ES = [(at(f"expert_hi{j}", 88 + 16 * j, [P, 4, 512], F32R), at(f"expert_lo{j}", 96 + 16 * j, [P, 4, 512], F32R))
              for j in range(SPLITS)]
        XS = at("slot_tokens", 136, [P, D])
        XST = (at("slot_tokens_T_hi", 140, [P, KD, P], F32R), at("slot_tokens_T_lo", 144, [P, KD, P], F32R))
        SG = at("silu_gate", 148, [P, 512])
        HID = at("hidden", 150, [P, 512])
        HIDT = (at("hidden_T_hi", 152, [P, 4, P], F32R), at("hidden_T_lo", 154, [P, 4, P], F32R))
        YE = at("expert_out", 156, [P, D])
        NGF = at("norm_f_g_all", 160, [P, D])
        XF = [at(f"final_rows{i}", 32 + 4 * i, [P, D]) for i in range(8)]
        XO = [at(f"final_out{i}", 64 + 4 * i, [P, D]) for i in range(2)]

        PS = ctx.enter_context(nc.psum_tensor("ps", [P, 8, 512], F32))

        def sem(name):
            return ctx.enter_context(nc.semaphore(name))

        def sems(name, n):
            return [sem(f"{name}{i}") for i in range(n)]

        def col(name, i=0, n=1):
            a = where[name][0]
            return SM[:, a + i:a + i + n]

        small_in, ffn_in, zpos_in = sem("small_in"), sem("ffn_in"), sem("zpos_in")
        x_in = sems("x_in", TT)
        ones_set, pads_set = sem("ones_set"), sem("pads_set")
        a_step, v_step = sem("act_step"), sem("dve_step")
        squares, roots, scaled = sem("squares"), sem("roots"), sem("x_scaled")
        var_ready = sem("var_ready")
        xT_ready, hT_hi, hT_lo = sem("xT_ready"), sem("hT_hi"), sem("hT_lo")
        mlp_mm, mlp_arg, mlp_sin = sem("mlp_mm"), sem("mlp_arg"), sem("mlp_sin")
        w_landed = sems("w_landed", 4)
        w_hi, w_lo, w_used, z_free = sem("w_hi"), sem("w_lo"), sem("w_used"), sem("z_free")
        sig_ready, a_ready = sem("sig_ready"), sem("a_ready")
        z_padded, short_mid, short_done = sem("z_padded"), sem("short_mid"), sem("short_done")
        v_ready, x0_stored = sem("v_ready"), sem("x0_stored")
        vT_mm, vT_hi, vT_lo = sem("vT_mm"), sem("vT_hi"), sem("vT_lo")
        g_ready, g_stored = sem("g_ready"), sems("g_stored", 4)
        conv_done = sem("conv_done")
        table_in, table_hi, table_lo = sem("table_in"), sem("table_hi"), sem("table_lo")
        decay_in, w4_in, skip_in = sem("decay_in"), sem("w4_in"), sem("skip_in")
        taps_mm, taps_ready, abs_ready, norm_mm, eo_sum, eo_hi, eo_lo = (
            sem("taps_mm"), sem("taps_ready"), sem("abs_ready"), sem("norm_mm"), sem("eo_sum"), sem("eo_hi"), sem("eo_lo"))
        taps_free, norm_used = sem("taps_free"), sem("norm_used")
        k_mm, k_ready = sem("k_mm"), sem("k_ready")
        u_mm, u_used, y_val, y_hi, y_lo = sem("u_mm"), sem("u_used"), sem("y_val"), sem("y_hi"), sem("y_lo")
        x0_in, y_mm, uy_ready, ub_hi, ub_lo = sem("x0_in"), sem("y_mm"), sem("uy_ready"), sem("ub_hi"), sem("ub_lo")
        ln_mm, ln_used = sem("ln_mm"), sem("ln_used")
        ln_sq, ln_root, ln_x, at_hi, at_lo = (
            sem("ln_sq"), sem("ln_root"), sem("ln_x"), sem("at_hi"), sem("at_lo"))
        o_landed = sems("o_landed", 4)
        o_hi, o_lo, o_used = sem("o_hi"), sem("o_lo"), sem("o_used")
        gin_in = sems("gin_in", 4)
        m_free, m_val, m_hi, m_lo = sem("m_free"), sem("m_val"), sem("m_hi"), sem("m_lo")
        wo_hi, wo_lo, wo_used = sem("wo_hi"), sem("wo_lo"), sem("wo_used")
        x2_mm, x2_ready, x2_sq = sem("x2_mm"), sem("x2_ready"), sem("x2_sq")
        ng2_in, ngf_in = sem("ng2_in"), sem("ngf_in")
        tok_ready, tok_stored, acc_stored = sem("tok_ready"), sems("tok_stored", 2), sem("acc_stored")
        tokT_mm, tokT_ready, logits_mm = sem("tokT_mm"), sem("tokT_ready"), sem("logits_mm")
        aff_ready, affT_mm, rows_ready, top_ready, pair_ready, slots_mm, slots_ready = (
            sem("aff_ready"), sem("affT_mm"), sem("rows_ready"), sem("top_ready"), sem("pair_ready"),
            sem("slots_mm"), sem("slots_ready"))
        exp_in, exp_out = sem("softmax_shifted"), sem("softmax_exp")
        e_landed = sems("e_landed", RAWS)
        e_hi, e_lo, e_used = sem("e_hi"), sem("e_lo"), sem("e_used")
        rows_next, xs_in, xsT_mm, xsT_hi, xsT_lo = (
            sem("rows_next"), sem("xs_in"), sem("xsT_mm"), sem("xsT_hi"), sem("xsT_lo"))
        silu_ready, hid_ready, hidT_mm, hidT_hi, hidT_lo = (
            sem("silu_ready"), sem("hid_ready"), sem("hidT_mm"), sem("hidT_hi"), sem("hidT_lo"))
        ye_ready, rows_done, added = sem("ye_ready"), sem("rows_done"), sem("rows_added")
        fin_out, fin_stored = sem("fin_ready"), sems("fin_stored", 2)

        block = ctx.enter_context(nc.Block())

        def ge(eng, s, value):
            if not isinstance(value, int) or value > 0:
                eng.wait_ge(s, value)

        class Steps:

            def __init__(self, eng, s):
                self.eng, self.sem, self.n = eng, s, 0

            def did(self, ins):
                ins.then_inc(self.sem, 1)
                self.n += 1

            def wait(self):
                self.eng.wait_ge(self.sem, self.n)

            def then(self, ins):
                self.did(ins)
                self.wait()

        CONV_SEC = (2, 4, lambda i, j: 2 * i + j // 2 + (KC if j % 2 == 0 else 0))
        HYENA_SEC = (KC, 3, lambda i, j: 2 * KC + (KC, 2 * KC, 0)[j] + i)
        GATE_SEC = (4, 4, lambda i, j: 5 * KC + 4 * i + j)
        SECTIONS = [CONV_SEC, HYENA_SEC, GATE_SEC]
        UNITS = [(s, i, j) for s in range(3) for i in range(SECTIONS[s][0]) for j in range(SECTIONS[s][1])]

        def use_of(s, i, j):
            return sum(n for n, width, _ in SECTIONS[:s] if j < width) + i

        def unit_after(s, i, j):
            if i + 1 < SECTIONS[s][0]:
                return s, i + 1, j
            for t in range(s + 1, 3):
                if j < SECTIONS[t][1]:
                    return t, 0, j
            return None

        SPLIT_ORDER = [(0, 0, j) for j in range(4)] + [unit_after(*u) for u in UNITS if unit_after(*u)]

        def split_count(u):
            return SPLIT_ORDER.index(u) + 1

        def used_count(u):
            return UNITS.index(u) + 1

        def unit_before(u):
            return next((v for v in UNITS if unit_after(*v) == u), None)

        def seq_rows(t):
            src = x_prompt if t < LT else x_sample
            return src[(t % LT) * P:(t % LT + 1) * P, :]

        FC = [(a, min(512, F - a)) for a in range(0, F, 512)]
        NF = len(FC)
        GU_UNITS = [(kind, c, kh) for c in range(NF) for kh in range(2) for kind in ("gate", "up")]

        def down_units(c):
            return [("down", c, dh) for dh in range(2)]

        def gu_units(c):
            return [u for u in GU_UNITS if u[1] == c]

        BODY = gu_units(0) + down_units(2) + gu_units(1) + down_units(0) + gu_units(2) + down_units(1)
        NB = len(BODY)
        LEAD = len(gu_units(0))
        SKIPPED = len(down_units(2))

        def src_of(kind, c, k, e):
            a, n = FC[c]
            if kind == "down":
                tiles = n // P
                return w_down[bass.ds(e, 1), a:a + n, k * 512:(k + 1) * 512].rearrange(
                    "o (t p) n -> p (o t) n", p=P), tiles, 512
            w = w_gate if kind == "gate" else w_up
            return w[bass.ds(e, 1), k * 4 * P:(k + 1) * 4 * P, a:a + n].rearrange(
                "o (t p) n -> p (o t) n", p=P), 4, n

        def place_of(kind, c, k):
            a, n = FC[c]
            return (n // P, 512) if kind == "down" else (4, n)

        FIRST = [n for n in range(NB) if not LEAD <= n < LEAD + SKIPPED]
        assert NB % RAWS == 0 and NB % SPLITS == 0

        def pos(n, e):
            return FIRST.index(n) if isinstance(e, int) and e == 0 else n

        def pos_mod(n, e, m):
            return (FIRST.index(n) if isinstance(e, int) and e == 0 else n - SKIPPED) % m

        def slot_of(n, e):
            return pos_mod(n, e, RAWS)

        def landed_of(n, e):
            if isinstance(e, int) and e == 0:
                return 16 * (FIRST.index(n) // RAWS + 1)
            return e * (16 * (NB // RAWS)) + 16 * ((n - SKIPPED) // RAWS + 1)

        def load_expert(sp, n, e, count):
            kind, c, k = BODY[n]
            owner = e - 1 if (kind, c) == ("down", 2) else e
            tiles, width = place_of(kind, c, k)
            src, _, _ = src_of(kind, c, k, owner)
            sp.dma_start(EW[count % RAWS][:, 0:tiles, 0:width], src).then_inc(e_landed[count % RAWS], 16)

        @block.sync
        def _(sp):
            sp.dma_start(FF[:], ffn).then_inc(ffn_in, 16)
            sp.dma_start(ZP[:], zpos).then_inc(zpos_in, 16)
            sp.dma_start(SM[:], small).then_inc(small_in, 16)
            for t in range(TT):
                sp.dma_start(X[:, t, :], seq_rows(t)).then_inc(x_in[t], 16)

            def load_w(s, i, j):
                c = SECTIONS[s][2](i, j)
                sp.dma_start(RAW[j][:], w_in[:, c * P:(c + 1) * P].rearrange("(k p) n -> p k n", p=P)).then_inc(w_landed[j], 16)

            for j in range(4):
                load_w(0, 0, j)
            for s, i, j in UNITS:
                after = unit_after(s, i, j)
                if after:
                    sp.wait_ge(w_lo, split_count((s, i, j)))
                    load_w(*after)
                if s == 1 and j == 2:
                    sp.wait_ge(short_done, 3 * i + 3)
                    sp.dma_start(x0_dram[i, :, :], SHORTS[0][:].rearrange("p s n -> p (s n)")).then_inc(x0_stored, 16)
                if s == 2:
                    sp.wait_ge(g_ready, 4 * i + j + 1)
                    sp.dma_start(gate_dram[4 * i + j, :, :], GSTAGE[j][:].rearrange("p s n -> p (s n)")).then_inc(g_stored[j], 16)

            sp.wait_ge(w_used, len(UNITS))
            for raw, table in zip(TABLE_RAW, (cosine, sine)):
                sp.dma_start(raw[:], table.rearrange("(t p) n -> p t n", p=P)).then_inc(table_in, 16)
            sp.dma_start(W4[:], ffn_w4).then_inc(w4_in, 16)
            sp.dma_start(DECAY[:], decay.rearrange("(t p) n -> p t n", p=P)).then_inc(decay_in, 16)
            sp.dma_start(SKIP[:], hy_skip.to_broadcast([P, DC])).then_inc(skip_in, 16)
            for s in range(2):
                if s == 0:
                    for j in range(4):
                        sp.wait_ge(g_stored[j], 16 * SECTIONS[2][0])
                    sp.wait_ge(x0_stored, 16 * KC)
                else:
                    sp.wait_ge(uy_ready, KC)
                sp.dma_start(X0[:], x0_dram[:, :, s * L:(s + 1) * L].rearrange("k p n -> p k n")).then_inc(x0_in, 16)

            sp.wait_ge(k_ready, LT)
            sp.wait_ge(u_mm, 2 * LT)
            for dt in range(KD):
                for n in (2 * dt, 2 * dt + 1):
                    if n >= 4:
                        sp.wait_ge(o_lo, n - 3)
                    src = (conv_w_out, hy_w_out)[n % 2][:, dt * P:(dt + 1) * P]
                    sp.dma_start(OUT_RAW[n % 4][:], src.rearrange("(k p) n -> p k n", p=P)).then_inc(o_landed[n % 4], 16)
                if dt == 0:
                    sp.wait_ge(uy_ready, 2 * KC)
                    sp.wait_ge(y_lo, 4 * LT)
                if dt >= 2:
                    sp.wait_ge(m_lo, dt - 1)
                for n in (2 * dt, 2 * dt + 1):
                    sp.dma_start(GIN[n % 4][:].rearrange("p s n -> p (s n)"),
                                 gate_dram[(n % 2) * KD + dt, :, :]).then_inc(gin_in[n % 4], 16)

            sp.wait_ge(o_used, 2 * KD)
            for n in range(2 * KD):
                h, k = n // KD, n % KD
                if n >= 4:
                    sp.wait_ge(wo_lo, n - 3)
                sp.dma_start(WO_RAW[n % 4][:], w_o[k * P:(k + 1) * P, h * 512:(h + 1) * 512]).then_inc(o_landed[n % 4], 16)
                if n == 0:
                    sp.dma_start(NG2[:], norm2_g.to_broadcast([P, D])).then_inc(ng2_in, 16)
            for n in range(2 * TT):
                h, t = n // TT, n % TT
                if n >= 4:
                    sp.wait_ge(x2_ready, n - 3)
                sp.dma_start(XRES[n % 4][:], seq_rows(t)[:, h * 512:(h + 1) * 512]).then_inc(gin_in[n % 4], 16)

            for count, n in enumerate(FIRST):
                if count == 0:
                    sp.wait_ge(o_used, 2 * KD)
                    sp.wait_ge(m_lo, KD)
                elif count == 6:
                    sp.wait_ge(x2_mm, 2 * TT)
                elif count >= RAWS:
                    sp.wait_ge(e_lo, count - RAWS + 1)
                load_expert(sp, n, 0, count)
                if count == RAWS - 1:
                    sp.wait_ge(logits_mm, TT)
                    sp.dma_start(NGF[:], norm_f_g.to_broadcast([P, D])).then_inc(ngf_in, 16)
            with sp.Fori(1, E) as e:
                for n in range(NB):
                    sp.wait_ge(e_lo, e * NB + (n - SKIPPED - RAWS + 1))
                    load_expert(sp, n, e, n - SKIPPED + NB)
            for n in range(LEAD, LEAD + SKIPPED):
                count = NB * E - SKIPPED + n - LEAD
                sp.wait_ge(e_lo, count - RAWS + 1)
                load_expert(sp, n, E, count)

            sp.wait_ge(added, 16 * E)
            for t in range(TT):
                sp.dma_start(XF[t][:], acc_dram[t * P:(t + 1) * P, :]).then_inc(x_in[t], 16)
            for t in range(TT):
                sp.wait_ge(fin_out, t + 1)
                dst = (y_prompt if t < LT else y_sample)[(t % LT) * P:(t % LT + 1) * P, :]
                sp.dma_start(dst, XO[t % 2][:]).then_inc(fin_stored[t % 2], 16)
            for i in range(2):
                sp.wait_ge(fin_stored[i], 16 * TT // 2)

        @block.gpsimd
        def _(pool):
            nc.gpsimd.memset(ONES[:], 1.0 / DC).then_inc(ones_set, 1)
            nc.gpsimd.memset(EPS[:, 0:1], 1e-6).then_inc(ones_set, 1)
            nc.gpsimd.memset(APAD[:], 0.0).then_inc(pads_set, 1)
            pool.wait_ge(mlp_sin, 3)
            for j in range(3):
                nc.gpsimd.memset(ZPAD[j][:], 0.0).then_inc(pads_set, 1)
            pool.wait_ge(x2_ready, 2 * TT)
            nc.gpsimd.memset(ROWS[0][:], 0.0).then_inc(pads_set, 1)
            for t in range(TT):
                pool.dma_start(acc_dram[t * P:(t + 1) * P, :], X2[:, t, :]).then_inc(acc_stored, 16)
            for t in range(TT):
                pool.wait_ge(tok_ready, t + 1)
                pool.dma_start(tok_dram[t * P:(t + 1) * P, :], TOK[t % 2][:]).then_inc(tok_stored[t % 2], 16)

            def gather(e):
                if not isinstance(e, int):
                    pool.wait_ge(xs_in, e * 16)
                    pool.wait_ge(xsT_mm, e)
                pool.wait_ge(slots_ready, 2)
                nc.gpsimd.tensor_copy(NEXT_ROWS[:], SLOTS[:, bass.ds(e, 1)]).then_inc(rows_next, 1)
                pool.wait_ge(x2_mm, 2 * TT)
                pool.wait_ge(rows_next, e)
                pool.indirect_dma_start(XS[:], None, tok_dram,
                                        bass.IndirectOffsetOnAxis(ap=NEXT_ROWS[:], axis=0)).then_inc(xs_in, 16)

            def scatter(e):
                if not isinstance(e, int):
                    pool.wait_ge(added, e * 16)
                pool.wait_ge(slots_ready, 2)
                nc.gpsimd.tensor_copy(DONE_ROWS[:], SLOTS[:, bass.ds(e, 1)]).then_inc(rows_done, 1)
                pool.wait_ge(slots_ready, 2)
                pool.wait_ge(rows_done, e + 1)
                pool.wait_ge(ye_ready, e + 1)
                pool.indirect_dma_start(acc_dram, bass.IndirectOffsetOnAxis(ap=DONE_ROWS[:], axis=0), YE[:], None,
                                        compute_op=ALU.add).then_inc(added, 16)

            for i in range(2):
                pool.wait_ge(tok_stored[i], 16 * TT // 2)
            pool.wait_ge(acc_stored, 16 * TT)
            pool.wait_ge(slots_ready, 2)
            nc.gpsimd.tensor_copy(NEXT_ROWS[:], SLOTS[:, 0:1]).then_inc(pads_set, 1)
            pool.wait_ge(pads_set, 6)
            pool.wait_ge(x2_mm, 2 * TT)
            pool.indirect_dma_start(XS[:], None, tok_dram,
                                    bass.IndirectOffsetOnAxis(ap=NEXT_ROWS[:], axis=0)).then_inc(xs_in, 16)
            pool.wait_ge(xs_in, 16)
            pool.wait_ge(xsT_mm, 1)
            gather(1)
            scatter(0)
            with pool.Fori(1, E - 1) as e:
                gather(e + 1)
                scatter(e)
            pool.wait_ge(added, 16 * (E - 1))
            scatter(E - 1)

        @block.scalar
        def _(act):
            steps = Steps(act, a_step)

            def high(out, src, s, **scale):
                nc.scalar.activation(out, src, ACT.Copy, **scale).then_inc(s, 1)

            for layer in range(3):
                act.wait_ge(mlp_arg, layer + 1)
                nc.scalar.activation(FH[layer][:], FARG[:], ACT.Sin).then_inc(mlp_sin, 1)

            for t in range(TT):
                act.wait_ge(x_in[t], 16)
                if t >= 2:
                    act.wait_ge(squares, t - 1)
                nc.scalar.activation(SQJUNK[t % 2][:], X[:, t, :], ACT.Square, accum_out=SUMSQ[:, t:t + 1]).then_inc(squares, 1)
                if t % LT == LT - 1:
                    h = t // LT
                    act.wait_ge(var_ready, h + 1)
                    nc.scalar.activation(RSTD[:, h * LT:(h + 1) * LT], RSTD[:, h * LT:(h + 1) * LT], ACT.Sqrt).then_inc(roots, 1)
            act.wait_ge(small_in, 16)
            for g in range(2 * KD):
                s, k = g // KD, g % KD
                act.wait_ge(xT_ready, g + 1)
                high(HT[0][:, k, s * L:(s + 1) * L], PS[:, g % 4, :], hT_hi, scale=col("norm1", k))

            def split_w(s, i, j):
                use = use_of(s, i, j)
                act.wait_ge(w_landed[j], 16 * (use + 1))
                if unit_before((s, i, j)):
                    act.wait_ge(w_used, used_count(unit_before((s, i, j))))
                high(SPLIT[j][0][:], RAW[j][:], w_hi)

            for j in range(4):
                split_w(0, 0, j)
            for s, i, j in UNITS:
                c = SECTIONS[s][2](i, j)
                z = PS[:, 2 * j:2 * j + 2, :]
                if s == 0 and j % 2 == 0:
                    ct = 2 * i + j // 2
                    act.wait_ge(w_used, used_count((s, i, j)))
                    ge(act, a_ready, ct - 1)
                    nc.scalar.activation(SIG[ct % 2][:], z, ACT.Sigmoid, bias=col("b_in", c)).then_inc(z_free, 1)
                if s == 1:
                    act.wait_ge(w_used, used_count((s, i, j)))
                    act.wait_ge(pads_set, 4)
                    ge(act, short_done, 3 * (i - 1) + j + 1)
                    nc.scalar.activation(ZPAD[j][:, :, 1:L + 1], z, ACT.Identity, bias=col("b_in", c)).then_inc(z_free, 1)
                    act.wait_ge(z_free, KC + 3 * i + j + 1)
                    if j == 0:
                        ge(act, x0_stored, 16 * i)
                        act.wait_ge(a_ready, KC)
                    if j == 1:
                        ge(act, vT_mm, 2 * i)
                    if j == 2:
                        act.wait_ge(v_ready, i + 1)
                    cc = c - 2 * KC
                    nc.scalar.activation(SHORTS[j % 2][:], ZPAD[j][:, :, 1:L + 1], ACT.Identity, bias=col("short_b", cc),
                                         scale=col("short_w", cc * SHORT + 1)).then_inc(short_mid, 1)
                if s == 2:
                    act.wait_ge(w_used, used_count((s, i, j)))
                    ge(act, g_stored[j], 16 * i)
                    if i == 0:
                        act.wait_ge(short_done, 3 * KC)
                        act.wait_ge(x0_stored, 16 * KC)
                    nc.scalar.activation(GSTAGE[j][:], z, ACT.Sigmoid, bias=col("b_in", c)).then_inc(g_ready, 1)
                after = unit_after(s, i, j)
                if after:
                    split_w(*after)
                if s == 1 and j == 2:
                    for q in range(2):
                        act.wait_ge(vT_mm, 2 * i + q + 1)
                        high(VT[0][:, q * LT:(q + 1) * LT, i * P:(i + 1) * P],
                             PS[:, 6 + q, :].rearrange("p (t n) -> p t n", n=P), vT_hi)

            for n, table in enumerate((COS, SIN)):
                act.wait_ge(table_in, 32)
                high(table[0][:], TABLE_RAW[n][:], table_hi)
            for lt in range(LT):
                act.wait_ge(taps_ready, lt + 1)
                ge(act, norm_mm, lt)
                nc.scalar.activation(HABS[:], HF[:], ACT.Abs).then_inc(abs_ready, 1)
                act.wait_ge(eo_sum, lt + 1)
                high(EO[0][:, lt, :, :], HSUM[:].rearrange("p (s n) -> p s n", s=2), eo_hi)

            for ct in range(KC):
                act.wait_ge(ln_x, ct + 1)
                ge(act, ln_used, ct)
                nc.scalar.activation(LNSQ[:], CONV[:, ct, :, :], ACT.Square).then_inc(ln_sq, 1)
            act.wait_ge(ln_root, 1)
            nc.scalar.activation(LNRS[:], LNRS[:], ACT.Sqrt).then_inc(ln_root, 1)
            for ct in range(KC):
                act.wait_ge(ln_x, KC + ct + 1)
                steps.then(nc.scalar.activation(CONV[:, ct, :, :], CONV[:, ct, :, :], ACT.Silu,
                                                bias=col("ln_b", ct), scale=col("ln_g", ct)))
                high(AT[0][:, ct, :, :], CONV[:, ct, :, :], at_hi)

            for s in range(2):
                for f in range(LT):
                    for part, (y, tmp) in enumerate(((YRE, YT[0]), (YIM, YT[2]))):
                        act.wait_ge(y_val, 2 * (s * LT + f) + part + 1)
                        ge(act, y_mm, s * KC)
                        high(y[0][:, f, :], tmp[:], y_hi)
                for ct in range(KC):
                    act.wait_ge(uy_ready, s * KC + ct + 1)
                    high(UB[0][:, ct, s, :], UY[ct % 2][:], ub_hi)

            def split_out(n):
                j = n % 4
                act.wait_ge(o_landed[j], 16 * (n // 4 + 1))
                ge(act, o_used, n - 3)
                high(OUT_SPLIT[j][0][:], OUT_RAW[j][:], o_hi)

            for n in range(4):
                split_out(n)
            for dt in range(KD):
                act.wait_ge(m_val, dt + 1)
                high(MT[0][:, dt, :, :], GIN[2 * dt % 4][:], m_hi)
                for n in (2 * dt + 4, 2 * dt + 5):
                    if n < 2 * KD:
                        split_out(n)

            def split_wo(n):
                act.wait_ge(o_landed[n % 4], 16 * (KD // 2 + n // 4 + 1))
                before = n - 4
                if before == KD - 1:
                    act.wait_ge(x2_mm, TT)
                else:
                    ge(act, wo_used, before + 1 if before < KD else before)
                high(WO_SPLIT[n % 4][0][:], WO_RAW[n % 4][:], wo_hi)

            def square_rows(h):
                for t in range(TT):
                    n = h * TT + t
                    act.wait_ge(x2_ready, n + 1)
                    ge(act, x2_sq, n)
                    nc.scalar.activation(JUNK2[0][:], X2[:, t, h * 512:(h + 1) * 512], ACT.Square,
                                         accum_out=SUMSQ2[:, t, h:h + 1]).then_inc(x2_sq, 1)

            for n in range(TT + 4):
                split_wo(n)
            square_rows(0)
            for n in range(TT + 4, 2 * TT):
                split_wo(n)
            square_rows(1)
            act.wait_ge(ln_root, 3)
            nc.scalar.activation(RSTD2[:], RSTD2[:], ACT.Sqrt).then_inc(ln_root, 1)
            for t in range(TT):
                act.wait_ge(tokT_mm, t + 1)
                ge(act, logits_mm, t - 1)
                nc.scalar.activation(TOKT[t % 2][:].rearrange("p k n -> p (k n)"),
                                     PS[:, 2 * (t % 2):2 * (t % 2) + 2, :].rearrange("p a n -> p (a n)"),
                                     ACT.Copy).then_inc(tokT_ready, 1)
            act.wait_ge(exp_in, 1)
            nc.scalar.activation(AFF[:], AFF[:], ACT.Exp).then_inc(exp_out, 1)
            act.wait_ge(pads_set, 5)
            act.wait_ge(affT_mm, 1)
            for q in range(2):
                nc.scalar.activation(ROWS[0][32 * q:32 * q + E, :], PS[0:E, q, :], ACT.Copy).then_inc(rows_ready, 1)

            def split_e(n, e, base):
                r, (tiles, width) = slot_of(n, e), place_of(*BODY[n][:2], 0)
                act.wait_ge(e_landed[r], landed_of(n, e))
                ge(act, e_used, base + pos(n, e) - SPLITS + 1)
                q = pos_mod(n, e, SPLITS)
                high(ES[q][0][:, 0:tiles, 0:width], EW[r][:, 0:tiles, 0:width], e_hi)

            def silu(c, e, base):
                last_gate = pos(BODY.index(("gate", c, 1)), e)
                act.wait_ge(e_used, base + last_gate + 1)
                ge(act, hid_ready, NF * e + c)
                w = FC[c][1]
                nc.scalar.activation(SG[:, 0:w], PS[:, 0, 0:w], ACT.Silu).then_inc(silu_ready, 1)

            def hidT_high(c, e, base):
                act.wait_ge(hidT_mm, NF * e + c + 1)
                tiles = FC[c][1] // P
                high(HIDT[0][:, 0:tiles, :].rearrange("p t n -> p (t n)"), PS[:, 6, 0:tiles * P], hidT_hi)

            def xsT_high(e):
                act.wait_ge(xsT_mm, e + 1)
                high(XST[0][:].rearrange("p k n -> p (k n)"), PS[:, 6:8, :].rearrange("p a n -> p (a n)"), xsT_hi)

            def gate_out(e, used):
                for dh in range(2):
                    act.wait_ge(slots_ready, 2)
                    act.wait_ge(e_used, used + dh)
                    ge(act, added, e * 16)
                    out = nc.scalar.activation(YE[:, dh * 512:(dh + 1) * 512], PS[:, 4 + dh, :], ACT.Copy,
                                               scale=GATES[:, bass.ds(e, 1)])
                out.then_inc(ye_ready, 1)

            def act_body(e, base, first):
                for n in range(NB):
                    if not (first and LEAD <= n < LEAD + SKIPPED):
                        split_e(n, e, base)
                    if n == 0:
                        xsT_high(e)
                    if n == 2 and not first:
                        hidT_high(2, e - 1, base)
                    if n == 5:
                        silu(0, e, base)
                    if n == 8:
                        if not first:
                            gate_out(e - 1, base + LEAD + 1)
                        hidT_high(0, e, base)
                    if n == 11:
                        silu(1, e, base)
                    if n == 14:
                        hidT_high(1, e, base)
                    if n == 17:
                        silu(2, e, base)

            act.wait_ge(x2_mm, 2 * TT)
            act.wait_ge(slots_ready, 2)
            act_body(0, 0, True)
            with act.Fori(1, E) as e:
                act_body(e, e * NB - SKIPPED, False)
            base = E * NB - SKIPPED
            for q in range(SKIPPED):
                count = base + q
                act.wait_ge(e_landed[count % RAWS], 16 * (count // RAWS + 1))
                act.wait_ge(e_used, count - SPLITS + 1)
                tiles = FC[2][1] // P
                high(ES[count % SPLITS][0][:, 0:tiles, :], EW[count % RAWS][:, 0:tiles, :], e_hi)
            hidT_high(2, E - 1, base)
            gate_out(E - 1, base + 1)

            for t in range(TT):
                act.wait_ge(x_in[t], 32)
                act.wait_ge(squares, TT + t)
                nc.scalar.activation(YE[:], XF[t][:], ACT.Square, accum_out=SUMSQF[:, t:t + 1]).then_inc(squares, 1)
            act.wait_ge(ln_root, 5)
            nc.scalar.activation(RSTDF[:], RSTDF[:], ACT.Sqrt).then_inc(ln_root, 1)

        @block.vector
        def _(dve):
            steps = Steps(dve, v_step)
            V = nc.vector

            def low(out, src, high_part, s):
                V.tensor_tensor(out, src, high_part.bitcast(F32), ALU.subtract).then_inc(s, 1)

            dve.wait_ge(ffn_in, 16)
            for layer in range(3):
                dve.wait_ge(mlp_mm, layer + 1)
                steps.then(V.tensor_scalar(FARG[:], PS[0:FFN, 4, :], FF[:, 3 * FFN + layer:3 * FFN + layer + 1],
                                           FF[:, 3 * FFN + 3:3 * FFN + 4], ALU.add, ALU.mult))
                steps.then(V.tensor_scalar(FK[:], FARG[:], 1.0 / (2.0 * math.pi), ROUNDER, ALU.mult, ALU.add))
                steps.then(V.tensor_scalar(FK[:], FK[:], ROUNDER, None, ALU.subtract))
                steps.then(V.scalar_tensor_tensor(FARG[:], FK[:], -TWO_PI_HEAD, FARG[:], ALU.mult, ALU.add))
                steps.then(V.scalar_tensor_tensor(FARG[:], FK[:], -TWO_PI_TAIL, FARG[:], ALU.mult, ALU.add))
                V.tensor_scalar(FARG[:], FARG[:], 3.1415925, -3.1415925, ALU.min, ALU.max).then_inc(mlp_arg, 1)

            for h in range(2):
                part = slice(h * LT, (h + 1) * LT)
                dve.wait_ge(squares, (h + 1) * LT)
                V.tensor_scalar(RSTD[:, part], SUMSQ[:, part], 1.0 / D, 1e-6, ALU.mult, ALU.add).then_inc(var_ready, 1)
                dve.wait_ge(roots, h + 1)
                steps.then(V.reciprocal(RSTD[:, part], RSTD[:, part]))
                for t in range(h * LT, (h + 1) * LT):
                    V.tensor_scalar(X[:, t, :], X[:, t, :], RSTD[:, t:t + 1], None, ALU.mult).then_inc(scaled, 1)
            dve.wait_ge(small_in, 16)
            for g in range(2 * KD):
                s, k = g // KD, g % KD
                part = slice(s * L, (s + 1) * L)
                dve.wait_ge(hT_hi, g + 1)
                V.scalar_tensor_tensor(HT[1][:, k, part], PS[:, g % 4, :], col("norm1", k), HT[0][:, k, part].bitcast(F32),
                                       ALU.mult, ALU.subtract).then_inc(hT_lo, 1)

            def split_w(s, i, j):
                dve.wait_ge(w_hi, split_count((s, i, j)))
                low(SPLIT[j][1][:], RAW[j][:], SPLIT[j][0][:], w_lo)

            def conv_taps(ct, taps):
                for tap in taps:
                    src = APAD[:, ct, :, tap:tap + L]
                    w = col("dw_w", ct * TAPS + tap)
                    if tap == 0:
                        ins = V.tensor_scalar(CONV[:, ct, :, :], src, w, col("dw_b", ct), ALU.mult, ALU.add)
                    else:
                        ins = V.scalar_tensor_tensor(CONV[:, ct, :, :], src, w, CONV[:, ct, :, :], ALU.mult, ALU.add)
                    if tap == TAPS - 1:
                        ins.then_inc(conv_done, 1)
                    else:
                        steps.then(ins)

            for j in range(4):
                split_w(0, 0, j)
            for s, i, j in UNITS:
                c = SECTIONS[s][2](i, j)
                if s == 0 and j % 2 == 1:
                    ct = 2 * i + j // 2
                    dve.wait_ge(w_used, used_count((s, i, j)))
                    dve.wait_ge(z_free, ct + 1)
                    dve.wait_ge(pads_set, 1)
                    V.scalar_tensor_tensor(APAD[:, ct, :, PAD:PAD + L], PS[:, 2 * j:2 * j + 2, :], col("b_in", c),
                                           SIG[ct % 2][:], ALU.add, ALU.mult).then_inc(a_ready, 1)
                if s == 1:
                    cc = c - 2 * KC
                    r = SHORTS[j % 2]
                    dve.wait_ge(short_mid, 3 * i + j + 1)
                    steps.then(V.scalar_tensor_tensor(r[:], ZPAD[j][:, :, 0:L], col("short_w", cc * SHORT), r[:],
                                                      ALU.mult, ALU.add))
                    V.scalar_tensor_tensor(r[:], ZPAD[j][:, :, 2:L + 2], col("short_w", cc * SHORT + 2), r[:],
                                           ALU.mult, ALU.add).then_inc(short_done, 1)
                    dve.wait_ge(short_done, 3 * i + j + 1)
                    if j == 1:
                        V.tensor_tensor(r[:], r[:], SHORTS[0][:], ALU.mult).then_inc(v_ready, 1)
                after = unit_after(s, i, j)
                if after:
                    split_w(*after)
                if s == 1 and j == 2:
                    for q in range(2):
                        dve.wait_ge(vT_hi, 2 * i + q + 1)
                        low(VT[1][:, q * LT:(q + 1) * LT, i * P:(i + 1) * P],
                            PS[:, 6 + q, :].rearrange("p (t n) -> p t n", n=P),
                            VT[0][:, q * LT:(q + 1) * LT, i * P:(i + 1) * P], vT_lo)
                if s == 1:
                    dve.wait_ge(a_ready, KC)
                    conv_taps(i, range(4 * j, 4 * j + 4))
                if s == 2:
                    conv_taps(i, range(12 + 5 * j, min(12 + 5 * j + 5, TAPS)))

            for n, table in enumerate((COS, SIN)):
                dve.wait_ge(table_hi, n + 1)
                low(table[1][:], TABLE_RAW[n][:], table[0][:], table_lo)
            dve.wait_ge(decay_in, 16)
            for lt in range(LT):
                dve.wait_ge(taps_mm, lt + 1)
                ge(dve, abs_ready, lt)
                ge(dve, eo_sum, lt)
                for q in range(2):
                    V.tensor_tensor(HF[:, q * DC:(q + 1) * DC], PS[:, 4 + q, :], DECAY[:, lt, :],
                                    ALU.mult).then_inc((taps_free, taps_ready)[q], 1)
                dve.wait_ge(taps_ready, lt + 1)
                dve.wait_ge(taps_free, lt + 1)
                ge(dve, eo_lo, lt)
                ge(dve, eo_hi, lt)
                steps.then(V.tensor_tensor(HSUM[:, 0:DC], HF[:, 0:DC], HF[:, DC:2 * DC], ALU.add))
                V.tensor_tensor(HSUM[:, DC:2 * DC], HF[:, DC:2 * DC], HF[:, 0:DC], ALU.subtract).then_inc(eo_sum, 1)
                dve.wait_ge(eo_hi, lt + 1)
                low(EO[1][:, lt, :, :], HSUM[:].rearrange("p (s n) -> p s n", s=2), EO[0][:, lt, :, :], eo_lo)
            dve.wait_ge(norm_mm, LT)
            V.reciprocal(NORM[:], PS[:, 6, :]).then_inc(norm_used, 1)
            dve.wait_ge(norm_used, 1)
            dve.wait_ge(skip_in, 16)
            steps.then(V.tensor_scalar(SKIP[:], SKIP[:], float(DC), None, ALU.mult))

            dve.wait_ge(ln_mm, 1)
            for ct in range(KC):
                V.tensor_tensor(CONV[:, ct, :, :], CONV[:, ct, :, :], PS[:, 0:2, :], ALU.subtract).then_inc(ln_x, 1)

            def spectrum(f):
                re, im = (PS[:, 4, :], PS[:, 5, :]) if f % 2 == 0 else (PS[:, 6, :], PS[:, 7, :])
                cos_h, sin_h = col("cos_half", f), col("sin_half", f)
                dve.wait_ge(k_mm, f + 1)
                dve.wait_ge(table_lo, 2)
                steps.then(V.tensor_scalar(KTMP[0][:], im, sin_h, None, ALU.mult))
                steps.then(V.scalar_tensor_tensor(KR[:, f, :], re, cos_h, KTMP[0][:], ALU.mult, ALU.subtract))
                steps.then(V.tensor_tensor(KR[:, f, :], KR[:, f, :], NORM[:], ALU.mult))
                steps.then(V.tensor_scalar(KTMP[1][:], re, sin_h, None, ALU.mult))
                steps.then(V.scalar_tensor_tensor(KI[:, f, :], im, cos_h, KTMP[1][:], ALU.mult, ALU.add))
                steps.then(V.tensor_tensor(KR[:, f, :], KR[:, f, :], SKIP[:], ALU.add))
                V.tensor_tensor(KI[:, f, :], KI[:, f, :], NORM[:], ALU.mult).then_inc(k_ready, 1)

            spectrum(0)
            spectrum(1)
            dve.wait_ge(ln_mm, 2)
            V.tensor_scalar(LNRS[:], PS[:, 2:4, :], 1e-5, None, ALU.add).then_inc(ln_root, 1)
            spectrum(2)
            spectrum(3)
            dve.wait_ge(ln_root, 2)
            steps.then(V.reciprocal(LNRS[:], LNRS[:]))
            for ct in range(KC):
                dve.wait_ge(ln_sq, ct + 1)
                V.tensor_tensor(CONV[:, ct, :, :], CONV[:, ct, :, :], LNRS[:], ALU.mult).then_inc(ln_x, 1)
            for ct in range(KC):
                dve.wait_ge(at_hi, ct + 1)
                low(AT[1][:, ct, :, :], CONV[:, ct, :, :], AT[0][:, ct, :, :], at_lo)

            dve.wait_ge(k_ready, LT)
            for s in range(2):
                for f in range(LT):
                    n = s * LT + f
                    uc, us = PS[:, 2 * (f % 2), :], PS[:, 2 * (f % 2) + 1, :]
                    dve.wait_ge(u_mm, n + 1)
                    ge(dve, y_lo, 2 * n)
                    steps.then(V.tensor_tensor(YT[0][:], uc, KR[:, f, :], ALU.mult))
                    steps.then(V.tensor_tensor(YT[1][:], us, KI[:, f, :], ALU.mult))
                    V.tensor_tensor(YT[0][:], YT[0][:], YT[1][:], ALU.add).then_inc(y_val, 1)
                    steps.then(V.tensor_tensor(YT[2][:], us, KR[:, f, :], ALU.mult))
                    V.tensor_tensor(YT[3][:], uc, KI[:, f, :], ALU.mult).then_inc(u_used, 1)
                    dve.wait_ge(u_used, n + 1)
                    V.tensor_tensor(YT[2][:], YT[2][:], YT[3][:], ALU.subtract).then_inc(y_val, 1)
                    for part, (y, tmp) in enumerate(((YRE, YT[0]), (YIM, YT[2]))):
                        dve.wait_ge(y_hi, 2 * n + part + 1)
                        low(y[1][:, f, :], tmp[:], y[0][:, f, :], y_lo)
                for ct in range(KC):
                    n = s * KC + ct
                    dve.wait_ge(y_mm, n + 1)
                    dve.wait_ge(x0_in, 16 * (s + 1))
                    ge(dve, ub_lo, n - 1)
                    V.scalar_tensor_tensor(UY[ct % 2][:], PS[:, 4 + ct % 2, :], 1.0 / DC / DC, X0[:, ct, :],
                                           ALU.mult, ALU.mult).then_inc(uy_ready, 1)
                    dve.wait_ge(ub_hi, n + 1)
                    low(UB[1][:, ct, s, :], UY[ct % 2][:], UB[0][:, ct, s, :], ub_lo)

            def split_out(n):
                j = n % 4
                dve.wait_ge(o_hi, n + 1)
                low(OUT_SPLIT[j][1][:], OUT_RAW[j][:], OUT_SPLIT[j][0][:], o_lo)

            for n in range(4):
                split_out(n)
            for dt in range(KD):
                for q in range(2):
                    n = 2 * dt + q
                    j = n % 4
                    dve.wait_ge(o_used, n + 1)
                    dve.wait_ge(gin_in[j], 16 * (n // 4 + 1))
                    V.scalar_tensor_tensor(GIN[j][:], PS[:, 2 * j:2 * j + 2, :], col(("conv_b", "hy_b")[q], dt), GIN[j][:],
                                           ALU.add, ALU.mult).then_inc(m_free, 1)
                j = 2 * dt % 4
                dve.wait_ge(m_free, 2 * dt + 2)
                V.tensor_tensor(GIN[j][:], GIN[j][:], GIN[j + 1][:], ALU.add).then_inc(m_val, 1)
                for n in (2 * dt + 4, 2 * dt + 5):
                    if n < 2 * KD:
                        split_out(n)
                dve.wait_ge(m_hi, dt + 1)
                low(MT[1][:, dt, :, :], GIN[j][:], MT[0][:, dt, :, :], m_lo)

            def split_wo(n):
                dve.wait_ge(wo_hi, n + 1)
                low(WO_SPLIT[n % 4][1][:], WO_RAW[n % 4][:], WO_SPLIT[n % 4][0][:], wo_lo)

            def add_residual(h):
                for t in range(TT):
                    n = h * TT + t
                    dve.wait_ge(x2_mm, n + 1)
                    dve.wait_ge(gin_in[n % 4], 16 * (KD // 2 + n // 4 + 1))
                    V.tensor_tensor(X2[:, t, h * 512:(h + 1) * 512], PS[:, t, :], XRES[n % 4][:], ALU.add).then_inc(x2_ready, 1)

            for n in range(TT + 4):
                split_wo(n)
            add_residual(0)
            for n in range(TT + 4, 2 * TT):
                split_wo(n)
            add_residual(1)
            dve.wait_ge(x2_sq, 2 * TT)
            steps.then(V.tensor_tensor(RSTD2[:], SUMSQ2[:, :, 0], SUMSQ2[:, :, 1], ALU.add))
            V.tensor_scalar(RSTD2[:], RSTD2[:], 1.0 / D, 1e-6, ALU.mult, ALU.add).then_inc(ln_root, 1)
            dve.wait_ge(ln_root, 4)
            steps.then(V.reciprocal(RSTD2[:], RSTD2[:]))
            dve.wait_ge(ng2_in, 16)
            for t in range(TT):
                if t >= 2:
                    dve.wait_ge(tok_stored[t % 2], 16 * (t // 2))
                    dve.wait_ge(tokT_mm, t - 1)
                V.scalar_tensor_tensor(TOK[t % 2][:], X2[:, t, :], RSTD2[:, t:t + 1], NG2[:], ALU.mult, ALU.mult).then_inc(tok_ready, 1)

            logits = PS[:, 4, 0:TT * E].rearrange("p (t e) -> p t e", e=E)
            dve.wait_ge(logits_mm, TT)
            steps.then(V.reduce_max(RMAX[:], logits, AX_X))
            V.tensor_tensor(AFF[:], logits, RMAX[:, :, None].to_broadcast([P, TT, E]), ALU.subtract).then_inc(exp_in, 1)
            dve.wait_ge(exp_out, 1)
            steps.then(V.reduce_sum(RSUM[:], AFF[:], AX_X))
            steps.then(V.reciprocal(RSUM[:], RSUM[:]))
            V.tensor_tensor(AFF[:], AFF[:], RSUM[:, :, None].to_broadcast([P, TT, E]), ALU.mult).then_inc(aff_ready, 1)

            dve.wait_ge(rows_ready, 2)
            rows = ROWS[0]
            for r in range(CAP // 8):
                part = slice(8 * r, 8 * r + 8)
                steps.then(V.max(TOPV[:, part], rows[:]))
                steps.then(V.max_index(TOPI[:, part], TOPV[:, part], rows[:]))
                left = ROWS[1 + r % 2]
                if r + 1 < CAP // 8:
                    steps.then(V.match_replace(left[:], TOPV[:, part], rows[:], -1.0))
                rows = left
            steps.then(V.tensor_copy(TOPF[:], TOPI[:]))
            for q in range(2):
                rows_of, slots_of = slice(32 * q, 32 * q + E), slice(CAP * q, CAP * (q + 1))
                steps.then(V.tensor_copy(PAIR[:, 0, slots_of], TOPV[rows_of, :]))
                V.tensor_scalar(PAIR[:, 1, slots_of], TOPF[rows_of, :], float(L * q), None, ALU.add).then_inc(pair_ready, 1)
            dve.wait_ge(slots_mm, 2)
            V.tensor_copy(GATES[:], PS[:, 2, 0:E]).then_inc(slots_ready, 1)
            V.tensor_copy(SLOTS[:], PS[:, 3, 0:E]).then_inc(slots_ready, 1)

            def split_e(n, e, base):
                r, (tiles, width) = slot_of(n, e), place_of(*BODY[n][:2], 0)
                dve.wait_ge(e_hi, base + pos(n, e) + 1)
                q = pos_mod(n, e, SPLITS)
                low(ES[q][1][:, 0:tiles, 0:width], EW[r][:, 0:tiles, 0:width], ES[q][0][:, 0:tiles, 0:width], e_lo)

            def hidden(c, e, base):
                last_up = pos(BODY.index(("up", c, 1)), e)
                dve.wait_ge(e_used, base + last_up + 1)
                dve.wait_ge(silu_ready, NF * e + c + 1)
                ge(dve, hidT_mm, NF * e + c)
                w = FC[c][1]
                V.tensor_tensor(HID[:, 0:w], SG[:, 0:w], PS[:, 1, 0:w], ALU.mult).then_inc(hid_ready, 1)

            def hidT_low(c, e):
                dve.wait_ge(hidT_hi, NF * e + c + 1)
                tiles = FC[c][1] // P
                low(HIDT[1][:, 0:tiles, :].rearrange("p t n -> p (t n)"), PS[:, 6, 0:tiles * P],
                    HIDT[0][:, 0:tiles, :].rearrange("p t n -> p (t n)"), hidT_lo)

            def xsT_low(e):
                dve.wait_ge(xsT_hi, e + 1)
                low(XST[1][:].rearrange("p k n -> p (k n)"), PS[:, 6:8, :].rearrange("p a n -> p (a n)"),
                    XST[0][:].rearrange("p k n -> p (k n)"), xsT_lo)

            def dve_body(e, base, first):
                for n in range(NB):
                    if not (first and LEAD <= n < LEAD + SKIPPED):
                        split_e(n, e, base)
                    if n == 0:
                        xsT_low(e)
                    if n == 2 and not first:
                        hidT_low(2, e - 1)
                    if n == 5:
                        hidden(0, e, base)
                    if n == 8:
                        hidT_low(0, e)
                    if n == 11:
                        hidden(1, e, base)
                    if n == 14:
                        hidT_low(1, e)
                    if n == 17:
                        hidden(2, e, base)

            dve_body(0, 0, True)
            with dve.Fori(1, E) as e:
                dve_body(e, e * NB - SKIPPED, False)
            base = E * NB - SKIPPED
            for q in range(SKIPPED):
                count = base + q
                tiles = FC[2][1] // P
                dve.wait_ge(e_hi, count + 1)
                low(ES[count % SPLITS][1][:, 0:tiles, :], EW[count % RAWS][:, 0:tiles, :],
                    ES[count % SPLITS][0][:, 0:tiles, :], e_lo)
            hidT_low(2, E - 1)

            dve.wait_ge(squares, 2 * TT)
            V.tensor_scalar(RSTDF[:], SUMSQF[:], 1.0 / D, 1e-6, ALU.mult, ALU.add).then_inc(ln_root, 1)
            dve.wait_ge(ln_root, 6)
            steps.then(V.reciprocal(RSTDF[:], RSTDF[:]))
            dve.wait_ge(ngf_in, 16)
            for t in range(TT):
                if t >= 2:
                    dve.wait_ge(fin_stored[t % 2], 16 * (t // 2))
                V.scalar_tensor_tensor(XO[t % 2][:], XF[t][:], RSTDF[:, t:t + 1], NGF[:], ALU.mult, ALU.mult).then_inc(fin_out, 1)

        @block.tensor
        def _(pe):
            def product(out, a, b, first, last):
                nc.tensor.matmul(out, a[0], b[0], start=first, stop=False)
                nc.tensor.matmul(out, a[0], b[1], start=False, stop=False)
                return nc.tensor.matmul(out, a[1], b[0], start=False, stop=last)

            pe.wait_ge(ffn_in, 16)
            pe.wait_ge(zpos_in, 16)
            for layer in range(3):
                if layer:
                    pe.wait_ge(mlp_sin, layer)
                rows = zpos.shape[0] if layer == 0 else FFN
                src = ZP[:] if layer == 0 else FH[layer - 1][:]
                nc.tensor.matmul(PS[0:FFN, 4, :], FF[0:rows, layer * FFN:(layer + 1) * FFN], src,
                                 start=True, stop=True).then_inc(mlp_mm, 1)

            pe.wait_ge(small_in, 16)
            for g in range(2 * KD):
                s, k = g // KD, g % KD
                pe.wait_ge(scaled, (s + 1) * LT)
                ge(pe, hT_lo, g - 3)
                for t in range(LT):
                    mm = nc.tensor.transpose(PS[:, g % 4, t * P:(t + 1) * P], X[:, s * LT + t, k * P:(k + 1) * P], IDENT)
                mm.then_inc(xT_ready, 1)
            pe.wait_ge(hT_lo, 2 * KD)

            for s, i, j in UNITS:
                pe.wait_ge(w_lo, split_count((s, i, j)))
                before = unit_before((s, i, j))
                if before:
                    bs, bi, bj = before
                    if bs == 0 and bj % 2 == 0:
                        pe.wait_ge(z_free, 2 * bi + bj // 2 + 1)
                    elif bs == 0:
                        pe.wait_ge(a_ready, 2 * bi + bj // 2 + 1)
                    elif bs == 1:
                        pe.wait_ge(z_free, KC + 3 * bi + bj + 1)
                    else:
                        pe.wait_ge(g_ready, 4 * bi + bj + 1)
                if s == 2 and i == 0 and j == 3:
                    pe.wait_ge(vT_lo, 2 * KC)
                for k in range(KD):
                    for q in range(2):
                        mm = product(PS[:, 2 * j + q, :], (SPLIT[j][0][:, k, :], SPLIT[j][1][:, k, :]),
                                     (HT[0][:, k, q * L:(q + 1) * L], HT[1][:, k, q * L:(q + 1) * L]), k == 0, k == KD - 1)
                mm.then_inc(w_used, 1)
                if s == 1 and j == 2:
                    pe.wait_ge(v_ready, i + 1)
                    if i == 0:
                        pe.wait_ge(a_ready, KC)
                    for q in range(2):
                        ge(pe, vT_lo, 2 * (i - 1) + q + 1)
                        for t in range(LT):
                            mm = nc.tensor.transpose(PS[:, 6 + q, t * P:(t + 1) * P], SHORTS[1][:, q, t * P:(t + 1) * P], IDENT)
                        mm.then_inc(vT_mm, 1)

            pe.wait_ge(g_ready, 4 * SECTIONS[2][0])
            pe.wait_ge(w4_in, 16)
            pe.wait_ge(ones_set, 2)

            def taps(lt):
                ge(pe, taps_ready, lt)
                for q in range(2):
                    mm = nc.tensor.matmul(PS[:, 4 + q, :], FH[2][:, lt * P:(lt + 1) * P], W4[:, q * DC:(q + 1) * DC],
                                          start=True, stop=True)
                mm.then_inc(taps_mm, 1)

            def norm(lt):
                pe.wait_ge(abs_ready, lt + 1)
                for q in range(2):
                    mm = nc.tensor.matmul(PS[:, 6, :], ONES[:], HABS[:, q * DC:(q + 1) * DC],
                                          start=lt == 0 and q == 0, stop=lt == LT - 1 and q == 1)
                mm.then_inc(norm_mm, 1)

            for lt in range(LT):
                taps(lt)
                if lt:
                    norm(lt - 1)
            norm(LT - 1)
            pe.wait_ge(conv_done, KC)
            for ct in range(KC):
                for q in range(2):
                    mm = nc.tensor.matmul(PS[:, q, :], ONES[:], CONV[:, ct, q, :], start=ct == 0, stop=ct == KC - 1)
            mm.then_inc(ln_mm, 1)

            def table_tile(table, n, f):
                return table[0][:, n, f * P:(f + 1) * P], table[1][:, n, f * P:(f + 1) * P]

            def spectrum(f):
                if f == 0:
                    pe.wait_ge(table_lo, 2)
                    pe.wait_ge(eo_lo, LT)
                    pe.wait_ge(taps_ready, LT)
                elif f == 1:
                    pe.wait_ge(eo_lo, LT)
                    pe.wait_ge(norm_used, 1)
                else:
                    pe.wait_ge(k_ready, f - 1)
                for q, table in enumerate((COS, SIN)):
                    bank = 4 + 2 * (f % 2) + q
                    for n in range(LT):
                        mm = product(PS[:, bank, :], table_tile(table, n, f), (EO[0][:, n, q, :], EO[1][:, n, q, :]),
                                     n == 0, n == LT - 1)
                mm.then_inc(k_mm, 1)

            spectrum(0)
            spectrum(1)
            for ct in range(KC):
                pe.wait_ge(ln_sq, ct + 1)
                for q in range(2):
                    mm = nc.tensor.matmul(PS[:, 2 + q, :], ONES[:], LNSQ[:, q, :], start=ct == 0, stop=ct == KC - 1)
                if ct < KC - 1:
                    mm.then_inc(ln_used, 1)
            mm.then_inc(ln_mm, 1)
            spectrum(2)
            spectrum(3)

            pe.wait_ge(vT_lo, 2 * KC)
            for s in range(2):
                for f in range(LT):
                    n = s * LT + f
                    if n < 2:
                        pe.wait_ge(ln_root, 1)
                        pe.wait_ge(ln_x, KC)
                    else:
                        pe.wait_ge(u_used, n - 1)
                    for q, table in enumerate((COS, SIN)):
                        for m in range(LT):
                            mm = product(PS[:, 2 * (f % 2) + q, :], table_tile(table, m, f),
                                         (VT[0][:, s * LT + m, :], VT[1][:, s * LT + m, :]), m == 0, m == LT - 1)
                    mm.then_inc(u_mm, 1)
                pe.wait_ge(y_lo, 2 * LT * (s + 1))
                pe.wait_ge(k_ready, LT)
                for ct in range(KC):
                    ge(pe, uy_ready, s * KC + ct - 1)
                    for f in range(LT):
                        for q, (y, table) in enumerate(((YRE, COS), (YIM, SIN))):
                            mm = product(PS[:, 4 + ct % 2, :], (y[0][:, f, ct * P:(ct + 1) * P], y[1][:, f, ct * P:(ct + 1) * P]),
                                         (table[0][:, f, :], table[1][:, f, :]), f == 0 and q == 0, f == LT - 1 and q == 1)
                    mm.then_inc(y_mm, 1)

            pe.wait_ge(at_lo, KC)
            pe.wait_ge(u_used, 2 * LT)
            for n in range(2 * KD):
                j = n % 4
                pe.wait_ge(o_lo, n + 1)
                if n == 0:
                    pe.wait_ge(uy_ready, 2 * KC)
                ge(pe, m_free, n - 3)
                src = (AT, UB)[n % 2]
                if n == 1:
                    pe.wait_ge(ub_lo, 2 * KC)
                for k in range(KC):
                    for q in range(2):
                        mm = product(PS[:, 2 * j + q, :], (OUT_SPLIT[j][0][:, k, :], OUT_SPLIT[j][1][:, k, :]),
                                     (src[0][:, k, q, :], src[1][:, k, q, :]), k == 0, k == KC - 1)
                mm.then_inc(o_used, 1)

            pe.wait_ge(m_lo, KD)
            for n in range(2 * KD):
                h, k = n // KD, n % KD
                pe.wait_ge(wo_lo, n + 1)
                for t in range(TT):
                    part = slice((t % LT) * P, (t % LT + 1) * P)
                    if h and k == 0:
                        pe.wait_ge(x2_ready, t + 1)
                    mm = product(PS[:, t, :], (MT[0][:, k, t // LT, part], MT[1][:, k, t // LT, part]),
                                 (WO_SPLIT[n % 4][0][:], WO_SPLIT[n % 4][1][:]), k == 0, k == KD - 1)
                    if k == KD - 1:
                        mm.then_inc(x2_mm, 1)
                    elif t == TT - 1:
                        mm.then_inc(wo_used, 1)

            def tokens_T(t):
                pe.wait_ge(tok_ready, t + 1)
                ge(pe, tokT_ready, t - 1)
                for k in range(KD):
                    mm = nc.tensor.transpose(PS[:, 2 * (t % 2) + k // 4, (k % 4) * P:(k % 4 + 1) * P],
                                             TOK[t % 2][:, k * P:(k + 1) * P], IDENT)
                mm.then_inc(tokT_mm, 1)

            pe.wait_ge(x2_ready, 2 * TT)
            tokens_T(0)
            for t in range(TT):
                if t + 1 < TT:
                    tokens_T(t + 1)
                pe.wait_ge(tokT_ready, t + 1)
                for k in range(KD):
                    mm = nc.tensor.matmul(PS[:, 4, t * E:(t + 1) * E], TOKT[t % 2][:, k, :], col("router", k * E, E),
                                          start=k == 0, stop=k == KD - 1)
                mm.then_inc(logits_mm, 1)
            pe.wait_ge(aff_ready, 1)
            pe.wait_ge(tokT_ready, TT)
            for t in range(TT):
                mm = nc.tensor.transpose(PS[0:E, t // LT, (t % LT) * P:(t % LT + 1) * P], AFF[:, t, :], IDENT)
            mm.then_inc(affT_mm, 1)
            pe.wait_ge(pair_ready, 2)
            for q in range(2):
                nc.tensor.transpose(PS[:, 2 + q, 0:E], PAIR[:, q, :], IDENT[0:E, 0:E]).then_inc(slots_mm, 1)

            def tokens_of(e):
                pe.wait_ge(xs_in, (e + 1) * 16)
                for k in range(KD):
                    mm = nc.tensor.transpose(PS[:, 6 + k // 4, (k % 4) * P:(k % 4 + 1) * P], XS[:, k * P:(k + 1) * P], IDENT)
                mm.then_inc(xsT_mm, 1)

            def hidden_T(c, e):
                pe.wait_ge(hid_ready, NF * e + c + 1)
                for t in range(FC[c][1] // P):
                    mm = nc.tensor.transpose(PS[:, 6, t * P:(t + 1) * P], HID[:, t * P:(t + 1) * P], IDENT)
                mm.then_inc(hidT_mm, 1)

            def gate_up(c, e, base):
                for n, (kind, cc, kh) in enumerate(BODY):
                    if kind == "down" or cc != c:
                        continue
                    w = FC[c][1]
                    q = pos_mod(n, e, SPLITS)
                    pe.wait_ge(e_lo, base + pos(n, e) + 1)
                    bank = 0 if kind == "gate" else 1
                    if kh == 0 and kind == "gate":
                        ge(pe, hid_ready, NF * e + c)
                    for t in range(4):
                        k = 4 * kh + t
                        mm = product(PS[:, bank, 0:w], (XST[0][:, k, :], XST[1][:, k, :]),
                                     (ES[q][0][:, t, 0:w], ES[q][1][:, t, 0:w]), k == 0, k == KD - 1)
                    mm.then_inc(e_used, 1)

            def down(c, e, counts):
                tiles = FC[c][1] // P
                pe.wait_ge(hidT_lo, NF * e + c + 1)
                if c == 0:
                    ge(pe, ye_ready, e)
                for dh in range(2):
                    count, q = counts[dh]
                    pe.wait_ge(e_lo, count + 1)
                    for t in range(tiles):
                        mm = product(PS[:, 4 + dh, :], (HIDT[0][:, t, :], HIDT[1][:, t, :]),
                                     (ES[q][0][:, t, :], ES[q][1][:, t, :]), c == 0 and t == 0, c == NF - 1 and t == tiles - 1)
                    mm.then_inc(e_used, 1)

            def down_counts(c, e, base):
                ns = [BODY.index(("down", c, dh)) for dh in range(2)]
                return [(base + pos(n, e), pos_mod(n, e, SPLITS)) for n in ns]

            def pe_body(e, base, first, last):
                gate_up(0, e, base)
                if not first:
                    down(2, e - 1, down_counts(2, e, base))
                hidden_T(0, e)
                gate_up(1, e, base)
                down(0, e, down_counts(0, e, base))
                hidden_T(1, e)
                gate_up(2, e, base)
                pe.wait_ge(hidT_lo, NF * e + 2)
                if not last:
                    tokens_of(e + 1)
                down(1, e, down_counts(1, e, base))
                if not last:
                    pe.wait_ge(xsT_lo, e + 2)
                hidden_T(2, e)

            tokens_of(0)
            pe.wait_ge(xsT_lo, 1)
            pe_body(0, 0, True, False)
            with pe.Fori(1, E - 1) as e:
                pe_body(e, e * NB - SKIPPED, False, False)
            pe_body(E - 1, (E - 1) * NB - SKIPPED, False, True)
            base = E * NB - SKIPPED
            down(2, E - 1, [(base + dh, (base + dh) % SPLITS) for dh in range(2)])


def kernel(**inputs):
    import numpy as np
    import concourse.bacc as bacc
    from concourse.bass_utils import run_bass_kernel_spmd

    def w(name):
        return np.asarray(inputs[name])[0]

    f32 = np.float32
    xp, xs = np.asarray(inputs["x_prompt"])[0], np.asarray(inputs["x_sample"])[0]
    L, D = xp.shape
    DC = w("conv_w_out").shape[0]
    PROJ = w("w_in").shape[1]
    E = w("router_w").shape[1]
    TAPS, SHORT = w("conv_dw_w").shape[0], w("hy_short_w").shape[0]

    def columns(a):
        return a.reshape(-1, P).T

    def columns_taps(a):
        return a.reshape(a.shape[0], -1, P).transpose(2, 1, 0).reshape(P, -1)

    f = np.arange(L)
    half = np.pi * (2 * f + 1) / (4 * L)
    angle = np.pi * np.outer(2 * f + 1, 2 * f + 1) / (4 * L)
    parts = {
        "b_in": columns(w("b_in")), "dw_w": columns_taps(w("conv_dw_w")), "dw_b": columns(w("conv_dw_b")),
        "ln_g": columns(w("conv_ln_g")), "ln_b": columns(w("conv_ln_b")), "conv_b": columns(w("conv_b_out")),
        "short_w": columns_taps(w("hy_short_w")), "short_b": columns(w("hy_short_b")), "hy_b": columns(w("hy_b_out")),
        "norm1": columns(w("norm1_g")), "cos_half": columns(np.cos(half).astype(f32)),
        "sin_half": columns(np.sin(half).astype(f32)),
        "router": w("router_w").reshape(-1, P, E).transpose(1, 0, 2).reshape(P, -1), "ident": np.eye(P, dtype=f32),
    }
    where, _ = small_columns(D, DC, PROJ, TAPS, SHORT, E)
    small = np.concatenate([parts[name] for name in where], axis=1)
    w1 = w("hy_f_w1")
    N = w1.shape[1]
    ffn = np.concatenate([np.concatenate([w1, np.zeros((N - w1.shape[0], N), f32)]), w("hy_f_w2"), w("hy_f_w3"),
                          np.stack([w("hy_f_b1"), w("hy_f_b2"), w("hy_f_b3"), w("hy_f_freq")], axis=1)], axis=1)
    bands_n = (w1.shape[0] - 1) // 2
    time = np.linspace(0.0, 1.0, L, dtype=f32)[:, None]
    turn = (f32(2.0 * math.pi) * np.arange(L, dtype=f32)[:, None] / f32(L)).astype(f32)
    bands = np.linspace(1e-4, bands_n - 1, bands_n, dtype=f32)[None, :]
    zpos = np.concatenate([time, np.cos(bands * turn), -np.sin(bands * turn)], axis=1).astype(f32).T
    deltas = np.linspace(math.log(1e-2) / 1.5, math.log(1e-2) / 0.3, DC, dtype=f32)
    decay = np.exp(-time * np.abs(deltas)[None, :]).astype(f32)
    arrays = {
        "x_prompt": xp, "x_sample": xs, "small": small, "ffn": ffn, "ffn_w4": w("hy_f_w4"), "zpos": zpos, "decay": decay,
        "cosine": np.cos(angle).astype(f32), "sine": np.sin(angle).astype(f32),
        "w_in": w("w_in"), "conv_w_out": w("conv_w_out"), "hy_w_out": w("hy_w_out"), "w_o": w("w_o"),
        "hy_skip": np.asarray(inputs["hy_skip"]), "norm2_g": np.asarray(inputs["norm2_g"]),
        "norm_f_g": np.asarray(inputs["norm_f_g"]).reshape(1, D),
        "w_gate": w("exp_w_gate"), "w_up": w("exp_w_up"), "w_down": w("exp_w_down"),
    }
    arrays = {f"in_{k}": np.ascontiguousarray(v) for k, v in arrays.items()}
    nc = bacc.Bacc("TRN2", target_bir_lowering=False, num_devices=1)
    args = [nc.dram_tensor(k, a.shape, mybir.dt.from_np(a.dtype), kind="ExternalInput").ap() for k, a in arrays.items()]
    args += [nc.dram_tensor(k, (L, D), F32, kind="ExternalOutput").ap() for k in ("out_prompt", "out_sample")]
    hybrid_encoder_kernel(nc, *args)
    result = run_bass_kernel_spmd(nc, [arrays], core_ids=[0]).results[0]
    return result["out_prompt"].reshape(1, L, D), result["out_sample"].reshape(1, L, D)
```

```python
from contextlib import ExitStack
import math

import concourse.bass as bass
from concourse import mybir

P = 128
F32 = mybir.dt.float32
F32R = mybir.dt.float32r
U32 = mybir.dt.uint32
ALU = mybir.AluOpType
ACT = mybir.ActivationFunctionType
AX_X = mybir.AxisListType.X
KB = 1024
SBUF_BASE = 16 * KB + 128

TWO_PI_HEAD = 6.28125
TWO_PI_TAIL = 2.0 * math.pi - TWO_PI_HEAD
ROUNDER = 1.5 * 2.0 ** 23


def small_columns(D, DC, PROJ, TAPS, SHORT, E):
    widths = [
        ("b_in", PROJ // P), ("dw_w", DC // P * TAPS), ("dw_b", DC // P), ("ln_g", DC // P), ("ln_b", DC // P),
        ("conv_b", D // P), ("short_w", 3 * DC // P * SHORT), ("short_b", 3 * DC // P), ("hy_b", D // P),
        ("norm1", D // P), ("cos_half", DC // P), ("sin_half", DC // P), ("router", D // P * E), ("ident", P),
    ]
    at, where = 0, {}
    for name, width in widths:
        where[name] = (at, width)
        at += width
    return where, at


def hybrid_encoder_kernel(
    nc: bass.Bass,
    x_prompt: bass.AP,
    x_sample: bass.AP,
    small: bass.AP,
    ffn: bass.AP,
    ffn_w4: bass.AP,
    zpos: bass.AP,
    decay: bass.AP,
    cosine: bass.AP,
    sine: bass.AP,
    w_in: bass.AP,
    conv_w_out: bass.AP,
    hy_w_out: bass.AP,
    w_o: bass.AP,
    hy_skip: bass.AP,
    norm2_g: bass.AP,
    norm_f_g: bass.AP,
    w_gate: bass.AP,
    w_up: bass.AP,
    w_down: bass.AP,
    y_prompt: bass.AP,
    y_sample: bass.AP,
):
    L, D = x_prompt.shape
    PROJ = w_in.shape[1]
    DC = conv_w_out.shape[0]
    E, _, F = w_gate.shape
    FFN = ffn.shape[0]
    TAPS, SHORT = 31, 3
    PAD = TAPS // 2
    CAP = 2 * L // E
    KD, KC, LT = D // P, DC // P, L // P
    TT = 2 * LT
    where, small_n = small_columns(D, DC, PROJ, TAPS, SHORT, E)
    assert L == 512 and D == 1024 and DC == 512 and 2 * CAP == P and E == 16

    x0_dram = nc.dram_tensor("x0_spill", [KC, P, 2 * L], F32, kind="Internal").ap()
    gate_dram = nc.dram_tensor("gate_spill", [2 * KD, P, 2 * L], F32, kind="Internal").ap()
    tok_dram = nc.dram_tensor("tok_rows", [2 * L, D], F32, kind="Internal").ap()
    acc_dram = nc.dram_tensor("acc_rows", [2 * L, D], F32, kind="Internal").ap()

    ctx = ExitStack()
    with ctx:
        def at(name, kib, shape, dt=F32):
            return nc.alloc_sbuf_tensor_at(name, shape, dt, offset=SBUF_BASE + int(kib * KB))

        SM = at("small_params", 0, [P, small_n])
        IDENT = SM[:, where["ident"][0]:where["ident"][0] + P]
        ONES = at("ones", 2.5, [P, P])
        SUMSQ = at("sum_squares", 3.5, [P, TT])
        RSTD = at("rstd", 3.5625, [P, TT])
        SUMSQ2 = at("sum_squares2", 3.625, [P, TT, 2])
        RSTD2 = at("rstd2", 3.75, [P, TT])
        SUMSQF = at("sum_squares_f", 3.8125, [P, TT])
        RSTDF = at("rstd_f", 3.875, [P, TT])
        AFF = at("affinity", 4.0, [P, TT, E])
        AFFW = at("affinity_wide", 6.75, [P, LT, 48])
        NORMC = at("filter_norm_column", 7.5, [P, KC])
        RSUM = at("softmax_sum", 4.5, [P, TT])
        RMAX = at("softmax_max", 4.5625, [P, TT])
        TOPV = at("top_values", 4.625, [48, CAP])
        TOPI = at("top_index", 4.875, [48, CAP], U32)
        TOPF = at("top_index_float", 5.125, [48, CAP])
        PAIR = at("slots_of_experts", 5.375, [E, 2, P])
        GATES = at("slot_gates", 6.375, [P, E])
        SLOTS = at("slot_rows", 6.4375, [P, E], U32)
        NEXT_ROWS = at("rows_to_gather", 6.5, [P, 1], U32)
        DONE_ROWS = at("rows_to_scatter", 6.53125, [P, 1], U32)
        CUR_GATE = at("gate_of_slot", 6.5625, [P, 1])
        EPS = at("eps", 6.59375, [P, 2])

        HT = (at("hT_hi", 8, [P, KD, 2 * L], F32R), at("hT_lo", 40, [P, KD, 2 * L], F32R))
        X = at("x_rows", 120, [P, TT, D])
        RAW = [at(f"w_raw{j}", 72 + 4 * j, [P, KD, P]) for j in range(4)]
        SPLIT = [(at(f"w_hi{j}", 88 + 8 * j, [P, KD, P], F32R), at(f"w_lo{j}", 92 + 8 * j, [P, KD, P], F32R))
                 for j in range(4)]
        VT = (at("v_rows_hi", 120, [P, TT, DC], F32R), at("v_rows_lo", 136, [P, TT, DC], F32R))
        APAD = at("a_padded", 152, [P, KC, 2, L + 2 * PAD])
        CONV = at("conv_sum", 169, [P, KC, 2, L])
        FF = at("ffn_params", 185, [FFN, ffn.shape[1]])
        ZP = at("zpos", 186, [zpos.shape[0], L])
        FARG = at("sin_argument", 188, [FFN, L])
        FK = at("sin_turns", 190, [FFN, L])
        FH = [at("filter_h1", 192, [FFN, L]), at("filter_h2", 194, [FFN, L]), at("filter_h3", 205.5, [FFN, L])]
        SQJUNK = [at(f"square_out{i}", 185 - 16 + 4 * i, [P, D]) for i in range(2)]
        SIG = [at(f"sigmoid{i}", 197.5 + 4 * i, [P, 2, L]) for i in range(2)]
        ZPAD = [at(f"z_padded{j}", 185 + 4.0625 * j, [P, 2, L + 2]) for j in range(3)]
        SHORTS = [at(f"short_conv{i}", 197.25 + 4 * i, [P, 2, L]) for i in range(2)]
        GSTAGE = [at(f"gate_stage{j}", 185 + 4 * j, [P, 2, L]) for j in range(2)]
        COS = (at("cos_hi", 8, [P, LT, L], F32R), at("cos_lo", 16, [P, LT, L], F32R))
        SIN = (at("sin_hi", 24, [P, LT, L], F32R), at("sin_lo", 32, [P, LT, L], F32R))
        TABLE_RAW = [at("cos_raw", 72, [P, LT, L]), at("sin_raw", 80, [P, LT, L])]
        DECAY = at("decay", 193, [P, LT, DC])
        W4 = at("w4", 201.25, [FFN, 2 * DC])
        HF = [at(f"filter_taps{i}", 56 + 4 * i, [P, 2 * DC]) for i in range(2)]
        HSUM = at("filter_even_odd", 64, [P, 2 * DC])
        HABS = at("filter_abs", 68, [P, 2 * DC])
        SKIPN = at("skip_times_norm", 72, [P, DC])
        SKIP = at("skip", 74, [P, DC])
        NROW = at("norm_row", 76, [1, DC])
        EO = (at("even_odd_hi", 88, [P, LT, 2, DC], F32R), at("even_odd_lo", 104, [P, LT, 2, DC], F32R))
        KR = at("filter_re", 40, [P, LT, DC])
        KI = at("filter_im", 48, [P, LT, DC])
        KTMP = [at("spectrum_tmp0", 78, [P, DC]), at("spectrum_tmp1", 205.5, [P, DC])]
        YRE = (at("y_re_hi", 88, [P, LT, DC], F32R), at("y_re_lo", 96, [P, LT, DC], F32R))
        YIM = (at("y_im_hi", 104, [P, LT, DC], F32R), at("y_im_lo", 112, [P, LT, DC], F32R))
        YT = [at(f"product{i}", 185 + 2 * i, [P, DC]) for i in range(4)]
        X0 = at("x0", 193, [P, KC, L])
        YV = [at(f"spectrum_sum{i}", 201 + 2 * i, [P, DC]) for i in range(2)]
        UY = [at(f"x0_times_y{i}", 201 + 2 * i, [P, L]) for i in range(2)]
        UB = (at("hyena_out_hi", 56, [P, KC, 2, L], F32R), at("hyena_out_lo", 72, [P, KC, 2, L], F32R))
        LNSQ = at("ln_square", 185, [P, 2, L])
        LNRS = at("ln_rstd", 164, [P, 2, L])
        AT = (at("conv_out_hi", 152, [P, KC, 2, L], F32R), at("conv_out_lo", 169, [P, KC, 2, L], F32R))
        OUT_RAW = [at(f"wout_raw{j}", 120 + 2 * j, [P, KC, P]) for j in range(4)]
        OUT_SPLIT = [(at(f"wout_hi{j}", 128 + 4 * j, [P, KC, P], F32R), at(f"wout_lo{j}", 130 + 4 * j, [P, KC, P], F32R))
                     for j in range(4)]
        GIN = [at(f"gate_in{j}", 185 + 4 * j, [P, 2, L]) for j in range(4)]
        MT = (at("mixed_hi", 8, [P, KD, 2, L], F32R), at("mixed_lo", 88, [P, KD, 2, L], F32R))
        WO_RAW = [at(f"wo_raw{j}", 120 + 2 * j, [P, L]) for j in range(4)]
        WO_SPLIT = [(at(f"wo_hi{j}", 128 + 4 * j, [P, L], F32R), at(f"wo_lo{j}", 130 + 4 * j, [P, L], F32R))
                    for j in range(4)]
        WO_SPLIT += [(at(f"wo_hi{4 + j}", 72 + 4 * j, [P, L], F32R), at(f"wo_lo{4 + j}", 74 + 4 * j, [P, L], F32R))
                     for j in range(4)]
        X2 = at("x2_rows", 40, [P, TT, D])
        XRES = [at(f"x_again{i}", 144 + 2 * i, [P, 512]) for i in range(4)]
        TOK = [at(f"tok_rows{i}", 152 + 4 * i, [P, D]) for i in range(2)]
        TOKT = [at(f"tok_T{i}", 160 + 4 * i, [P, KD, P]) for i in range(2)]
        NG2 = at("norm2_g_all", 168, [P, D])
        JUNK2 = [at(f"square2_out{i}", 172 + 2 * i, [P, 512]) for i in range(1)]
        ROWS = [at(f"affinity_rows{i}", 144 + 2 * i, [48, L]) for i in range(3)]
        raw_at = [174, 182, 190, 198, 8, 16, 24, 72, 80]
        EARLY = 4
        RAWS = len(raw_at)
        EW = [at(f"expert_raw{j}", k, [P, 4, 512]) for j, k in enumerate(raw_at)]
        SPLITS = 3
        ES = [(at(f"expert_hi{j}", 88 + 16 * j, [P, 4, 512], F32R), at(f"expert_lo{j}", 96 + 16 * j, [P, 4, 512], F32R))
              for j in range(SPLITS)]
        XS = at("slot_tokens", 136, [P, D])
        XST = (at("slot_tokens_T_hi", 140, [P, KD, P], F32R), at("slot_tokens_T_lo", 144, [P, KD, P], F32R))
        SG = at("silu_gate", 148, [P, 512])
        HID = at("hidden", 150, [P, 512])
        HIDT = (at("hidden_T_hi", 152, [P, 4, P], F32R), at("hidden_T_lo", 154, [P, 4, P], F32R))
        YE = at("expert_out", 156, [P, D])
        NGF = at("norm_f_g_all", 160, [P, D])
        XF = [at(f"final_rows{i}", 32 + 4 * i, [P, D]) for i in range(8)]
        XO = [at(f"final_out{i}", 64 + 4 * i, [P, D]) for i in range(2)]

        PS = ctx.enter_context(nc.psum_tensor("ps", [P, 8, 512], F32))

        def sem(name):
            return ctx.enter_context(nc.semaphore(name))

        def sems(name, n):
            return [sem(f"{name}{i}") for i in range(n)]

        def col(name, i=0, n=1):
            a = where[name][0]
            return SM[:, a + i:a + i + n]

        small_in, ffn_in, zpos_in = sem("small_in"), sem("ffn_in"), sem("zpos_in")
        x_in = sems("x_in", TT)
        ones_set, pads_set = sem("ones_set"), sem("pads_set")
        a_step, v_step = sem("act_step"), sem("dve_step")
        squares, roots, scaled = sem("squares"), sem("roots"), sem("x_scaled")
        var_ready = sem("var_ready")
        xT_ready, hT_hi, hT_lo = sem("xT_ready"), sem("hT_hi"), sem("hT_lo")
        mlp_mm, mlp_arg, mlp_sin = sem("mlp_mm"), sem("mlp_arg"), sem("mlp_sin")
        w_landed = sems("w_landed", 4)
        w_hi, w_lo, w_used, z_free = sem("w_hi"), sem("w_lo"), sem("w_used"), sem("z_free")
        sig_ready, a_ready = sem("sig_ready"), sem("a_ready")
        z_padded, short_mid, short_done = sem("z_padded"), sem("short_mid"), sem("short_done")
        v_ready, x0_stored = sem("v_ready"), sem("x0_stored")
        vT_mm, vT_hi, vT_lo = sem("vT_mm"), sem("vT_hi"), sem("vT_lo")
        g_ready, g_stored = sem("g_ready"), sems("g_stored", 2)
        conv_done = sem("conv_done")
        table_in, table_hi, cos_lo, sin_lo = sem("table_in"), sem("table_hi"), sem("cos_lo"), sem("sin_lo")
        decay_in, w4_in, skip_in = sem("decay_in"), sem("w4_in"), sem("skip_in")
        taps_mm, taps_ready, abs_ready, norm_mm, eo_sum, eo_hi, eo_lo = (
            sem("taps_mm"), sem("taps_ready"), sem("abs_ready"), sem("norm_mm"), sem("eo_sum"), sem("eo_hi"), sem("eo_lo"))
        norm_row, norm_col = sem("norm_row"), sem("norm_col")
        k_mm, k_ready = sem("k_mm"), sem("k_ready")
        u_mm, u_used, y_val, y_hi, y_lo = sem("u_mm"), sem("u_used"), sem("y_val"), sem("y_hi"), sem("y_lo")
        x0_in, y_mm, uy_ready, ub_hi, ub_lo = sem("x0_in"), sem("y_mm"), sem("uy_ready"), sem("ub_hi"), sem("ub_lo")
        skip_norm = sem("skip_norm")
        ln_mm, ln_used = sem("ln_mm"), sem("ln_used")
        ln_sq, ln_root, ln_x, at_hi, at_lo = (
            sem("ln_sq"), sem("ln_root"), sem("ln_x"), sem("at_hi"), sem("at_lo"))
        o_landed = sems("o_landed", 4)
        o_hi, o_lo, o_used = sem("o_hi"), sem("o_lo"), sem("o_used")
        gin_in = sems("gin_in", 4)
        m_free, m_val, m_hi, m_lo = sem("m_free"), sem("m_val"), sem("m_hi"), sem("m_lo")
        x2_mm, x2_ready, x2_sq = sem("x2_mm"), sem("x2_ready"), sem("x2_sq")
        ng2_in, ngf_in = sem("ng2_in"), sem("ngf_in")
        tok_ready, tok_stored, acc_stored = sem("tok_ready"), sems("tok_stored", 2), sem("acc_stored")
        tokT_mm, tokT_ready, logits_mm = sem("tokT_mm"), sem("tokT_ready"), sem("logits_mm")
        aff_ready, affT_mm, rows_ready, top_ready, pair_ready, slots_mm, slots_ready = (
            sem("aff_ready"), sem("affT_mm"), sem("rows_ready"), sem("top_ready"), sem("pair_ready"),
            sem("slots_mm"), sem("slots_ready"))
        exp_in, exp_out = sem("softmax_shifted"), sem("softmax_exp")
        e_landed = sems("e_landed", RAWS)
        e_hi, e_lo, e_used = sem("e_hi"), sem("e_lo"), sem("e_used")
        rows_next, xs_in, xsT_mm, xsT_hi, xsT_lo = (
            sem("rows_next"), sem("xs_in"), sem("xsT_mm"), sem("xsT_hi"), sem("xsT_lo"))
        silu_ready, hid_ready, hidT_mm, hidT_hi, hidT_lo = (
            sem("silu_ready"), sem("hid_ready"), sem("hidT_mm"), sem("hidT_hi"), sem("hidT_lo"))
        ye_ready, rows_done, added = sem("ye_ready"), sem("rows_done"), sem("rows_added")
        fin_out, fin_stored = sem("fin_ready"), sems("fin_stored", 2)

        block = ctx.enter_context(nc.Block())

        def ge(eng, s, value):
            if not isinstance(value, int) or value > 0:
                eng.wait_ge(s, value)

        class Steps:

            def __init__(self, eng, s):
                self.eng, self.sem, self.n = eng, s, 0

            def did(self, ins):
                ins.then_inc(self.sem, 1)
                self.n += 1

            def wait(self):
                self.eng.wait_ge(self.sem, self.n)

            def then(self, ins):
                self.did(ins)
                self.wait()

        CONV_SEC = (2, 4, lambda i, j: 2 * i + j // 2 + (KC if j % 2 == 0 else 0))
        HYENA_SEC = (KC, 3, lambda i, j: 2 * KC + (KC, 2 * KC, 0)[j] + i)
        GATE_SEC = (4, 4, lambda i, j: 5 * KC + 4 * i + j)
        SECTIONS = [CONV_SEC, HYENA_SEC, GATE_SEC]
        UNITS = [(s, i, j) for s in range(3) for i in range(SECTIONS[s][0]) for j in range(SECTIONS[s][1])]

        def use_of(s, i, j):
            return sum(n for n, width, _ in SECTIONS[:s] if j < width) + i

        def unit_after(s, i, j):
            if i + 1 < SECTIONS[s][0]:
                return s, i + 1, j
            for t in range(s + 1, 3):
                if j < SECTIONS[t][1]:
                    return t, 0, j
            return None

        SPLIT_ORDER = [(0, 0, j) for j in range(4)] + [unit_after(*u) for u in UNITS if unit_after(*u)]

        def split_count(u):
            return SPLIT_ORDER.index(u) + 1

        def used_count(u):
            return UNITS.index(u) + 1

        def unit_before(u):
            return next((v for v in UNITS if unit_after(*v) == u), None)

        def seq_rows(t):
            src = x_prompt if t < LT else x_sample
            return src[(t % LT) * P:(t % LT + 1) * P, :]

        FC = [(a, min(512, F - a)) for a in range(0, F, 512)]
        NF = len(FC)
        GU_UNITS = [(kind, c, kh) for c in range(NF) for kh in range(2) for kind in ("gate", "up")]

        def down_units(c):
            return [("down", c, dh) for dh in range(2)]

        def gu_units(c):
            return [u for u in GU_UNITS if u[1] == c]

        BODY = gu_units(0) + down_units(2) + gu_units(1) + down_units(0) + gu_units(2) + down_units(1)
        NB = len(BODY)
        LEAD = len(gu_units(0))
        SKIPPED = len(down_units(2))

        def src_of(kind, c, k, e):
            a, n = FC[c]
            if kind == "down":
                tiles = n // P
                return w_down[bass.ds(e, 1), a:a + n, k * 512:(k + 1) * 512].rearrange(
                    "o (t p) n -> p (o t) n", p=P), tiles, 512
            w = w_gate if kind == "gate" else w_up
            return w[bass.ds(e, 1), k * 4 * P:(k + 1) * 4 * P, a:a + n].rearrange(
                "o (t p) n -> p (o t) n", p=P), 4, n

        def place_of(kind, c, k):
            a, n = FC[c]
            return (n // P, 512) if kind == "down" else (4, n)

        FIRST = [n for n in range(NB) if not LEAD <= n < LEAD + SKIPPED]
        assert NB % RAWS == 0 and NB % SPLITS == 0

        def pos(n, e):
            return FIRST.index(n) if isinstance(e, int) and e == 0 else n

        def pos_mod(n, e, m):
            return (FIRST.index(n) if isinstance(e, int) and e == 0 else n - SKIPPED) % m

        def slot_of(n, e):
            return pos_mod(n, e, RAWS)

        def landed_of(n, e):
            if isinstance(e, int) and e == 0:
                return 16 * (FIRST.index(n) // RAWS + 1)
            return e * (16 * (NB // RAWS)) + 16 * ((n - SKIPPED) // RAWS + 1)

        def wo_slot(n):
            return n % 4 + (4 if KD <= n < KD + 4 else 0)

        def load_expert(sp, n, e, count):
            kind, c, k = BODY[n]
            owner = e - 1 if (kind, c) == ("down", 2) else e
            tiles, width = place_of(kind, c, k)
            src, _, _ = src_of(kind, c, k, owner)
            sp.dma_start(EW[count % RAWS][:, 0:tiles, 0:width], src).then_inc(e_landed[count % RAWS], 16)

        @block.sync
        def _(sp):
            sp.dma_start(SM[:], small).then_inc(small_in, 16)
            for t in range(TT):
                sp.dma_start(X[:, t, :], seq_rows(t)).then_inc(x_in[t], 16)

            def load_w(s, i, j):
                c = SECTIONS[s][2](i, j)
                sp.dma_start(RAW[j][:], w_in[:, c * P:(c + 1) * P].rearrange("(k p) n -> p k n", p=P)).then_inc(w_landed[j], 16)

            for j in range(4):
                load_w(0, 0, j)
                if j == 0:
                    sp.dma_start(FF[:], ffn).then_inc(ffn_in, 16)
                    sp.dma_start(ZP[:], zpos).then_inc(zpos_in, 16)
            for s, i, j in UNITS:
                if (s, i, j) == (2, 0, 0):
                    sp.wait_ge(short_done, 3 * KC)
                    sp.wait_ge(vT_mm, 2 * KC)
                    sp.wait_ge(x0_stored, 16 * KC)
                    sp.dma_start(W4[:], ffn_w4).then_inc(w4_in, 16)
                    sp.dma_start(DECAY[:], decay.rearrange("(t p) n -> p t n", p=P)).then_inc(decay_in, 16)
                after = unit_after(s, i, j)
                if after:
                    sp.wait_ge(w_lo, split_count((s, i, j)))
                    load_w(*after)
                if s == 1 and j == 2:
                    sp.wait_ge(short_done, 3 * i + 3)
                    sp.dma_start(x0_dram[i, :, :], SHORTS[0][:].rearrange("p s n -> p (s n)")).then_inc(x0_stored, 16)
                if s == 2 and i == SECTIONS[2][0] - 1 and j % 2:
                    sp.wait_ge(w_lo, len(UNITS) - 3 + j)
                    table = (cosine, sine)[j // 2]
                    sp.dma_start(TABLE_RAW[j // 2][:], table.rearrange("(t p) n -> p t n", p=P)).then_inc(table_in, 16)
                if s == 2:
                    q = 4 * i + j
                    sp.wait_ge(g_ready, q + 1)
                    sp.dma_start(gate_dram[q, :, :], GSTAGE[q % 2][:].rearrange("p s n -> p (s n)")).then_inc(g_stored[q % 2], 16)

            sp.wait_ge(cos_lo, 1)
            sp.dma_start(SKIP[:], hy_skip.to_broadcast([P, DC])).then_inc(skip_in, 16)
            for s in range(2):
                if s == 0:
                    sp.wait_ge(taps_ready, LT)
                else:
                    sp.wait_ge(uy_ready, KC)
                sp.dma_start(X0[:], x0_dram[:, :, s * L:(s + 1) * L].rearrange("k p n -> p k n")).then_inc(x0_in, 16)

            sp.wait_ge(k_ready, LT)
            sp.wait_ge(u_mm, 2 * LT)
            for dt in range(KD):
                for n in (2 * dt, 2 * dt + 1):
                    if n >= 4:
                        sp.wait_ge(o_lo, n - 3)
                    src = (conv_w_out, hy_w_out)[n % 2][:, dt * P:(dt + 1) * P]
                    sp.dma_start(OUT_RAW[n % 4][:], src.rearrange("(k p) n -> p k n", p=P)).then_inc(o_landed[n % 4], 16)
                if dt == 0:
                    sp.wait_ge(uy_ready, 2 * KC)
                    sp.wait_ge(y_lo, 4 * LT)
                    for q in range(2):
                        sp.wait_ge(g_stored[q], 16 * KD)
                if dt >= 2:
                    sp.wait_ge(m_lo, dt - 1)
                for n in (2 * dt, 2 * dt + 1):
                    sp.dma_start(GIN[n % 4][:].rearrange("p s n -> p (s n)"),
                                 gate_dram[(n % 2) * KD + dt, :, :]).then_inc(gin_in[n % 4], 16)

            def load_residual(n):
                h, t = n // TT, n % TT
                ge(sp, x2_ready, n - 3)
                sp.dma_start(XRES[n % 4][:], seq_rows(t)[:, h * 512:(h + 1) * 512]).then_inc(gin_in[n % 4], 16)

            for n in range(2 * KD):
                h, k = n // KD, n % KD
                sp.wait_ge(o_lo, 2 * KD + n - 3)
                sp.dma_start(WO_RAW[n % 4][:], w_o[k * P:(k + 1) * P, h * 512:(h + 1) * 512]).then_inc(o_landed[n % 4], 16)
                if n == 3:
                    sp.wait_ge(o_used, 2 * KD)
                    sp.wait_ge(m_lo, KD)
                    sp.dma_start(NG2[:], norm2_g.to_broadcast([P, D])).then_inc(ng2_in, 16)
                    for r in range(4):
                        load_residual(r)
            for count in range(EARLY):
                load_expert(sp, FIRST[count], 0, count)
            for n in range(4, 2 * TT):
                load_residual(n)

            for count, n in enumerate(FIRST):
                if count < EARLY:
                    continue
                if count == EARLY:
                    sp.wait_ge(x2_mm, 2 * TT)
                elif count >= RAWS:
                    sp.wait_ge(e_lo, count - RAWS + 1)
                load_expert(sp, n, 0, count)
                if count == RAWS - 1:
                    sp.wait_ge(logits_mm, TT)
                    sp.dma_start(NGF[:], norm_f_g.to_broadcast([P, D])).then_inc(ngf_in, 16)
            with sp.Fori(1, E) as e:
                for n in range(NB):
                    sp.wait_ge(e_lo, e * NB + (n - SKIPPED - RAWS + 1))
                    load_expert(sp, n, e, n - SKIPPED + NB)
            for n in range(LEAD, LEAD + SKIPPED):
                count = NB * E - SKIPPED + n - LEAD
                sp.wait_ge(e_lo, count - RAWS + 1)
                load_expert(sp, n, E, count)

            sp.wait_ge(added, 16 * E)
            for t in range(TT):
                sp.dma_start(XF[t][:], acc_dram[t * P:(t + 1) * P, :]).then_inc(x_in[t], 16)
            for t in range(TT):
                sp.wait_ge(fin_out, t + 1)
                dst = (y_prompt if t < LT else y_sample)[(t % LT) * P:(t % LT + 1) * P, :]
                sp.dma_start(dst, XO[t % 2][:]).then_inc(fin_stored[t % 2], 16)
            for i in range(2):
                sp.wait_ge(fin_stored[i], 16 * TT // 2)

        @block.gpsimd
        def _(pool):
            nc.gpsimd.memset(ONES[:], 1.0 / DC).then_inc(ones_set, 1)
            nc.gpsimd.memset(EPS[:, 0:1], 1e-6).then_inc(ones_set, 1)
            nc.gpsimd.memset(EPS[:, 1:2], 1e-5).then_inc(ones_set, 1)
            nc.gpsimd.memset(AFFW[:], 0.0).then_inc(ones_set, 1)
            nc.gpsimd.memset(APAD[:], 0.0).then_inc(pads_set, 1)
            pool.wait_ge(mlp_sin, 3)
            for j in range(3):
                nc.gpsimd.memset(ZPAD[j][:], 0.0).then_inc(pads_set, 1)

            pool.wait_ge(table_hi, 2)
            nc.gpsimd.tensor_tensor(SIN[1][:], TABLE_RAW[1][:], SIN[0][:].bitcast(F32), ALU.subtract).then_inc(sin_lo, 1)
            for lt in range(LT):
                h = HF[lt % 2]
                pool.wait_ge(taps_ready, lt + 1)
                ge(pool, eo_lo, lt)
                nc.gpsimd.tensor_tensor(HSUM[:, 0:DC], h[:, 0:DC], h[:, DC:2 * DC], ALU.add).then_inc(eo_sum, 1)
                nc.gpsimd.tensor_tensor(HSUM[:, DC:2 * DC], h[:, DC:2 * DC], h[:, 0:DC], ALU.subtract).then_inc(eo_sum, 1)

            for s in range(2):
                for f in range(LT):
                    n = s * LT + f
                    pool.wait_ge(u_used, n + 1)
                    ge(pool, y_lo, 2 * n)
                    ge(pool, ub_lo, s * KC)
                    if n == 0:
                        pool.wait_ge(taps_mm, LT)
                    nc.gpsimd.tensor_tensor(YV[0][:], YT[0][:], YT[1][:], ALU.add).then_inc(y_val, 1)
                    nc.gpsimd.tensor_tensor(YV[1][:], YT[2][:], YT[3][:], ALU.subtract).then_inc(y_val, 1)
                    if s == 0:
                        pool.wait_ge(ln_root, 2)
                        pool.wait_ge(ln_sq, f + 1)
                        nc.gpsimd.tensor_tensor(CONV[:, f, :, :], CONV[:, f, :, :], LNRS[:], ALU.mult).then_inc(ln_x, 1)
                    else:
                        pool.wait_ge(at_hi, f + 1)
                        nc.gpsimd.tensor_tensor(AT[1][:, f, :, :], CONV[:, f, :, :], AT[0][:, f, :, :].bitcast(F32),
                                                ALU.subtract).then_inc(at_lo, 1)

            for t in range(TT):
                pool.wait_ge(x2_ready, TT + t + 1)
                pool.dma_start(acc_dram[t * P:(t + 1) * P, :], X2[:, t, :]).then_inc(acc_stored, 16)
                pool.wait_ge(tok_ready, t + 1)
                pool.dma_start(tok_dram[t * P:(t + 1) * P, :], TOK[t % 2][:]).then_inc(tok_stored[t % 2], 16)

            def gather(e):
                if not isinstance(e, int):
                    pool.wait_ge(xs_in, e * 16)
                    pool.wait_ge(xsT_mm, e)
                pool.wait_ge(slots_ready, 2)
                nc.gpsimd.tensor_copy(NEXT_ROWS[:], SLOTS[:, bass.ds(e, 1)]).then_inc(rows_next, 1)
                pool.wait_ge(x2_mm, 2 * TT)
                pool.wait_ge(rows_next, e)
                pool.indirect_dma_start(XS[:], None, tok_dram,
                                        bass.IndirectOffsetOnAxis(ap=NEXT_ROWS[:], axis=0)).then_inc(xs_in, 16)

            def scatter(e):
                if not isinstance(e, int):
                    pool.wait_ge(added, e * 16)
                pool.wait_ge(slots_ready, 2)
                nc.gpsimd.tensor_copy(DONE_ROWS[:], SLOTS[:, bass.ds(e, 1)]).then_inc(rows_done, 1)
                pool.wait_ge(slots_ready, 2)
                pool.wait_ge(rows_done, e + 1)
                pool.wait_ge(ye_ready, e + 1)
                pool.indirect_dma_start(acc_dram, bass.IndirectOffsetOnAxis(ap=DONE_ROWS[:], axis=0), YE[:], None,
                                        compute_op=ALU.add).then_inc(added, 16)

            for i in range(2):
                pool.wait_ge(tok_stored[i], 16 * TT // 2)
            pool.wait_ge(acc_stored, 16 * TT)
            pool.wait_ge(slots_ready, 2)
            nc.gpsimd.tensor_copy(NEXT_ROWS[:], SLOTS[:, 0:1]).then_inc(pads_set, 1)
            pool.wait_ge(pads_set, 5)
            pool.wait_ge(x2_mm, 2 * TT)
            pool.indirect_dma_start(XS[:], None, tok_dram,
                                    bass.IndirectOffsetOnAxis(ap=NEXT_ROWS[:], axis=0)).then_inc(xs_in, 16)
            pool.wait_ge(xs_in, 16)
            pool.wait_ge(xsT_mm, 1)
            gather(1)
            scatter(0)
            with pool.Fori(1, E - 1) as e:
                gather(e + 1)
                scatter(e)
            pool.wait_ge(added, 16 * (E - 1))
            scatter(E - 1)

        @block.scalar
        def _(act):
            steps = Steps(act, a_step)

            def high(out, src, s, **scale):
                nc.scalar.activation(out, src, ACT.Copy, **scale).then_inc(s, 1)

            def root(t):
                act.wait_ge(var_ready, t + 1)
                nc.scalar.activation(RSTD[:, t:t + 1], RSTD[:, t:t + 1], ACT.Sqrt).then_inc(roots, 1)

            def hT_high(g):
                s, k = g // KD, g % KD
                act.wait_ge(xT_ready, g + 1)
                high(HT[0][:, k, s * L:(s + 1) * L], PS[:, g % 4, :], hT_hi, scale=col("norm1", k))

            act.wait_ge(small_in, 16)
            for t in range(TT):
                act.wait_ge(x_in[t], 16)
                if t >= 2:
                    act.wait_ge(squares, t - 1)
                nc.scalar.activation(SQJUNK[t % 2][:], X[:, t, :], ACT.Square, accum_out=SUMSQ[:, t:t + 1]).then_inc(squares, 1)
                if t:
                    root(t - 1)
                if t > LT:
                    hT_high(2 * (t - LT - 1))
                    hT_high(2 * (t - LT - 1) + 1)
            root(TT - 1)

            def split_w(s, i, j):
                use = use_of(s, i, j)
                act.wait_ge(w_landed[j], 16 * (use + 1))
                if unit_before((s, i, j)):
                    act.wait_ge(w_used, used_count(unit_before((s, i, j))))
                high(SPLIT[j][0][:], RAW[j][:], w_hi)

            for g in range(2 * (LT - 1), 2 * KD):
                hT_high(g)
                if g == 2 * KD - 5:
                    split_w(0, 0, 0)
            for j in range(1, 4):
                split_w(0, 0, j)

            def mlp_sine(layer):
                act.wait_ge(mlp_arg, layer + 1)
                nc.scalar.activation(FH[layer][:], FARG[:], ACT.Sin).then_inc(mlp_sin, 1)

            mlp_sine(0)
            for s, i, j in UNITS:
                c = SECTIONS[s][2](i, j)
                z = PS[:, 2 * j:2 * j + 2, :]
                if s == 0 and j % 2 == 0:
                    ct = 2 * i + j // 2
                    act.wait_ge(w_used, used_count((s, i, j)))
                    ge(act, a_ready, ct - 1)
                    nc.scalar.activation(SIG[ct % 2][:], z, ACT.Sigmoid, bias=col("b_in", c)).then_inc(z_free, 1)
                if s == 1:
                    act.wait_ge(w_used, used_count((s, i, j)))
                    act.wait_ge(pads_set, 4)
                    ge(act, short_done, 3 * (i - 1) + j + 1)
                    nc.scalar.activation(ZPAD[j][:, :, 1:L + 1], z, ACT.Identity, bias=col("b_in", c)).then_inc(z_free, 1)
                    act.wait_ge(z_free, KC + 3 * i + j + 1)
                    if j == 0:
                        ge(act, x0_stored, 16 * i)
                        act.wait_ge(a_ready, KC)
                    if j == 1:
                        ge(act, vT_mm, 2 * i)
                    if j == 2:
                        act.wait_ge(v_ready, i + 1)
                    cc = c - 2 * KC
                    nc.scalar.activation(SHORTS[j % 2][:], ZPAD[j][:, :, 1:L + 1], ACT.Identity, bias=col("short_b", cc),
                                         scale=col("short_w", cc * SHORT + 1)).then_inc(short_mid, 1)
                if s == 2:
                    q = 4 * i + j
                    act.wait_ge(w_used, used_count((s, i, j)))
                    ge(act, g_stored[q % 2], 16 * (q // 2))
                    if q == 0:
                        act.wait_ge(short_done, 3 * KC)
                    nc.scalar.activation(GSTAGE[q % 2][:], z, ACT.Sigmoid, bias=col("b_in", c)).then_inc(g_ready, 1)
                after = unit_after(s, i, j)
                if after:
                    split_w(*after)
                if s == 0 and i == 0 and j < 2:
                    mlp_sine(j + 1)
                if s == 1 and j == 2:
                    for q in range(2):
                        act.wait_ge(vT_mm, 2 * i + q + 1)
                        high(VT[0][:, q * LT:(q + 1) * LT, i * P:(i + 1) * P],
                             PS[:, 6 + q, :].rearrange("p (t n) -> p t n", n=P), vT_hi)

            act.wait_ge(w_used, len(UNITS))
            for n, table in enumerate((COS, SIN)):
                act.wait_ge(table_in, 32)
                high(table[0][:], TABLE_RAW[n][:], table_hi)
            for lt in range(LT):
                act.wait_ge(taps_ready, lt + 1)
                ge(act, norm_mm, lt)
                nc.scalar.activation(HABS[:], HF[lt % 2][:], ACT.Abs).then_inc(abs_ready, 1)
                act.wait_ge(eo_sum, 2 * lt + 2)
                high(EO[0][:, lt, :, :], HSUM[:].rearrange("p (s n) -> p s n", s=2), eo_hi)
            act.wait_ge(norm_mm, LT)
            act.wait_ge(cos_lo, 1)
            nc.scalar.activation(NROW[:], PS[0:1, 6, :], ACT.Copy).then_inc(norm_row, 1)

            act.wait_ge(g_stored[0], 16 * KD)
            act.wait_ge(g_stored[1], 16 * KD)
            for ct in range(KC):
                act.wait_ge(ln_x, ct + 1)
                ge(act, ln_used, ct)
                nc.scalar.activation(LNSQ[:], CONV[:, ct, :, :], ACT.Square).then_inc(ln_sq, 1)
            act.wait_ge(ln_mm, 2)
            act.wait_ge(ones_set, 4)
            nc.scalar.activation(LNRS[:], PS[:, 2:4, :], ACT.Sqrt, bias=EPS[:, 1:2]).then_inc(ln_root, 1)

            def spectrum_high(s, f):
                for part, y in enumerate((YRE, YIM)):
                    act.wait_ge(y_val, 2 * (s * LT + f) + part + 1)
                    ge(act, y_mm, s * KC)
                    high(y[0][:, f, :], YV[part][:], y_hi)

            for s in range(2):
                for f in range(LT):
                    spectrum_high(s, f)
                    if s == 0:
                        act.wait_ge(ln_x, KC + f + 1)
                        steps.then(nc.scalar.activation(CONV[:, f, :, :], CONV[:, f, :, :], ACT.Silu,
                                                        bias=col("ln_b", f), scale=col("ln_g", f)))
                        high(AT[0][:, f, :, :], CONV[:, f, :, :], at_hi)
                for ct in range(KC):
                    act.wait_ge(uy_ready, s * KC + ct + 1)
                    high(UB[0][:, ct, s, :], UY[ct % 2][:], ub_hi)

            def split_out(n):
                j = n % 4
                act.wait_ge(o_landed[j], 16 * (n // 4 + 1))
                ge(act, o_used, n - 3)
                high(OUT_SPLIT[j][0][:], OUT_RAW[j][:], o_hi)

            def split_wo(n):
                act.wait_ge(o_landed[n % 4], 16 * (KD // 2 + n // 4 + 1))
                if n < KD:
                    act.wait_ge(o_used, 2 * KD + n - 3)
                elif n == 2 * KD - 1:
                    act.wait_ge(x2_mm, TT)
                else:
                    act.wait_ge(o_used, 2 * KD + max(n - KD + 1, 0) if n >= KD + 4 else 2 * KD)
                high(WO_SPLIT[wo_slot(n)][0][:], WO_RAW[n % 4][:], o_hi)

            for n in range(4):
                split_out(n)
            for dt in range(KD):
                act.wait_ge(m_val, dt + 1)
                high(MT[0][:, dt, :, :], GIN[2 * dt % 4][:], m_hi)
                for n in (2 * dt + 4, 2 * dt + 5):
                    if n < 2 * KD:
                        split_out(n)
                    else:
                        split_wo(n - 2 * KD)

            def square_rows(h, t):
                n = h * TT + t
                act.wait_ge(x2_ready, n + 1)
                ge(act, x2_sq, n)
                nc.scalar.activation(JUNK2[0][:], X2[:, t, h * 512:(h + 1) * 512], ACT.Square,
                                     accum_out=SUMSQ2[:, t, h:h + 1]).then_inc(x2_sq, 1)

            def tokT_copy(t):
                act.wait_ge(tokT_mm, t + 1)
                ge(act, logits_mm, t - 1)
                nc.scalar.activation(TOKT[t % 2][:].rearrange("p k n -> p (k n)"),
                                     PS[:, 4 + 2 * (t % 2):6 + 2 * (t % 2), :].rearrange("p a n -> p (a n)"),
                                     ACT.Copy).then_inc(tokT_ready, 1)

            for n in range(4, 2 * KD):
                split_wo(n)
            for t in range(TT):
                square_rows(0, t)
            for t in range(TT):
                square_rows(1, t)
                act.wait_ge(var_ready, TT + t + 1)
                nc.scalar.activation(RSTD2[:, t:t + 1], RSTD2[:, t:t + 1], ACT.Sqrt, bias=EPS[:, 0:1]).then_inc(roots, 1)
                if t:
                    tokT_copy(t - 1)
            tokT_copy(TT - 1)
            act.wait_ge(exp_in, 1)
            nc.scalar.activation(AFF[:], AFF[:], ACT.Exp).then_inc(exp_out, 1)
            act.wait_ge(affT_mm, 1)
            nc.scalar.activation(ROWS[0][:], PS[0:48, 3, :], ACT.Copy).then_inc(rows_ready, 1)

            def split_e(n, e, base):
                r, (tiles, width) = slot_of(n, e), place_of(*BODY[n][:2], 0)
                act.wait_ge(e_landed[r], landed_of(n, e))
                ge(act, e_used, base + pos(n, e) - SPLITS + 1)
                q = pos_mod(n, e, SPLITS)
                high(ES[q][0][:, 0:tiles, 0:width], EW[r][:, 0:tiles, 0:width], e_hi)

            def silu(c, e, base):
                last_gate = pos(BODY.index(("gate", c, 1)), e)
                act.wait_ge(e_used, base + last_gate + 1)
                ge(act, hid_ready, NF * e + c)
                w = FC[c][1]
                nc.scalar.activation(SG[:, 0:w], PS[:, 0, 0:w], ACT.Silu).then_inc(silu_ready, 1)

            def hidT_high(c, e, base):
                act.wait_ge(hidT_mm, NF * e + c + 1)
                tiles = FC[c][1] // P
                high(HIDT[0][:, 0:tiles, :].rearrange("p t n -> p (t n)"), PS[:, 6, 0:tiles * P], hidT_hi)

            def xsT_high(e):
                act.wait_ge(xsT_mm, e + 1)
                high(XST[0][:].rearrange("p k n -> p (k n)"), PS[:, 6:8, :].rearrange("p a n -> p (a n)"), xsT_hi)

            def gate_out(e, used):
                for dh in range(2):
                    act.wait_ge(slots_ready, 2)
                    act.wait_ge(e_used, used + dh)
                    ge(act, added, e * 16)
                    out = nc.scalar.activation(YE[:, dh * 512:(dh + 1) * 512], PS[:, 4 + dh, :], ACT.Copy,
                                               scale=GATES[:, bass.ds(e, 1)])
                out.then_inc(ye_ready, 1)

            def act_body(e, base, first):
                for n in range(NB):
                    if not (first and LEAD <= n < LEAD + SKIPPED):
                        split_e(n, e, base)
                    if n == (2 if first else 0):
                        xsT_high(e)
                    if n == 2 and not first:
                        hidT_high(2, e - 1, base)
                    if n == 5:
                        silu(0, e, base)
                    if n == 8:
                        if not first:
                            gate_out(e - 1, base + LEAD + 1)
                        hidT_high(0, e, base)
                    if n == 11:
                        silu(1, e, base)
                    if n == 14:
                        hidT_high(1, e, base)
                    if n == 17:
                        silu(2, e, base)

            act.wait_ge(x2_mm, 2 * TT)
            act_body(0, 0, True)
            with act.Fori(1, E) as e:
                act_body(e, e * NB - SKIPPED, False)
            base = E * NB - SKIPPED
            for q in range(SKIPPED):
                count = base + q
                act.wait_ge(e_landed[count % RAWS], 16 * (count // RAWS + 1))
                act.wait_ge(e_used, count - SPLITS + 1)
                tiles = FC[2][1] // P
                high(ES[count % SPLITS][0][:, 0:tiles, :], EW[count % RAWS][:, 0:tiles, :], e_hi)
            hidT_high(2, E - 1, base)
            gate_out(E - 1, base + 1)

            def final_root(t):
                act.wait_ge(var_ready, 2 * TT + t + 1)
                nc.scalar.activation(RSTDF[:, t:t + 1], RSTDF[:, t:t + 1], ACT.Sqrt).then_inc(roots, 1)

            for t in range(TT):
                act.wait_ge(x_in[t], 32)
                act.wait_ge(squares, TT + t)
                nc.scalar.activation(YE[:], XF[t][:], ACT.Square, accum_out=SUMSQF[:, t:t + 1]).then_inc(squares, 1)
                if t:
                    final_root(t - 1)
            final_root(TT - 1)

        @block.vector
        def _(dve):
            steps = Steps(dve, v_step)
            V = nc.vector

            def low(out, src, high_part, s):
                V.tensor_tensor(out, src, high_part.bitcast(F32), ALU.subtract).then_inc(s, 1)

            def scale_rows(t):
                dve.wait_ge(roots, t + 1)
                steps.then(V.reciprocal(RSTD[:, t:t + 1], RSTD[:, t:t + 1]))
                V.tensor_scalar(X[:, t, :], X[:, t, :], RSTD[:, t:t + 1], None, ALU.mult).then_inc(scaled, 1)

            def hT_low(g):
                s, k = g // KD, g % KD
                part = slice(s * L, (s + 1) * L)
                dve.wait_ge(hT_hi, g + 1)
                V.scalar_tensor_tensor(HT[1][:, k, part], PS[:, g % 4, :], col("norm1", k), HT[0][:, k, part].bitcast(F32),
                                       ALU.mult, ALU.subtract).then_inc(hT_lo, 1)

            dve.wait_ge(small_in, 16)
            for t in range(TT):
                dve.wait_ge(squares, t + 1)
                V.tensor_scalar(RSTD[:, t:t + 1], SUMSQ[:, t:t + 1], 1.0 / D, 1e-6, ALU.mult, ALU.add).then_inc(var_ready, 1)
                if t:
                    scale_rows(t - 1)
                if t > LT:
                    hT_low(2 * (t - LT - 1))
                    hT_low(2 * (t - LT - 1) + 1)
            scale_rows(TT - 1)

            def split_w(s, i, j):
                dve.wait_ge(w_hi, split_count((s, i, j)))
                low(SPLIT[j][1][:], RAW[j][:], SPLIT[j][0][:], w_lo)

            def conv_taps(ct, taps):
                for tap in taps:
                    src = APAD[:, ct, :, tap:tap + L]
                    w = col("dw_w", ct * TAPS + tap)
                    if tap == 0:
                        ins = V.tensor_scalar(CONV[:, ct, :, :], src, w, col("dw_b", ct), ALU.mult, ALU.add)
                    else:
                        ins = V.scalar_tensor_tensor(CONV[:, ct, :, :], src, w, CONV[:, ct, :, :], ALU.mult, ALU.add)
                    if tap == TAPS - 1:
                        ins.then_inc(conv_done, 1)
                    else:
                        steps.then(ins)

            for g in range(2 * (LT - 1), 2 * KD):
                hT_low(g)
                if g == 2 * KD - 5:
                    split_w(0, 0, 0)
            for j in range(1, 4):
                split_w(0, 0, j)

            def mlp_argument(layer):
                dve.wait_ge(ffn_in, 16)
                dve.wait_ge(mlp_mm, layer + 1)
                steps.then(V.tensor_scalar(FARG[:], PS[0:FFN, 6, :], FF[:, 3 * FFN + layer:3 * FFN + layer + 1],
                                           FF[:, 3 * FFN + 3:3 * FFN + 4], ALU.add, ALU.mult))
                steps.then(V.tensor_scalar(FK[:], FARG[:], 1.0 / (2.0 * math.pi), ROUNDER, ALU.mult, ALU.add))
                steps.then(V.tensor_scalar(FK[:], FK[:], ROUNDER, None, ALU.subtract))
                steps.then(V.scalar_tensor_tensor(FARG[:], FK[:], -TWO_PI_HEAD, FARG[:], ALU.mult, ALU.add))
                steps.then(V.scalar_tensor_tensor(FARG[:], FK[:], -TWO_PI_TAIL, FARG[:], ALU.mult, ALU.add))
                V.tensor_scalar(FARG[:], FARG[:], 3.1415925, -3.1415925, ALU.min, ALU.max).then_inc(mlp_arg, 1)

            mlp_argument(0)
            for s, i, j in UNITS:
                c = SECTIONS[s][2](i, j)
                if s == 0 and j % 2 == 1:
                    ct = 2 * i + j // 2
                    dve.wait_ge(w_used, used_count((s, i, j)))
                    dve.wait_ge(z_free, ct + 1)
                    dve.wait_ge(pads_set, 1)
                    V.scalar_tensor_tensor(APAD[:, ct, :, PAD:PAD + L], PS[:, 2 * j:2 * j + 2, :], col("b_in", c),
                                           SIG[ct % 2][:], ALU.add, ALU.mult).then_inc(a_ready, 1)
                if s == 1:
                    cc = c - 2 * KC
                    r = SHORTS[j % 2]
                    dve.wait_ge(short_mid, 3 * i + j + 1)
                    steps.then(V.scalar_tensor_tensor(r[:], ZPAD[j][:, :, 0:L], col("short_w", cc * SHORT), r[:],
                                                      ALU.mult, ALU.add))
                    V.scalar_tensor_tensor(r[:], ZPAD[j][:, :, 2:L + 2], col("short_w", cc * SHORT + 2), r[:],
                                           ALU.mult, ALU.add).then_inc(short_done, 1)
                    dve.wait_ge(short_done, 3 * i + j + 1)
                    if j == 1:
                        V.tensor_tensor(r[:], r[:], SHORTS[0][:], ALU.mult).then_inc(v_ready, 1)
                after = unit_after(s, i, j)
                if after:
                    split_w(*after)
                if s == 0 and i == 0 and j < 2:
                    mlp_argument(j + 1)
                if s == 1 and j == 2:
                    for q in range(2):
                        dve.wait_ge(vT_hi, 2 * i + q + 1)
                        low(VT[1][:, q * LT:(q + 1) * LT, i * P:(i + 1) * P],
                            PS[:, 6 + q, :].rearrange("p (t n) -> p t n", n=P),
                            VT[0][:, q * LT:(q + 1) * LT, i * P:(i + 1) * P], vT_lo)
                if s == 1:
                    dve.wait_ge(a_ready, KC)
                    conv_taps(i, range(4 * j, 4 * j + 4))
                if s == 2:
                    conv_taps(i, range(12 + 5 * j, min(12 + 5 * j + 5, TAPS)))

            dve.wait_ge(table_hi, 1)
            low(COS[1][:], TABLE_RAW[0][:], COS[0][:], cos_lo)
            dve.wait_ge(decay_in, 16)

            def eo_low(lt):
                dve.wait_ge(eo_hi, lt + 1)
                low(EO[1][:, lt, :, :], HSUM[:].rearrange("p (s n) -> p s n", s=2), EO[0][:, lt, :, :], eo_lo)

            for lt in range(LT):
                dve.wait_ge(taps_mm, lt + 1)
                ge(dve, abs_ready, lt - 1)
                ge(dve, eo_sum, 2 * (lt - 1))
                for q in range(2):
                    out = V.tensor_tensor(HF[lt % 2][:, q * DC:(q + 1) * DC], PS[:, 4 + q, :], DECAY[:, lt, :], ALU.mult)
                out.then_inc(taps_ready, 1)
                if lt:
                    eo_low(lt - 1)
            eo_low(LT - 1)
            dve.wait_ge(norm_mm, LT)
            dve.wait_ge(norm_row, 1)
            dve.wait_ge(skip_in, 16)
            V.scalar_tensor_tensor(SKIPN[:], PS[:, 6, :], float(DC), SKIP[:], ALU.mult, ALU.mult).then_inc(skip_norm, 1)

            dve.wait_ge(ln_mm, 1)
            for ct in range(KC):
                V.tensor_tensor(CONV[:, ct, :, :], CONV[:, ct, :, :], PS[:, 0:2, :], ALU.subtract).then_inc(ln_x, 1)
            dve.wait_ge(norm_col, 1)
            steps.then(V.reciprocal(NORMC[:], PS[:, 7, 0:KC]))
            V.tensor_scalar(NORMC[:], NORMC[:], 1.0 / DC / DC, None, ALU.mult).then_inc(norm_col, 1)
            dve.wait_ge(norm_col, 2)

            def spectrum(f):
                re, im = (PS[:, 4, :], PS[:, 5, :]) if f % 2 == 0 else (PS[:, 6, :], PS[:, 7, :])
                cos_h, sin_h = col("cos_half", f), col("sin_half", f)
                dve.wait_ge(k_mm, f + 1)
                dve.wait_ge(skip_norm, 1)
                steps.did(V.scalar_tensor_tensor(KTMP[0][:], im, sin_h, SKIPN[:], ALU.mult, ALU.subtract))
                steps.then(V.tensor_scalar(KTMP[1][:], re, sin_h, None, ALU.mult))
                V.scalar_tensor_tensor(KR[:, f, :], re, cos_h, KTMP[0][:], ALU.mult, ALU.subtract).then_inc(k_ready, 1)
                V.scalar_tensor_tensor(KI[:, f, :], im, cos_h, KTMP[1][:], ALU.mult, ALU.add).then_inc(k_ready, 1)
                dve.wait_ge(k_ready, 2 * f + 2)

            spectrum(0)
            spectrum(1)
            dve.wait_ge(ln_root, 1)
            V.reciprocal(LNRS[:], LNRS[:]).then_inc(ln_root, 1)
            spectrum(2)
            spectrum(3)

            def products(s, f):
                n = s * LT + f
                uc, us = PS[:, 2 * (f % 2), :], PS[:, 2 * (f % 2) + 1, :]
                dve.wait_ge(u_mm, n + 1)
                ge(dve, y_val, 2 * n)
                for tmp, (u, k) in zip(YT, ((uc, KR), (us, KI), (us, KR), (uc, KI))):
                    out = V.tensor_tensor(tmp[:], u, k[:, f, :], ALU.mult)
                out.then_inc(u_used, 1)

            def spectrum_low(s, f):
                for part, y in enumerate((YRE, YIM)):
                    dve.wait_ge(y_hi, 2 * (s * LT + f) + part + 1)
                    low(y[1][:, f, :], YV[part][:], y[0][:, f, :], y_lo)

            def hyena_out(s, ct):
                n = s * KC + ct
                dve.wait_ge(y_mm, n + 1)
                dve.wait_ge(x0_in, 16 * (s + 1))
                dve.wait_ge(y_lo, 2 * LT * (s + 1))
                ge(dve, ub_lo, n - 1)
                V.scalar_tensor_tensor(UY[ct % 2][:], PS[:, 4 + ct % 2, :], NORMC[:, ct:ct + 1], X0[:, ct, :],
                                       ALU.mult, ALU.mult).then_inc(uy_ready, 1)
                dve.wait_ge(ub_hi, n + 1)
                low(UB[1][:, ct, s, :], UY[ct % 2][:], UB[0][:, ct, s, :], ub_lo)

            dve.wait_ge(ln_mm, 2)
            for f in range(LT):
                products(0, f)
                if f:
                    spectrum_low(0, f - 1)
            spectrum_low(0, LT - 1)
            products(1, 0)
            for ct in range(KC):
                hyena_out(0, ct)
            for f in range(1, LT):
                products(1, f)
                spectrum_low(1, f - 1)
            spectrum_low(1, LT - 1)
            for ct in range(KC):
                hyena_out(1, ct)

            def split_out(n):
                j = n % 4
                dve.wait_ge(o_hi, n + 1)
                low(OUT_SPLIT[j][1][:], OUT_RAW[j][:], OUT_SPLIT[j][0][:], o_lo)

            def split_wo(n):
                dve.wait_ge(o_hi, 2 * KD + n + 1)
                slot = WO_SPLIT[wo_slot(n)]
                low(slot[1][:], WO_RAW[n % 4][:], slot[0][:], o_lo)

            for n in range(4):
                split_out(n)
            for dt in range(KD):
                for q in range(2):
                    n = 2 * dt + q
                    j = n % 4
                    dve.wait_ge(o_used, n + 1)
                    dve.wait_ge(gin_in[j], 16 * (n // 4 + 1))
                    V.scalar_tensor_tensor(GIN[j][:], PS[:, 2 * j:2 * j + 2, :], col(("conv_b", "hy_b")[q], dt), GIN[j][:],
                                           ALU.add, ALU.mult).then_inc(m_free, 1)
                j = 2 * dt % 4
                dve.wait_ge(m_free, 2 * dt + 2)
                V.tensor_tensor(GIN[j][:], GIN[j][:], GIN[j + 1][:], ALU.add).then_inc(m_val, 1)
                for n in (2 * dt + 4, 2 * dt + 5):
                    if n < 2 * KD:
                        split_out(n)
                dve.wait_ge(m_hi, dt + 1)
                low(MT[1][:, dt, :, :], GIN[j][:], MT[0][:, dt, :, :], m_lo)
                for n in (2 * dt + 4 - 2 * KD, 2 * dt + 5 - 2 * KD):
                    if n >= 0:
                        split_wo(n)

            def add_residual(h, t):
                n = h * TT + t
                dve.wait_ge(x2_mm, n + 1)
                dve.wait_ge(gin_in[n % 4], 16 * (KD // 2 + n // 4 + 1))
                V.tensor_tensor(X2[:, t, h * 512:(h + 1) * 512], PS[:, t if h == 0 else t % 2, :], XRES[n % 4][:],
                                ALU.add).then_inc(x2_ready, 1)

            for n in range(4, 2 * KD - 1):
                split_wo(n)
            add_residual(0, 0)
            split_wo(2 * KD - 1)
            for t in range(1, TT):
                add_residual(0, t)
            dve.wait_ge(ng2_in, 16)
            for t in range(TT):
                add_residual(1, t)
                dve.wait_ge(x2_sq, TT + t + 1)
                V.tensor_scalar(RSTD2[:, t:t + 1], SUMSQ2[:, t, 0:1], SUMSQ2[:, t, 1:2], 1.0 / D,
                                ALU.add, ALU.mult).then_inc(var_ready, 1)
                dve.wait_ge(roots, TT + t + 1)
                steps.then(V.reciprocal(RSTD2[:, t:t + 1], RSTD2[:, t:t + 1]))
                if t >= 2:
                    dve.wait_ge(tok_stored[t % 2], 16 * (t // 2))
                    dve.wait_ge(tokT_mm, t - 1)
                V.scalar_tensor_tensor(TOK[t % 2][:], X2[:, t, :], RSTD2[:, t:t + 1], NG2[:], ALU.mult, ALU.mult).then_inc(tok_ready, 1)

            logits = PS[:, 2, 0:TT * E].rearrange("p (t e) -> p t e", e=E)
            dve.wait_ge(logits_mm, TT)
            steps.then(V.reduce_max(RMAX[:], logits, AX_X))
            V.tensor_tensor(AFF[:], logits, RMAX[:, :, None].to_broadcast([P, TT, E]), ALU.subtract).then_inc(exp_in, 1)
            dve.wait_ge(exp_out, 1)
            steps.then(V.reduce_sum(RSUM[:], AFF[:], AX_X))
            steps.then(V.reciprocal(RSUM[:], RSUM[:]))
            for q in range(2):
                part = slice(q * LT, (q + 1) * LT)
                V.tensor_tensor(AFFW[:, :, 32 * q:32 * q + E], AFF[:, part, :], RSUM[:, part, None].to_broadcast([P, LT, E]),
                                ALU.mult).then_inc(aff_ready, 1)

            dve.wait_ge(rows_ready, 1)
            rows = ROWS[0]
            for r in range(CAP // 8):
                part = slice(8 * r, 8 * r + 8)
                steps.then(V.max(TOPV[:, part], rows[:]))
                steps.then(V.max_index(TOPI[:, part], TOPV[:, part], rows[:]))
                left = ROWS[1 + r % 2]
                if r + 1 < CAP // 8:
                    steps.then(V.match_replace(left[:], TOPV[:, part], rows[:], -1.0))
                rows = left
            steps.then(V.tensor_copy(TOPF[:], TOPI[:]))
            for q in range(2):
                rows_of, slots_of = slice(32 * q, 32 * q + E), slice(CAP * q, CAP * (q + 1))
                steps.then(V.tensor_copy(PAIR[:, 0, slots_of], TOPV[rows_of, :]))
                V.tensor_scalar(PAIR[:, 1, slots_of], TOPF[rows_of, :], float(L * q), None, ALU.add).then_inc(pair_ready, 1)
            dve.wait_ge(slots_mm, 2)
            V.tensor_copy(GATES[:], PS[:, 0, 0:E]).then_inc(slots_ready, 1)
            V.tensor_copy(SLOTS[:], PS[:, 1, 0:E]).then_inc(slots_ready, 1)

            def split_e(n, e, base):
                r, (tiles, width) = slot_of(n, e), place_of(*BODY[n][:2], 0)
                dve.wait_ge(e_hi, base + pos(n, e) + 1)
                q = pos_mod(n, e, SPLITS)
                low(ES[q][1][:, 0:tiles, 0:width], EW[r][:, 0:tiles, 0:width], ES[q][0][:, 0:tiles, 0:width], e_lo)

            def hidden(c, e, base):
                last_up = pos(BODY.index(("up", c, 1)), e)
                dve.wait_ge(e_used, base + last_up + 1)
                dve.wait_ge(silu_ready, NF * e + c + 1)
                ge(dve, hidT_mm, NF * e + c)
                w = FC[c][1]
                V.tensor_tensor(HID[:, 0:w], SG[:, 0:w], PS[:, 1, 0:w], ALU.mult).then_inc(hid_ready, 1)

            def hidT_low(c, e):
                dve.wait_ge(hidT_hi, NF * e + c + 1)
                tiles = FC[c][1] // P
                low(HIDT[1][:, 0:tiles, :].rearrange("p t n -> p (t n)"), PS[:, 6, 0:tiles * P],
                    HIDT[0][:, 0:tiles, :].rearrange("p t n -> p (t n)"), hidT_lo)

            def xsT_low(e):
                dve.wait_ge(xsT_hi, e + 1)
                low(XST[1][:].rearrange("p k n -> p (k n)"), PS[:, 6:8, :].rearrange("p a n -> p (a n)"),
                    XST[0][:].rearrange("p k n -> p (k n)"), xsT_lo)

            def dve_body(e, base, first):
                for n in range(NB):
                    if not (first and LEAD <= n < LEAD + SKIPPED):
                        split_e(n, e, base)
                    if n == (1 if first else 0):
                        xsT_low(e)
                    if n == 2 and not first:
                        hidT_low(2, e - 1)
                    if n == 5:
                        hidden(0, e, base)
                    if n == 8:
                        hidT_low(0, e)
                    if n == 11:
                        hidden(1, e, base)
                    if n == 14:
                        hidT_low(1, e)
                    if n == 17:
                        hidden(2, e, base)

            dve_body(0, 0, True)
            with dve.Fori(1, E) as e:
                dve_body(e, e * NB - SKIPPED, False)
            base = E * NB - SKIPPED
            for q in range(SKIPPED):
                count = base + q
                tiles = FC[2][1] // P
                dve.wait_ge(e_hi, count + 1)
                low(ES[count % SPLITS][1][:, 0:tiles, :], EW[count % RAWS][:, 0:tiles, :],
                    ES[count % SPLITS][0][:, 0:tiles, :], e_lo)
            hidT_low(2, E - 1)

            def final_rows(t):
                dve.wait_ge(roots, 2 * TT + t + 1)
                steps.then(V.reciprocal(RSTDF[:, t:t + 1], RSTDF[:, t:t + 1]))
                if t >= 2:
                    dve.wait_ge(fin_stored[t % 2], 16 * (t // 2))
                V.scalar_tensor_tensor(XO[t % 2][:], XF[t][:], RSTDF[:, t:t + 1], NGF[:], ALU.mult, ALU.mult).then_inc(fin_out, 1)

            dve.wait_ge(ngf_in, 16)
            for t in range(TT):
                dve.wait_ge(squares, TT + t + 1)
                V.tensor_scalar(RSTDF[:, t:t + 1], SUMSQF[:, t:t + 1], 1.0 / D, 1e-6, ALU.mult, ALU.add).then_inc(var_ready, 1)
                if t:
                    final_rows(t - 1)
            final_rows(TT - 1)

        @block.tensor
        def _(pe):
            def product(out, a, b, first, last):
                nc.tensor.matmul(out, a[0], b[0], start=first, stop=False)
                nc.tensor.matmul(out, a[0], b[1], start=False, stop=False)
                return nc.tensor.matmul(out, a[1], b[0], start=False, stop=last)

            pe.wait_ge(small_in, 16)
            for g in range(2 * KD):
                s, k = g // KD, g % KD
                pe.wait_ge(scaled, (s + 1) * LT)
                ge(pe, hT_lo, g - 3)
                for t in range(LT):
                    mm = nc.tensor.transpose(PS[:, g % 4, t * P:(t + 1) * P], X[:, s * LT + t, k * P:(k + 1) * P], IDENT)
                mm.then_inc(xT_ready, 1)
            pe.wait_ge(hT_lo, 2 * KD)

            def filter_layer(layer):
                pe.wait_ge(ffn_in, 16)
                pe.wait_ge(zpos_in, 16)
                ge(pe, mlp_sin, layer)
                rows = zpos.shape[0] if layer == 0 else FFN
                src = ZP[:] if layer == 0 else FH[layer - 1][:]
                nc.tensor.matmul(PS[0:FFN, 6, :], FF[0:rows, layer * FFN:(layer + 1) * FFN], src,
                                 start=True, stop=True).then_inc(mlp_mm, 1)

            filter_layer(0)
            for s, i, j in UNITS:
                pe.wait_ge(w_lo, split_count((s, i, j)))
                before = unit_before((s, i, j))
                if before:
                    bs, bi, bj = before
                    if bs == 0 and bj % 2 == 0:
                        pe.wait_ge(z_free, 2 * bi + bj // 2 + 1)
                    elif bs == 0:
                        pe.wait_ge(a_ready, 2 * bi + bj // 2 + 1)
                    elif bs == 1:
                        pe.wait_ge(z_free, KC + 3 * bi + bj + 1)
                    else:
                        pe.wait_ge(g_ready, 4 * bi + bj + 1)
                if s == 2 and i == 0 and j == 3:
                    pe.wait_ge(vT_lo, 2 * KC)
                if (s, i, j) == (0, 0, 3):
                    pe.wait_ge(mlp_arg, 3)
                for k in range(KD):
                    for q in range(2):
                        mm = product(PS[:, 2 * j + q, :], (SPLIT[j][0][:, k, :], SPLIT[j][1][:, k, :]),
                                     (HT[0][:, k, q * L:(q + 1) * L], HT[1][:, k, q * L:(q + 1) * L]), k == 0, k == KD - 1)
                mm.then_inc(w_used, 1)
                if s == 0 and i == 0 and j < 2:
                    filter_layer(j + 1)
                if s == 1 and j == 2:
                    pe.wait_ge(v_ready, i + 1)
                    if i == 0:
                        pe.wait_ge(a_ready, KC)
                    for q in range(2):
                        ge(pe, vT_lo, 2 * (i - 1) + q + 1)
                        for t in range(LT):
                            mm = nc.tensor.transpose(PS[:, 6 + q, t * P:(t + 1) * P], SHORTS[1][:, q, t * P:(t + 1) * P], IDENT)
                        mm.then_inc(vT_mm, 1)

            pe.wait_ge(g_ready, 4 * SECTIONS[2][0])
            pe.wait_ge(w4_in, 16)
            pe.wait_ge(ones_set, 4)

            def taps(lt):
                ge(pe, taps_ready, lt)
                for q in range(2):
                    mm = nc.tensor.matmul(PS[:, 4 + q, :], FH[2][:, lt * P:(lt + 1) * P], W4[:, q * DC:(q + 1) * DC],
                                          start=True, stop=True)
                mm.then_inc(taps_mm, 1)

            def norm(lt):
                pe.wait_ge(abs_ready, lt + 1)
                for q in range(2):
                    mm = nc.tensor.matmul(PS[:, 6, :], ONES[:], HABS[:, q * DC:(q + 1) * DC],
                                          start=lt == 0 and q == 0, stop=lt == LT - 1 and q == 1)
                mm.then_inc(norm_mm, 1)

            for lt in range(LT):
                taps(lt)
                if lt:
                    norm(lt - 1)
            norm(LT - 1)
            pe.wait_ge(conv_done, KC)
            for ct in range(KC):
                for q in range(2):
                    mm = nc.tensor.matmul(PS[:, q, :], ONES[:], CONV[:, ct, q, :], start=ct == 0, stop=ct == KC - 1)
            mm.then_inc(ln_mm, 1)
            pe.wait_ge(norm_row, 1)
            for ct in range(KC):
                mm = nc.tensor.matmul(PS[:, 7, ct:ct + 1], NROW[:, ct * P:(ct + 1) * P], IDENT[0:1, 0:1], start=True, stop=True)
            mm.then_inc(norm_col, 1)

            def table_tile(table, n, f):
                return table[0][:, n, f * P:(f + 1) * P], table[1][:, n, f * P:(f + 1) * P]

            def spectrum(f):
                if f == 0:
                    pe.wait_ge(cos_lo, 1)
                    pe.wait_ge(sin_lo, 1)
                    pe.wait_ge(eo_lo, LT)
                elif f == 1:
                    pe.wait_ge(skip_norm, 1)
                    pe.wait_ge(norm_col, 2)
                else:
                    pe.wait_ge(k_ready, 2 * (f - 1))
                for q, table in enumerate((COS, SIN)):
                    bank = 4 + 2 * (f % 2) + q
                    for n in range(LT):
                        mm = product(PS[:, bank, :], table_tile(table, n, f), (EO[0][:, n, q, :], EO[1][:, n, q, :]),
                                     n == 0, n == LT - 1)
                mm.then_inc(k_mm, 1)

            spectrum(0)
            spectrum(1)
            for ct in range(KC):
                pe.wait_ge(ln_sq, ct + 1)
                for q in range(2):
                    mm = nc.tensor.matmul(PS[:, 2 + q, :], ONES[:], LNSQ[:, q, :], start=ct == 0, stop=ct == KC - 1)
                if ct < KC - 1:
                    mm.then_inc(ln_used, 1)
            mm.then_inc(ln_mm, 1)
            spectrum(2)
            spectrum(3)

            def transform(s, f):
                n = s * LT + f
                if n < 2:
                    pe.wait_ge(ln_root, 1)
                    pe.wait_ge(ln_x, KC)
                else:
                    pe.wait_ge(u_used, n - 1)
                for q, table in enumerate((COS, SIN)):
                    for m in range(LT):
                        mm = product(PS[:, 2 * (f % 2) + q, :], table_tile(table, m, f),
                                     (VT[0][:, s * LT + m, :], VT[1][:, s * LT + m, :]), m == 0, m == LT - 1)
                mm.then_inc(u_mm, 1)

            def back(s):
                pe.wait_ge(y_lo, 2 * LT * (s + 1))
                pe.wait_ge(k_ready, 2 * LT)
                for ct in range(KC):
                    ge(pe, uy_ready, s * KC + ct - 1)
                    part = slice(ct * P, (ct + 1) * P)
                    for f in range(LT):
                        for q, (y, table) in enumerate(((YRE, COS), (YIM, SIN))):
                            mm = product(PS[:, 4 + ct % 2, :], (y[0][:, f, part], y[1][:, f, part]),
                                         (table[0][:, f, :], table[1][:, f, :]), f == 0 and q == 0, f == LT - 1 and q == 1)
                    mm.then_inc(y_mm, 1)

            pe.wait_ge(vT_lo, 2 * KC)
            for f in range(LT):
                transform(0, f)
            transform(1, 0)
            transform(1, 1)
            back(0)
            transform(1, 2)
            transform(1, 3)
            back(1)

            pe.wait_ge(at_lo, KC)
            pe.wait_ge(u_used, 2 * LT)
            for n in range(2 * KD):
                j = n % 4
                pe.wait_ge(o_lo, n + 1)
                if n == 0:
                    pe.wait_ge(uy_ready, 2 * KC)
                ge(pe, m_free, n - 3)
                src = (AT, UB)[n % 2]
                if n == 1:
                    pe.wait_ge(ub_lo, 2 * KC)
                for k in range(KC):
                    for q in range(2):
                        mm = product(PS[:, 2 * j + q, :], (OUT_SPLIT[j][0][:, k, :], OUT_SPLIT[j][1][:, k, :]),
                                     (src[0][:, k, q, :], src[1][:, k, q, :]), k == 0, k == KC - 1)
                mm.then_inc(o_used, 1)

            def mixed(k, t):
                part = slice((t % LT) * P, (t % LT + 1) * P)
                return MT[0][:, k, t // LT, part], MT[1][:, k, t // LT, part]

            for k in range(KD):
                pe.wait_ge(o_lo, 2 * KD + k + 1)
                pe.wait_ge(m_lo, k + 1)
                for t in range(TT):
                    if k == 0:
                        pe.wait_ge(m_free, 2 * KD - 2 + max(t // 2 - 1, 0))
                    mm = product(PS[:, t, :], mixed(k, t), (WO_SPLIT[wo_slot(k)][0][:], WO_SPLIT[wo_slot(k)][1][:]),
                                 k == 0, k == KD - 1)
                    if k == KD - 1:
                        mm.then_inc(x2_mm, 1)
                    elif t == TT - 1:
                        mm.then_inc(o_used, 1)

            def second_half(t):
                pe.wait_ge(x2_ready, t + 1 if t < 2 else TT + t - 1)
                for k in range(KD):
                    if t == 0:
                        pe.wait_ge(o_lo, 3 * KD + k + 1)
                    slot = WO_SPLIT[wo_slot(KD + k)]
                    mm = product(PS[:, t % 2, :], mixed(k, t), (slot[0][:], slot[1][:]), k == 0, k == KD - 1)
                mm.then_inc(x2_mm, 1)

            def tokens_T(t):
                pe.wait_ge(tok_ready, t + 1)
                pe.wait_ge(x2_ready, TT)
                ge(pe, tokT_ready, t - 1)
                for k in range(KD):
                    mm = nc.tensor.transpose(PS[:, 4 + 2 * (t % 2) + k // 4, (k % 4) * P:(k % 4 + 1) * P],
                                             TOK[t % 2][:, k * P:(k + 1) * P], IDENT)
                mm.then_inc(tokT_mm, 1)

            def logits(t):
                pe.wait_ge(tokT_ready, t + 1)
                for k in range(KD):
                    mm = nc.tensor.matmul(PS[:, 2, t * E:(t + 1) * E], TOKT[t % 2][:, k, :], col("router", k * E, E),
                                          start=k == 0, stop=k == KD - 1)
                mm.then_inc(logits_mm, 1)

            for t in range(TT + 2):
                if t < TT:
                    second_half(t)
                if 1 <= t <= TT:
                    tokens_T(t - 1)
                if t >= 2:
                    logits(t - 2)
            pe.wait_ge(aff_ready, 2)
            for t in range(LT):
                mm = nc.tensor.transpose(PS[0:48, 3, t * P:(t + 1) * P], AFFW[:, t, :], IDENT)
            mm.then_inc(affT_mm, 1)
            pe.wait_ge(pair_ready, 2)
            for q in range(2):
                nc.tensor.transpose(PS[:, q, 0:E], PAIR[:, q, :], IDENT[0:E, 0:E]).then_inc(slots_mm, 1)

            def tokens_of(e):
                pe.wait_ge(xs_in, (e + 1) * 16)
                for k in range(KD):
                    mm = nc.tensor.transpose(PS[:, 6 + k // 4, (k % 4) * P:(k % 4 + 1) * P], XS[:, k * P:(k + 1) * P], IDENT)
                mm.then_inc(xsT_mm, 1)

            def hidden_T(c, e):
                pe.wait_ge(hid_ready, NF * e + c + 1)
                for t in range(FC[c][1] // P):
                    mm = nc.tensor.transpose(PS[:, 6, t * P:(t + 1) * P], HID[:, t * P:(t + 1) * P], IDENT)
                mm.then_inc(hidT_mm, 1)

            def gate_up(c, e, base):
                for n, (kind, cc, kh) in enumerate(BODY):
                    if kind == "down" or cc != c:
                        continue
                    w = FC[c][1]
                    q = pos_mod(n, e, SPLITS)
                    pe.wait_ge(e_lo, base + pos(n, e) + 1)
                    bank = 0 if kind == "gate" else 1
                    if kh == 0 and kind == "gate":
                        ge(pe, hid_ready, NF * e + c)
                    for t in range(4):
                        k = 4 * kh + t
                        mm = product(PS[:, bank, 0:w], (XST[0][:, k, :], XST[1][:, k, :]),
                                     (ES[q][0][:, t, 0:w], ES[q][1][:, t, 0:w]), k == 0, k == KD - 1)
                    mm.then_inc(e_used, 1)

            def down(c, e, counts):
                tiles = FC[c][1] // P
                pe.wait_ge(hidT_lo, NF * e + c + 1)
                if c == 0:
                    ge(pe, ye_ready, e)
                for dh in range(2):
                    count, q = counts[dh]
                    pe.wait_ge(e_lo, count + 1)
                    for t in range(tiles):
                        mm = product(PS[:, 4 + dh, :], (HIDT[0][:, t, :], HIDT[1][:, t, :]),
                                     (ES[q][0][:, t, :], ES[q][1][:, t, :]), c == 0 and t == 0, c == NF - 1 and t == tiles - 1)
                    mm.then_inc(e_used, 1)

            def down_counts(c, e, base):
                ns = [BODY.index(("down", c, dh)) for dh in range(2)]
                return [(base + pos(n, e), pos_mod(n, e, SPLITS)) for n in ns]

            def pe_body(e, base, first, last):
                gate_up(0, e, base)
                if not first:
                    down(2, e - 1, down_counts(2, e, base))
                hidden_T(0, e)
                gate_up(1, e, base)
                down(0, e, down_counts(0, e, base))
                hidden_T(1, e)
                gate_up(2, e, base)
                pe.wait_ge(hidT_lo, NF * e + 2)
                if not last:
                    tokens_of(e + 1)
                down(1, e, down_counts(1, e, base))
                if not last:
                    pe.wait_ge(xsT_lo, e + 2)
                hidden_T(2, e)

            tokens_of(0)
            pe.wait_ge(xsT_lo, 1)
            pe_body(0, 0, True, False)
            with pe.Fori(1, E - 1) as e:
                pe_body(e, e * NB - SKIPPED, False, False)
            pe_body(E - 1, (E - 1) * NB - SKIPPED, False, True)
            base = E * NB - SKIPPED
            down(2, E - 1, [(base + dh, (base + dh) % SPLITS) for dh in range(2)])


def kernel(**inputs):
    import numpy as np
    import concourse.bacc as bacc
    from concourse.bass_utils import run_bass_kernel_spmd

    def w(name):
        return np.asarray(inputs[name])[0]

    f32 = np.float32
    xp, xs = np.asarray(inputs["x_prompt"])[0], np.asarray(inputs["x_sample"])[0]
    L, D = xp.shape
    DC = w("conv_w_out").shape[0]
    PROJ = w("w_in").shape[1]
    E = w("router_w").shape[1]
    TAPS, SHORT = w("conv_dw_w").shape[0], w("hy_short_w").shape[0]

    def columns(a):
        return a.reshape(-1, P).T

    def columns_taps(a):
        return a.reshape(a.shape[0], -1, P).transpose(2, 1, 0).reshape(P, -1)

    f = np.arange(L)
    half = np.pi * (2 * f + 1) / (4 * L)
    angle = np.pi * np.outer(2 * f + 1, 2 * f + 1) / (4 * L)
    parts = {
        "b_in": columns(w("b_in")), "dw_w": columns_taps(w("conv_dw_w")), "dw_b": columns(w("conv_dw_b")),
        "ln_g": columns(w("conv_ln_g")), "ln_b": columns(w("conv_ln_b")), "conv_b": columns(w("conv_b_out")),
        "short_w": columns_taps(w("hy_short_w")), "short_b": columns(w("hy_short_b")), "hy_b": columns(w("hy_b_out")),
        "norm1": columns(w("norm1_g")), "cos_half": columns(np.cos(half).astype(f32)),
        "sin_half": columns(np.sin(half).astype(f32)),
        "router": w("router_w").reshape(-1, P, E).transpose(1, 0, 2).reshape(P, -1), "ident": np.eye(P, dtype=f32),
    }
    where, _ = small_columns(D, DC, PROJ, TAPS, SHORT, E)
    small = np.concatenate([parts[name] for name in where], axis=1)
    w1 = w("hy_f_w1")
    N = w1.shape[1]
    ffn = np.concatenate([np.concatenate([w1, np.zeros((N - w1.shape[0], N), f32)]), w("hy_f_w2"), w("hy_f_w3"),
                          np.stack([w("hy_f_b1"), w("hy_f_b2"), w("hy_f_b3"), w("hy_f_freq")], axis=1)], axis=1)
    bands_n = (w1.shape[0] - 1) // 2
    time = np.linspace(0.0, 1.0, L, dtype=f32)[:, None]
    turn = (f32(2.0 * math.pi) * np.arange(L, dtype=f32)[:, None] / f32(L)).astype(f32)
    bands = np.linspace(1e-4, bands_n - 1, bands_n, dtype=f32)[None, :]
    zpos = np.concatenate([time, np.cos(bands * turn), -np.sin(bands * turn)], axis=1).astype(f32).T
    deltas = np.linspace(math.log(1e-2) / 1.5, math.log(1e-2) / 0.3, DC, dtype=f32)
    decay = np.exp(-time * np.abs(deltas)[None, :]).astype(f32)
    arrays = {
        "x_prompt": xp, "x_sample": xs, "small": small, "ffn": ffn, "ffn_w4": w("hy_f_w4"), "zpos": zpos, "decay": decay,
        "cosine": np.cos(angle).astype(f32), "sine": np.sin(angle).astype(f32),
        "w_in": w("w_in"), "conv_w_out": w("conv_w_out"), "hy_w_out": w("hy_w_out"), "w_o": w("w_o"),
        "hy_skip": np.asarray(inputs["hy_skip"]), "norm2_g": np.asarray(inputs["norm2_g"]),
        "norm_f_g": np.asarray(inputs["norm_f_g"]).reshape(1, D),
        "w_gate": w("exp_w_gate"), "w_up": w("exp_w_up"), "w_down": w("exp_w_down"),
    }
    arrays = {f"in_{k}": np.ascontiguousarray(v) for k, v in arrays.items()}
    nc = bacc.Bacc("TRN2", target_bir_lowering=False, num_devices=1)
    args = [nc.dram_tensor(k, a.shape, mybir.dt.from_np(a.dtype), kind="ExternalInput").ap() for k, a in arrays.items()]
    args += [nc.dram_tensor(k, (L, D), F32, kind="ExternalOutput").ap() for k in ("out_prompt", "out_sample")]
    hybrid_encoder_kernel(nc, *args)
    result = run_bass_kernel_spmd(nc, [arrays], core_ids=[0]).results[0]
    return result["out_prompt"].reshape(1, L, D), result["out_sample"].reshape(1, L, D)
```

```python
from contextlib import ExitStack
import math

import concourse.bass as bass
from concourse import mybir

P = 128
F32 = mybir.dt.float32
F32R = mybir.dt.float32r
U32 = mybir.dt.uint32
ALU = mybir.AluOpType
ACT = mybir.ActivationFunctionType
AX_X = mybir.AxisListType.X
KB = 1024
SBUF_BASE = 16 * KB + 128

TWO_PI_HEAD = 6.28125
TWO_PI_TAIL = 2.0 * math.pi - TWO_PI_HEAD
ROUNDER = 1.5 * 2.0 ** 23


def small_columns(D, DC, PROJ, TAPS, SHORT, E):
    widths = [
        ("b_in", PROJ // P), ("dw_w", DC // P * TAPS), ("dw_b", DC // P), ("ln_g", DC // P), ("ln_b", DC // P),
        ("conv_b", D // P), ("short_w", 3 * DC // P * SHORT), ("short_b", 3 * DC // P), ("hy_b", D // P),
        ("norm1", D // P), ("norm2", D // P), ("cos_half", DC // P), ("sin_half", DC // P), ("router", D // P * E), ("ident", P),
    ]
    at, where = 0, {}
    for name, width in widths:
        where[name] = (at, width)
        at += width
    return where, at


def hybrid_encoder_kernel(
    nc: bass.Bass,
    x_prompt: bass.AP,
    x_sample: bass.AP,
    small: bass.AP,
    ffn: bass.AP,
    ffn_w4: bass.AP,
    zpos: bass.AP,
    decay: bass.AP,
    cosine: bass.AP,
    sine: bass.AP,
    w_in: bass.AP,
    conv_w_out: bass.AP,
    hy_w_out: bass.AP,
    w_o: bass.AP,
    hy_skip: bass.AP,
    norm2_g: bass.AP,
    norm_f_g: bass.AP,
    w_gate: bass.AP,
    w_up: bass.AP,
    w_down: bass.AP,
    y_prompt: bass.AP,
    y_sample: bass.AP,
):
    L, D = x_prompt.shape
    PROJ = w_in.shape[1]
    DC = conv_w_out.shape[0]
    E, _, F = w_gate.shape
    FFN = ffn.shape[0]
    TAPS, SHORT = 31, 3
    PAD = TAPS // 2
    CAP = 2 * L // E
    KD, KC, LT = D // P, DC // P, L // P
    TT = 2 * LT
    where, small_n = small_columns(D, DC, PROJ, TAPS, SHORT, E)
    assert L == 512 and D == 1024 and DC == 512 and 2 * CAP == P and E == 16

    x0_dram = nc.dram_tensor("x0_spill", [KC, P, 2 * L], F32, kind="Internal").ap()
    gate_dram = nc.dram_tensor("gate_spill", [2 * KD, P, 2 * L], F32, kind="Internal").ap()
    tok_dram = nc.dram_tensor("tok_rows", [2 * L, D], F32, kind="Internal").ap()
    acc_dram = nc.dram_tensor("acc_rows", [2 * L, D], F32, kind="Internal").ap()

    ctx = ExitStack()
    with ctx:
        def at(name, kib, shape, dt=F32):
            return nc.alloc_sbuf_tensor_at(name, shape, dt, offset=SBUF_BASE + int(kib * KB))

        SM = at("small_params", 0, [P, small_n])
        ROUTER = SM[:, where["router"][0]:where["router"][0] + KD * E].rearrange("p (k e) -> p k e", e=E)
        IDENT = SM[:, where["ident"][0]:where["ident"][0] + P]
        ONES = at("ones", 2.5, [P, P])
        SUMSQ = at("sum_squares", 3.5, [P, TT])
        RSTD = at("rstd", 3.5625, [P, TT])
        SUMSQ2 = at("sum_squares2", 3.625, [P, TT, 2])
        RSTD2 = at("rstd2", 3.75, [P, TT])
        SUMSQF = at("sum_squares_f", 3.8125, [P, TT])
        RSTDF = at("rstd_f", 3.875, [P, TT])
        AFF = at("affinity", 4.0, [P, TT, E])
        AFFW = at("affinity_wide", 6.75, [P, LT, 48])
        NORMC = at("filter_norm_column", 7.5, [P, KC])
        RSUM = at("softmax_sum", 4.5, [P, TT])
        RMAX = at("softmax_max", 4.5625, [P, TT])
        TOPV = at("top_values", 4.625, [48, CAP])
        TOPI = at("top_index", 4.875, [48, CAP], U32)
        TOPF = at("top_index_float", 5.125, [48, CAP])
        PAIR = at("slots_of_experts", 5.375, [E, 2, P])
        GATES = at("slot_gates", 6.375, [P, E])
        SLOTS = at("slot_rows", 6.4375, [P, E], U32)
        NEXT_ROWS = at("rows_to_gather", 6.5, [P, 1], U32)
        DONE_ROWS = at("rows_to_scatter", 6.53125, [P, 1], U32)
        EPS = at("eps", 6.59375, [P, 3])

        HT = (at("hT_hi", 8, [P, KD, 2 * L], F32R), at("hT_lo", 40, [P, KD, 2 * L], F32R))
        X = at("x_rows", 120, [P, TT, D])
        RAW = [at(f"w_raw{j}", 72 + 4 * j, [P, KD, P]) for j in range(4)]
        SPLIT = [(at(f"w_hi{j}", 88 + 8 * j, [P, KD, P], F32R), at(f"w_lo{j}", 92 + 8 * j, [P, KD, P], F32R))
                 for j in range(4)]
        VT = (at("v_rows_hi", 120, [P, TT, DC], F32R), at("v_rows_lo", 136, [P, TT, DC], F32R))
        APAD = at("a_padded", 152, [P, KC, 2, L + 2 * PAD])
        CONV = at("conv_sum", 169, [P, KC, 2, L])
        FF = at("ffn_params", 185, [FFN, ffn.shape[1]])
        ZP = at("zpos", 186, [zpos.shape[0], L])
        FARG = at("sin_argument", 188, [FFN, L])
        FK = at("sin_turns", 190, [FFN, L])
        FH = [at("filter_h1", 192, [FFN, L]), at("filter_h2", 194, [FFN, L]), at("filter_h3", 205.5, [FFN, L])]
        SQOUT = [at(f"square_out{i}", 185 - 16 + 4 * i, [P, D]) for i in range(2)]
        SIG = [at(f"sigmoid{i}", 197.5 + 4 * i, [P, 2, L]) for i in range(2)]
        ZPAD = [at(f"z_padded{j}", 185 + 4.0625 * j, [P, 2, L + 2]) for j in range(3)]
        SHORTS = [at(f"short_conv{i}", 197.25 + 4 * i, [P, 2, L]) for i in range(2)]
        GSTAGE = [at(f"gate_stage{j}", 185 + 4 * j, [P, 2, L]) for j in range(2)]
        COS = (at("cos_hi", 8, [P, LT, L], F32R), at("cos_lo", 16, [P, LT, L], F32R))
        SIN = (at("sin_hi", 24, [P, LT, L], F32R), at("sin_lo", 32, [P, LT, L], F32R))
        TABLE_RAW = [at("cos_raw", 72, [P, LT, L]), at("sin_raw", 80, [P, LT, L])]
        DECAY = at("decay", 193, [P, LT, DC])
        W4 = at("w4", 201.25, [FFN, 2 * DC])
        HF = [at(f"filter_taps{i}", 56 + 4 * i, [P, 2 * DC]) for i in range(2)]
        HSUM = at("filter_even_odd", 64, [P, 2 * DC])
        HABS = at("filter_abs", 68, [P, 2 * DC])
        SKIPN = at("skip_times_norm", 72, [P, DC])
        SKIP = at("skip", 74, [P, DC])
        NROW = at("norm_row", 76, [1, DC])
        EO = (at("even_odd_hi", 88, [P, LT, 2, DC], F32R), at("even_odd_lo", 104, [P, LT, 2, DC], F32R))
        KR = at("filter_re", 40, [P, LT, DC])
        KI = at("filter_im", 48, [P, LT, DC])
        KTMP = [at("spectrum_tmp0", 78, [P, DC]), at("spectrum_tmp1", 205.5, [P, DC])]
        YRE = (at("y_re_hi", 88, [P, LT, DC], F32R), at("y_re_lo", 96, [P, LT, DC], F32R))
        YIM = (at("y_im_hi", 104, [P, LT, DC], F32R), at("y_im_lo", 112, [P, LT, DC], F32R))
        YT = [at(f"product{i}", 185 + 2 * i, [P, DC]) for i in range(4)]
        X0 = at("x0", 193, [P, KC, L])
        YV = [at(f"spectrum_sum{i}", 201 + 2 * i, [P, DC]) for i in range(2)]
        UB = (at("hyena_out_hi", 56, [P, KC, 2, L], F32R), at("hyena_out_lo", 72, [P, KC, 2, L], F32R))
        LNSQ = [at(f"ln_square{i}", 185 + 4 * i, [P, 2, L]) for i in range(2)]
        LNRS = at("ln_rstd", 164, [P, 2, L])
        AT = (at("conv_out_hi", 152, [P, KC, 2, L], F32R), at("conv_out_lo", 169, [P, KC, 2, L], F32R))
        OUT_RAW = [at(f"wout_raw{j}", 120 + 2 * j, [P, KC, P]) for j in range(4)]
        OUT_SPLIT = [(at(f"wout_hi{j}", 128 + 4 * j, [P, KC, P], F32R), at(f"wout_lo{j}", 130 + 4 * j, [P, KC, P], F32R))
                     for j in range(4)]
        GIN = [at(f"gate_in{j}", 185 + 4 * j, [P, 2, L]) for j in range(4)]
        MT = (at("mixed_hi", 8, [P, KD, 2, L], F32R), at("mixed_lo", 88, [P, KD, 2, L], F32R))
        WO_RAW = [at(f"wo_raw{j}", 120 + 2 * j, [P, L]) for j in range(4)]
        WO_SPLIT = [(at(f"wo_hi{j}", 128 + 4 * j, [P, L], F32R), at(f"wo_lo{j}", 130 + 4 * j, [P, L], F32R))
                    for j in range(4)]
        WO_SPLIT += [(at(f"wo_hi{4 + j}", 72 + 4 * j, [P, L], F32R), at(f"wo_lo{4 + j}", 74 + 4 * j, [P, L], F32R))
                     for j in range(4)]
        X2 = at("x2_rows", 40, [P, TT, D])
        XRES = [at(f"x_again{i}", 144 + 2 * i, [P, 512]) for i in range(4)]
        TOK = [at(f"tok_rows{i}", 152 + 4 * i, [P, D]) for i in range(2)]
        X2T = [at(f"x2_T{i}", 160 + 4 * i, [P, KD, P]) for i in range(2)]
        NG2 = at("norm2_g_all", 168, [P, D])
        SQOUT2 = at("square2_out", 172, [P, 512])
        ROWS = [at(f"affinity_rows{i}", 144 + 2 * i, [48, L]) for i in range(3)]
        raw_at = [174, 182, 190, 198, 8, 16, 24, 32, 72, 80, 88, 96, 104, 40, 48, 56, 64, 164]
        EARLY = 4
        BEFORE_ROUTER = 13
        RAWS = len(raw_at)
        FLYING = 3
        EW = [at(f"expert_raw{j}", k, [P, 4, 512]) for j, k in enumerate(raw_at)]
        SPLITS = 3
        ES = [at(f"expert_hi{j}", 112 + 8 * j, [P, 4, 512], F32R) for j in range(SPLITS)]
        EL = [at(f"expert_lo{j}", k, [P, 4, 512], F32R) for j, k in enumerate(raw_at)]
        XS = at("slot_tokens", 136, [P, D])
        XST = (at("slot_tokens_T_hi", 140, [P, KD, P], F32R), at("slot_tokens_T_lo", 144, [P, KD, P], F32R))
        SG = at("silu_gate", 148, [P, 512])
        HID = at("hidden", 150, [P, 512])
        HIDT = (at("hidden_T_hi", 152, [P, 4, P], F32R), at("hidden_T_lo", 154, [P, 4, P], F32R))
        YE = at("expert_out", 156, [P, D])
        NGF = at("norm_f_g_all", 160, [P, D])
        XF = [at(f"final_rows{i}", 32 + 4 * i, [P, D]) for i in range(8)]

        PS = ctx.enter_context(nc.psum_tensor("ps", [P, 8, 512], F32))

        def sem(name):
            return ctx.enter_context(nc.semaphore(name))

        def sems(name, n):
            return [sem(f"{name}{i}") for i in range(n)]

        def col(name, i=0, n=1):
            a = where[name][0]
            return SM[:, a + i:a + i + n]

        small_in, ffn_in, zpos_in = sem("small_in"), sem("ffn_in"), sem("zpos_in")
        x_in = sems("x_in", TT)
        ones_set, pads_set = sem("ones_set"), sem("pads_set")
        a_step, v_step = sem("act_step"), sem("dve_step")
        squares, roots, scaled = sem("squares"), sem("roots"), sem("x_scaled")
        var_ready, root_table = sem("var_ready"), sem("root_table")
        xT_ready, hT_hi, hT_lo = sem("xT_ready"), sem("hT_hi"), sem("hT_lo")
        mlp_mm, mlp_arg, mlp_sin = sem("mlp_mm"), sem("mlp_arg"), sem("mlp_sin")
        w_landed = sems("w_landed", 4)
        w_hi, w_lo, w_used, z_free = sem("w_hi"), sem("w_lo"), sem("w_used"), sem("z_free")
        a_ready = sem("a_ready")
        z_padded, short_mid, short_done = sem("z_padded"), sem("short_mid"), sem("short_done")
        v_ready, x0_stored = sem("v_ready"), sem("x0_stored")
        vT_mm, vT_hi, vT_lo = sem("vT_mm"), sem("vT_hi"), sem("vT_lo")
        g_ready, g_stored = sem("g_ready"), sems("g_stored", 2)
        conv_done = sem("conv_done")
        table_in, table_hi, cos_lo, sin_lo = sem("table_in"), sem("table_hi"), sem("cos_lo"), sem("sin_lo")
        decay_in, w4_in, skip_in = sem("decay_in"), sem("w4_in"), sem("skip_in")
        taps_mm, taps_ready, abs_ready, norm_mm, eo_sum, eo_hi, eo_lo = (
            sem("taps_mm"), sem("taps_ready"), sem("abs_ready"), sem("norm_mm"), sem("eo_sum"), sem("eo_hi"), sem("eo_lo"))
        norm_row, norm_col = sem("norm_row"), sem("norm_col")
        k_mm, k_ready = sem("k_mm"), sem("k_ready")
        u_mm, u_used, y_val, y_hi, y_lo = sem("u_mm"), sem("u_used"), sem("y_val"), sem("y_hi"), sem("y_lo")
        x0_in, y_mm, uy_ready, ub_hi, ub_lo = sem("x0_in"), sem("y_mm"), sem("uy_ready"), sem("ub_hi"), sem("ub_lo")
        skip_norm = sem("skip_norm")
        ln_mm, ln_used = sem("ln_mm"), sem("ln_used")
        ln_sq, ln_root, ln_x, at_hi, at_lo = (
            sem("ln_sq"), sem("ln_root"), sem("ln_x"), sem("at_hi"), sem("at_lo"))
        o_landed = sems("o_landed", 4)
        o_hi, o_lo, o_used = sem("o_hi"), sem("o_lo"), sem("o_used")
        gin_in = sems("gin_in", 4)
        m_free, m_val, m_hi, m_lo = sem("m_free"), sem("m_val"), sem("m_hi"), sem("m_lo")
        x2_mm, x2_ready, x2_sq = sem("x2_mm"), sem("x2_ready"), sem("x2_sq")
        ng2_in, ngf_in = sem("ng2_in"), sem("ngf_in")
        tok_ready, tok_stored, acc_stored = sem("tok_ready"), sems("tok_stored", 2), sem("acc_stored")
        x2T_mm, x2T_ready, logits_mm, router_ready = sem("x2T_mm"), sem("x2T_ready"), sem("logits_mm"), sem("router_ready")
        aff_ready, affT_mm, rows_ready, pair_ready, slots_mm, slots_ready = (
            sem("aff_ready"), sem("affT_mm"), sem("rows_ready"), sem("pair_ready"),
            sem("slots_mm"), sem("slots_ready"))
        exp_in, exp_out = sem("softmax_shifted"), sem("softmax_exp")
        e_landed = sems("e_landed", RAWS)
        e_hi, e_lo, e_used = sem("e_hi"), sem("e_lo"), sem("e_used")
        rows_next, xs_in, xsT_mm, xsT_hi, xsT_lo = (
            sem("rows_next"), sem("xs_in"), sem("xsT_mm"), sem("xsT_hi"), sem("xsT_lo"))
        silu_ready, hid_ready, hidT_mm, hidT_hi, hidT_lo = (
            sem("silu_ready"), sem("hid_ready"), sem("hidT_mm"), sem("hidT_hi"), sem("hidT_lo"))
        ye_ready, rows_done, added = sem("ye_ready"), sem("rows_done"), sem("rows_added")
        fin_out, fin_stored = sem("fin_ready"), sem("fin_stored")

        block = ctx.enter_context(nc.Block())

        def ge(eng, s, value):
            if not isinstance(value, int) or value > 0:
                eng.wait_ge(s, value)

        class Steps:

            def __init__(self, eng, s):
                self.eng, self.sem, self.n = eng, s, 0

            def did(self, ins):
                ins.then_inc(self.sem, 1)
                self.n += 1

            def wait(self):
                self.eng.wait_ge(self.sem, self.n)

            def then(self, ins):
                self.did(ins)
                self.wait()

        CONV_SEC = (2, 4, lambda i, j: 2 * i + j // 2 + (KC if j % 2 == 0 else 0))
        HYENA_SEC = (KC, 3, lambda i, j: 2 * KC + (KC, 2 * KC, 0)[j] + i)
        GATE_SEC = (4, 4, lambda i, j: 5 * KC + 4 * i + j)
        SECTIONS = [CONV_SEC, HYENA_SEC, GATE_SEC]
        UNITS = [(s, i, j) for s in range(3) for i in range(SECTIONS[s][0]) for j in range(SECTIONS[s][1])]

        def use_of(s, i, j):
            return sum(n for n, width, _ in SECTIONS[:s] if j < width) + i

        def unit_after(s, i, j):
            if i + 1 < SECTIONS[s][0]:
                return s, i + 1, j
            for t in range(s + 1, 3):
                if j < SECTIONS[t][1]:
                    return t, 0, j
            return None

        SPLIT_ORDER = [(0, 0, j) for j in range(4)] + [unit_after(*u) for u in UNITS if unit_after(*u)]

        def split_count(u):
            return SPLIT_ORDER.index(u) + 1

        def used_count(u):
            return UNITS.index(u) + 1

        def unit_before(u):
            return next((v for v in UNITS if unit_after(*v) == u), None)

        def seq_rows(t):
            src = x_prompt if t < LT else x_sample
            return src[(t % LT) * P:(t % LT + 1) * P, :]

        FC = [(a, min(512, F - a)) for a in range(0, F, 512)]
        NF = len(FC)
        GU_UNITS = [(kind, c, kh) for c in range(NF) for kh in range(2) for kind in ("gate", "up")]

        def down_units(c):
            return [("down", c, dh) for dh in range(2)]

        def gu_units(c):
            return [u for u in GU_UNITS if u[1] == c]

        BODY = gu_units(0) + down_units(2) + gu_units(1) + down_units(0) + gu_units(2) + down_units(1)
        NB = len(BODY)
        LEAD = len(gu_units(0))
        SKIPPED = len(down_units(2))

        def src_of(kind, c, k, e):
            a, n = FC[c]
            if kind == "down":
                tiles = n // P
                return w_down[bass.ds(e, 1), a:a + n, k * 512:(k + 1) * 512].rearrange(
                    "o (t p) n -> p (o t) n", p=P), tiles, 512
            w = w_gate if kind == "gate" else w_up
            return w[bass.ds(e, 1), k * 4 * P:(k + 1) * 4 * P, a:a + n].rearrange(
                "o (t p) n -> p (o t) n", p=P), 4, n

        def place_of(kind, c, k):
            a, n = FC[c]
            return (n // P, 512) if kind == "down" else (4, n)

        FIRST = [n for n in range(NB) if not LEAD <= n < LEAD + SKIPPED]
        assert NB % RAWS == 0 and NB % SPLITS == 0

        def pos(n, e):
            return FIRST.index(n) if isinstance(e, int) and e == 0 else n

        def pos_mod(n, e, m):
            return (FIRST.index(n) if isinstance(e, int) and e == 0 else n - SKIPPED) % m

        def slot_of(n, e):
            return pos_mod(n, e, RAWS)

        def landed_of(n, e):
            if isinstance(e, int) and e == 0:
                return 16 * (FIRST.index(n) // RAWS + 1)
            return e * (16 * (NB // RAWS)) + 16 * ((n - SKIPPED) // RAWS + 1)

        def wo_slot(n):
            return n % 4 + (4 if KD <= n < KD + 4 else 0)

        X2T_ORDER = [(h, t - h) for t in range(TT + 1) for h in range(2) if 0 <= t - h < TT]

        def x2T_count(h, t):
            return X2T_ORDER.index((h, t)) + 1

        def load_expert(sp, n, e, count):
            kind, c, k = BODY[n]
            owner = e - 1 if (kind, c) == ("down", 2) else e
            tiles, width = place_of(kind, c, k)
            src, _, _ = src_of(kind, c, k, owner)
            sp.dma_start(EW[count % RAWS][:, 0:tiles, 0:width], src).then_inc(e_landed[count % RAWS], 16)

        @block.sync
        def _(sp):
            sp.dma_start(SM[:], small).then_inc(small_in, 16)
            for t in range(TT):
                sp.dma_start(X[:, t, :], seq_rows(t)).then_inc(x_in[t], 16)

            def load_w(s, i, j):
                c = SECTIONS[s][2](i, j)
                sp.dma_start(RAW[j][:], w_in[:, c * P:(c + 1) * P].rearrange("(k p) n -> p k n", p=P)).then_inc(w_landed[j], 16)

            for j in range(4):
                load_w(0, 0, j)
                if j == 0:
                    sp.dma_start(FF[:], ffn).then_inc(ffn_in, 16)
                    sp.dma_start(ZP[:], zpos).then_inc(zpos_in, 16)
            for s, i, j in UNITS:
                if (s, i, j) == (2, 0, 0):
                    sp.wait_ge(short_done, 3 * KC)
                    sp.wait_ge(vT_mm, 2 * KC)
                    sp.wait_ge(x0_stored, 16 * KC)
                    sp.dma_start(W4[:], ffn_w4).then_inc(w4_in, 16)
                    sp.dma_start(DECAY[:], decay.rearrange("(t p) n -> p t n", p=P)).then_inc(decay_in, 16)
                after = unit_after(s, i, j)
                if after:
                    sp.wait_ge(w_lo, split_count((s, i, j)))
                    load_w(*after)
                if s == 1 and j == 2:
                    sp.wait_ge(short_done, 3 * i + 3)
                    sp.dma_start(x0_dram[i, :, :], SHORTS[0][:].rearrange("p s n -> p (s n)")).then_inc(x0_stored, 16)
                if s == 2 and i == SECTIONS[2][0] - 1 and j % 2:
                    sp.wait_ge(w_lo, len(UNITS) - 3 + j)
                    table = (cosine, sine)[j // 2]
                    sp.dma_start(TABLE_RAW[j // 2][:], table.rearrange("(t p) n -> p t n", p=P)).then_inc(table_in, 16)
                if s == 2:
                    q = 4 * i + j
                    sp.wait_ge(g_ready, q + 1)
                    sp.dma_start(gate_dram[q, :, :], GSTAGE[q % 2][:].rearrange("p s n -> p (s n)")).then_inc(g_stored[q % 2], 16)

            sp.wait_ge(cos_lo, 1)
            sp.dma_start(SKIP[:], hy_skip.to_broadcast([P, DC])).then_inc(skip_in, 16)
            for s in range(2):
                if s == 0:
                    sp.wait_ge(taps_ready, LT)
                else:
                    sp.wait_ge(ub_lo, KC)
                sp.dma_start(X0[:], x0_dram[:, :, s * L:(s + 1) * L].rearrange("k p n -> p k n")).then_inc(x0_in, 16)

            sp.wait_ge(k_ready, LT)
            sp.wait_ge(u_mm, 2 * LT)
            for dt in range(KD):
                for n in ((0, 1, 2, 3) if dt == 0 else () if dt == 1 else (2 * dt, 2 * dt + 1)):
                    if n >= 4:
                        sp.wait_ge(o_lo, n - 3)
                    src = (conv_w_out, hy_w_out)[n % 2][:, n // 2 * P:(n // 2 + 1) * P]
                    sp.dma_start(OUT_RAW[n % 4][:], src.rearrange("(k p) n -> p k n", p=P)).then_inc(o_landed[n % 4], 16)
                if dt == 0:
                    sp.wait_ge(ub_lo, 2 * KC)
                    sp.wait_ge(y_lo, 4 * LT)
                    for q in range(2):
                        sp.wait_ge(g_stored[q], 16 * KD)
                if dt >= 2:
                    sp.wait_ge(m_lo, dt - 1)
                for n in (2 * dt, 2 * dt + 1):
                    sp.dma_start(GIN[n % 4][:].rearrange("p s n -> p (s n)"),
                                 gate_dram[(n % 2) * KD + dt, :, :]).then_inc(gin_in[n % 4], 16)

            def load_residual(n):
                h, t = n // TT, n % TT
                ge(sp, x2_ready, n - 3)
                sp.dma_start(XRES[n % 4][:], seq_rows(t)[:, h * 512:(h + 1) * 512]).then_inc(gin_in[n % 4], 16)

            for n in range(2 * KD):
                h, k = n // KD, n % KD
                sp.wait_ge(o_lo, 2 * KD + n - 3)
                sp.dma_start(WO_RAW[n % 4][:], w_o[k * P:(k + 1) * P, h * 512:(h + 1) * 512]).then_inc(o_landed[n % 4], 16)
                if n == 3:
                    sp.wait_ge(o_used, 2 * KD)
                    sp.wait_ge(m_lo, KD)
                    sp.dma_start(NG2[:], norm2_g.to_broadcast([P, D])).then_inc(ng2_in, 16)
                    for r in range(4):
                        load_residual(r)
            for count in range(EARLY):
                load_expert(sp, FIRST[count], 0, count)
            for n in range(4, 2 * TT):
                load_residual(n)

            def few_on_the_way(count):
                if count >= FLYING:
                    sp.wait_ge(e_landed[(count - FLYING) % RAWS], 16 * ((count - FLYING) // RAWS + 1))

            for count, n in enumerate(FIRST):
                if count < EARLY:
                    continue
                if count == EARLY:
                    sp.wait_ge(x2_mm, 2 * TT)
                elif count == BEFORE_ROUTER:
                    sp.wait_ge(logits_mm, TT)
                    sp.wait_ge(tok_ready, TT)
                    sp.wait_ge(acc_stored, 16 * TT)
                    sp.wait_ge(xs_in, 16)
                    sp.dma_start(NGF[:], norm_f_g.to_broadcast([P, D])).then_inc(ngf_in, 16)
                few_on_the_way(count)
                load_expert(sp, n, 0, count)
            with sp.Fori(1, E) as e:
                for n in range(NB):
                    if n % 3 == 0:
                        sp.wait_ge(e_used, e * NB + max(n + 2 - SKIPPED - RAWS + 1, 1 - NB))
                    else:
                        before = n - SKIPPED - FLYING
                        sp.wait_ge(e_landed[before % RAWS], e * 16 + 16 * (before // RAWS + 1))
                    load_expert(sp, n, e, n - SKIPPED + NB)
            for n in range(LEAD, LEAD + SKIPPED):
                count = NB * E - SKIPPED + n - LEAD
                sp.wait_ge(e_used, count - RAWS + 1)
                few_on_the_way(count)
                load_expert(sp, n, E, count)

            sp.wait_ge(added, 16 * E)
            for t in range(TT):
                sp.dma_start(XF[t][:], acc_dram[t * P:(t + 1) * P, :]).then_inc(x_in[t], 16)
            for t in range(TT):
                sp.wait_ge(fin_out, t + 1)
                dst = (y_prompt if t < LT else y_sample)[(t % LT) * P:(t % LT + 1) * P, :]
                sp.dma_start(dst, XF[t][:]).then_inc(fin_stored, 16)
            sp.wait_ge(fin_stored, 16 * TT)

        @block.gpsimd
        def _(pool):
            nc.gpsimd.memset(ONES[:], 1.0 / DC).then_inc(ones_set, 1)
            nc.gpsimd.memset(EPS[:, 0:1], 1e-6).then_inc(ones_set, 1)
            nc.gpsimd.memset(EPS[:, 1:2], 1e-5).then_inc(ones_set, 1)
            nc.gpsimd.memset(AFFW[:], 0.0).then_inc(ones_set, 1)
            nc.gpsimd.memset(APAD[:], 0.0).then_inc(pads_set, 1)
            pool.wait_ge(mlp_sin, 3)
            for j in range(3):
                nc.gpsimd.memset(ZPAD[j][:], 0.0).then_inc(pads_set, 1)

            pool.wait_ge(table_hi, 2)
            nc.gpsimd.tensor_tensor(SIN[1][:], TABLE_RAW[1][:], SIN[0][:].bitcast(F32), ALU.subtract).then_inc(sin_lo, 1)

            for s in range(2):
                for f in range(LT):
                    for part, y in enumerate((YRE, YIM)):
                        pool.wait_ge(y_hi, 2 * (s * LT + f) + part + 1)
                        nc.gpsimd.tensor_tensor(y[1][:, f, :], YV[part][:], y[0][:, f, :].bitcast(F32),
                                                ALU.subtract).then_inc(y_lo, 1)
                    if s == 0:
                        pool.wait_ge(ln_root, 2)
                        pool.wait_ge(ln_sq, f + 1)
                        nc.gpsimd.tensor_tensor(CONV[:, f, :, :], CONV[:, f, :, :], LNRS[:], ALU.mult).then_inc(ln_x, 1)
                    else:
                        pool.wait_ge(at_hi, f + 1)
                        nc.gpsimd.tensor_tensor(AT[1][:, f, :, :], CONV[:, f, :, :], AT[0][:, f, :, :].bitcast(F32),
                                                ALU.subtract).then_inc(at_lo, 1)

            for t in range(TT):
                pool.wait_ge(x2_ready, TT + t + 1)
                pool.dma_start(acc_dram[t * P:(t + 1) * P, :], X2[:, t, :]).then_inc(acc_stored, 16)
                pool.wait_ge(tok_ready, t + 1)
                pool.dma_start(tok_dram[t * P:(t + 1) * P, :], TOK[t % 2][:]).then_inc(tok_stored[t % 2], 16)

            def gather(e):
                if not isinstance(e, int):
                    pool.wait_ge(xs_in, e * 16)
                    pool.wait_ge(xsT_mm, e)
                pool.wait_ge(slots_ready, 2)
                nc.gpsimd.tensor_copy(NEXT_ROWS[:], SLOTS[:, bass.ds(e, 1)]).then_inc(rows_next, 1)
                pool.wait_ge(x2_mm, 2 * TT)
                pool.wait_ge(rows_next, e)
                pool.indirect_dma_start(XS[:], None, tok_dram,
                                        bass.IndirectOffsetOnAxis(ap=NEXT_ROWS[:], axis=0)).then_inc(xs_in, 16)

            def scatter(e):
                if not isinstance(e, int):
                    pool.wait_ge(added, e * 16)
                pool.wait_ge(slots_ready, 2)
                nc.gpsimd.tensor_copy(DONE_ROWS[:], SLOTS[:, bass.ds(e, 1)]).then_inc(rows_done, 1)
                pool.wait_ge(slots_ready, 2)
                pool.wait_ge(rows_done, e + 1)
                pool.wait_ge(ye_ready, e + 1)
                pool.indirect_dma_start(acc_dram, bass.IndirectOffsetOnAxis(ap=DONE_ROWS[:], axis=0), YE[:], None,
                                        compute_op=ALU.add).then_inc(added, 16)

            for i in range(2):
                pool.wait_ge(tok_stored[i], 16 * TT // 2)
            pool.wait_ge(acc_stored, 16 * TT)
            pool.wait_ge(slots_ready, 2)
            nc.gpsimd.tensor_copy(NEXT_ROWS[:], SLOTS[:, 0:1]).then_inc(pads_set, 1)
            pool.wait_ge(pads_set, 5)
            pool.wait_ge(x2_mm, 2 * TT)
            pool.indirect_dma_start(XS[:], None, tok_dram,
                                    bass.IndirectOffsetOnAxis(ap=NEXT_ROWS[:], axis=0)).then_inc(xs_in, 16)
            pool.wait_ge(xs_in, 16)
            pool.wait_ge(xsT_mm, 1)
            gather(1)
            scatter(0)
            with pool.Fori(1, E - 1) as e:
                gather(e + 1)
                scatter(e)
            pool.wait_ge(added, 16 * (E - 1))
            scatter(E - 1)

        @block.scalar
        def _(act):
            steps = Steps(act, a_step)

            def high(out, src, s, **scale):
                nc.scalar.activation(out, src, ACT.Copy, **scale).then_inc(s, 1)

            act.wait_ge(ones_set, 3)
            nc.scalar.activation(EPS[:, 2:3], EPS[:, 0:1], ACT.Sqrt).then_inc(root_table, 1)

            def root(t):
                act.wait_ge(var_ready, t + 1)
                nc.scalar.activation(RSTD[:, t:t + 1], RSTD[:, t:t + 1], ACT.Sqrt).then_inc(roots, 1)

            def hT_high(g):
                s, k = g // KD, g % KD
                act.wait_ge(xT_ready, g + 1)
                high(HT[0][:, k, s * L:(s + 1) * L], PS[:, g % 4, :], hT_hi, scale=col("norm1", k))

            act.wait_ge(small_in, 16)
            for t in range(TT):
                act.wait_ge(x_in[t], 16)
                if t >= 2:
                    act.wait_ge(squares, t - 1)
                nc.scalar.activation(SQOUT[t % 2][:], X[:, t, :], ACT.Square, accum_out=SUMSQ[:, t:t + 1]).then_inc(squares, 1)
                if t:
                    root(t - 1)
                if t > LT:
                    hT_high(2 * (t - LT - 1))
                    hT_high(2 * (t - LT - 1) + 1)
            root(TT - 1)

            def split_w(s, i, j):
                use = use_of(s, i, j)
                act.wait_ge(w_landed[j], 16 * (use + 1))
                if unit_before((s, i, j)):
                    act.wait_ge(w_used, used_count(unit_before((s, i, j))))
                high(SPLIT[j][0][:], RAW[j][:], w_hi)

            for g in range(2 * (LT - 1), 2 * KD):
                hT_high(g)
                if g == 2 * KD - 5:
                    split_w(0, 0, 0)
            for j in range(1, 4):
                split_w(0, 0, j)

            def mlp_sine(layer):
                act.wait_ge(mlp_arg, layer + 1)
                nc.scalar.activation(FH[layer][:], FARG[:], ACT.Sin).then_inc(mlp_sin, 1)

            mlp_sine(0)
            for s, i, j in UNITS:
                c = SECTIONS[s][2](i, j)
                z = PS[:, 2 * j:2 * j + 2, :]
                if s == 0 and j % 2 == 0:
                    ct = 2 * i + j // 2
                    act.wait_ge(w_used, used_count((s, i, j)))
                    ge(act, a_ready, ct - 1)
                    nc.scalar.activation(SIG[ct % 2][:], z, ACT.Sigmoid, bias=col("b_in", c)).then_inc(z_free, 1)
                if s == 1:
                    act.wait_ge(w_used, used_count((s, i, j)))
                    act.wait_ge(pads_set, 4)
                    ge(act, short_done, 3 * (i - 1) + j + 1)
                    nc.scalar.activation(ZPAD[j][:, :, 1:L + 1], z, ACT.Identity, bias=col("b_in", c)).then_inc(z_free, 1)
                    act.wait_ge(z_free, KC + 3 * i + j + 1)
                    if j == 0:
                        ge(act, x0_stored, 16 * i)
                        act.wait_ge(a_ready, KC)
                    if j == 1:
                        ge(act, vT_mm, 2 * i)
                    if j == 2:
                        act.wait_ge(v_ready, i + 1)
                    cc = c - 2 * KC
                    nc.scalar.activation(SHORTS[j % 2][:], ZPAD[j][:, :, 1:L + 1], ACT.Identity, bias=col("short_b", cc),
                                         scale=col("short_w", cc * SHORT + 1)).then_inc(short_mid, 1)
                if s == 2:
                    q = 4 * i + j
                    act.wait_ge(w_used, used_count((s, i, j)))
                    ge(act, g_stored[q % 2], 16 * (q // 2))
                    if q == 0:
                        act.wait_ge(short_done, 3 * KC)
                    nc.scalar.activation(GSTAGE[q % 2][:], z, ACT.Sigmoid, bias=col("b_in", c)).then_inc(g_ready, 1)
                after = unit_after(s, i, j)
                if after:
                    split_w(*after)
                if s == 0 and i == 0 and j < 2:
                    mlp_sine(j + 1)
                if s == 1 and j == 2:
                    for q in range(2):
                        act.wait_ge(vT_mm, 2 * i + q + 1)
                        high(VT[0][:, q * LT:(q + 1) * LT, i * P:(i + 1) * P],
                             PS[:, 6 + q, :].rearrange("p (t n) -> p t n", n=P), vT_hi)

            act.wait_ge(w_used, len(UNITS))
            for n, table in enumerate((COS, SIN)):
                act.wait_ge(table_in, 32)
                high(table[0][:], TABLE_RAW[n][:], table_hi)
            for lt in range(LT):
                act.wait_ge(taps_ready, lt + 1)
                ge(act, norm_mm, lt)
                nc.scalar.activation(HABS[:], HF[lt % 2][:], ACT.Abs).then_inc(abs_ready, 1)
                act.wait_ge(eo_sum, 2 * lt + 2)
                high(EO[0][:, lt, :, :], HSUM[:].rearrange("p (s n) -> p s n", s=2), eo_hi)
            act.wait_ge(norm_mm, LT)
            act.wait_ge(cos_lo, 1)
            nc.scalar.activation(NROW[:], PS[0:1, 6, :], ACT.Copy).then_inc(norm_row, 1)

            act.wait_ge(g_stored[0], 16 * KD)
            act.wait_ge(g_stored[1], 16 * KD)
            for ct in range(KC):
                act.wait_ge(ln_x, ct + 1)
                ge(act, ln_used, ct - 1)
                nc.scalar.activation(LNSQ[ct % 2][:], CONV[:, ct, :, :], ACT.Square).then_inc(ln_sq, 1)
            act.wait_ge(ln_mm, 2)
            act.wait_ge(ones_set, 4)
            nc.scalar.activation(LNRS[:], PS[:, 2:4, :], ACT.Sqrt, bias=EPS[:, 1:2]).then_inc(ln_root, 1)

            def spectrum_high(s, f):
                for part, y in enumerate((YRE, YIM)):
                    act.wait_ge(y_val, 2 * (s * LT + f) + part + 1)
                    if s:
                        act.wait_ge(y_mm, f + 1)
                    high(y[0][:, f, :], YV[part][:], y_hi)

            def hyena_high(s):
                for ct in range(KC):
                    act.wait_ge(uy_ready, s * KC + ct + 1)
                    high(UB[0][:, ct, s, :], X0[:, ct, :], ub_hi)

            def split_out(n):
                j = n % 4
                act.wait_ge(o_landed[j], 16 * (n // 4 + 1))
                ge(act, o_used, n - 3)
                high(OUT_SPLIT[j][0][:], OUT_RAW[j][:], o_hi)

            for s in range(2):
                for f in range(LT):
                    spectrum_high(s, f)
                    if s == 0:
                        act.wait_ge(ln_x, KC + f + 1)
                        steps.then(nc.scalar.activation(CONV[:, f, :, :], CONV[:, f, :, :], ACT.Silu,
                                                        bias=col("ln_b", f), scale=col("ln_g", f)))
                        high(AT[0][:, f, :, :], CONV[:, f, :, :], at_hi)
                    if (s, f) == (1, 1):
                        hyena_high(0)
            for n in range(4):
                split_out(n)
            hyena_high(1)

            def split_wo(n):
                act.wait_ge(o_landed[n % 4], 16 * (KD // 2 + n // 4 + 1))
                if n < KD:
                    act.wait_ge(o_used, 2 * KD + n - 3)
                elif n == 2 * KD - 1:
                    act.wait_ge(x2_mm, TT)
                else:
                    act.wait_ge(o_used, 2 * KD + max(n - KD + 1, 0) if n >= KD + 4 else 2 * KD)
                high(WO_SPLIT[wo_slot(n)][0][:], WO_RAW[n % 4][:], o_hi)

            for dt in range(KD):
                act.wait_ge(m_val, dt + 1)
                high(MT[0][:, dt, :, :], GIN[2 * dt % 4][:], m_hi)
                for n in (2 * dt + 4, 2 * dt + 5):
                    if n < 2 * KD:
                        split_out(n)
                    else:
                        split_wo(n - 2 * KD)

            def square_rows(h, t):
                n = h * TT + t
                act.wait_ge(x2_ready, n + 1)
                ge(act, x2_sq, n)
                nc.scalar.activation(SQOUT2[:], X2[:, t, h * 512:(h + 1) * 512], ACT.Square,
                                     accum_out=SUMSQ2[:, t, h:h + 1]).then_inc(x2_sq, 1)

            def x2T_copy(h, t):
                act.wait_ge(x2T_mm, x2T_count(h, t))
                ge(act, logits_mm, t - 1)
                nc.scalar.activation(X2T[t % 2][:, 4 * h:4 * h + 4, :].rearrange("p k n -> p (k n)"),
                                     PS[:, 4 + 2 * (t % 2) + h, :], ACT.Copy).then_inc(x2T_ready, 1)

            for n in range(4, 2 * KD):
                split_wo(n)
            for t in range(TT):
                square_rows(0, t)
            for t in range(TT + 1):
                if t < TT:
                    x2T_copy(0, t)
                if t:
                    x2T_copy(1, t - 1)
                    square_rows(1, t - 1)
                    act.wait_ge(var_ready, TT + t)
                    nc.scalar.activation(RSTD2[:, t - 1:t], RSTD2[:, t - 1:t], ACT.Sqrt, bias=EPS[:, 0:1]).then_inc(roots, 1)
            act.wait_ge(exp_in, 1)
            nc.scalar.activation(AFF[:], AFF[:], ACT.Exp).then_inc(exp_out, 1)
            act.wait_ge(affT_mm, 1)
            nc.scalar.activation(ROWS[0][:], PS[0:48, 3, :], ACT.Copy).then_inc(rows_ready, 1)

            def split_e(n, e, base):
                r, (tiles, width) = slot_of(n, e), place_of(*BODY[n][:2], 0)
                act.wait_ge(e_landed[r], landed_of(n, e))
                ge(act, e_used, base + pos(n, e) - SPLITS + 1)
                q = pos_mod(n, e, SPLITS)
                high(ES[q][:, 0:tiles, 0:width], EW[r][:, 0:tiles, 0:width], e_hi)

            def silu(c, e, base):
                last_gate = pos(BODY.index(("gate", c, 1)), e)
                act.wait_ge(e_used, base + last_gate + 1)
                ge(act, hid_ready, NF * e + c)
                w = FC[c][1]
                nc.scalar.activation(SG[:, 0:w], PS[:, 0, 0:w], ACT.Silu).then_inc(silu_ready, 1)

            def hidT_high(c, e, base):
                act.wait_ge(hidT_mm, NF * e + c + 1)
                tiles = FC[c][1] // P
                high(HIDT[0][:, 0:tiles, :].rearrange("p t n -> p (t n)"), PS[:, 6, 0:tiles * P], hidT_hi)

            def xsT_high(e):
                act.wait_ge(xsT_mm, e + 1)
                high(XST[0][:].rearrange("p k n -> p (k n)"), PS[:, 6:8, :].rearrange("p a n -> p (a n)"), xsT_hi)

            def gate_out(e, used):
                for dh in range(2):
                    act.wait_ge(slots_ready, 2)
                    act.wait_ge(e_used, used + dh)
                    ge(act, added, e * 16)
                    out = nc.scalar.activation(YE[:, dh * 512:(dh + 1) * 512], PS[:, 4 + dh, :], ACT.Copy,
                                               scale=GATES[:, bass.ds(e, 1)])
                out.then_inc(ye_ready, 1)

            def act_body(e, base, first):
                for n in range(NB):
                    if not (first and LEAD <= n < LEAD + SKIPPED):
                        split_e(n, e, base)
                    if n == (2 if first else 0):
                        xsT_high(e)
                    if n == 2 and not first:
                        hidT_high(2, e - 1, base)
                    if n == 5:
                        silu(0, e, base)
                    if n == 8:
                        if not first:
                            gate_out(e - 1, base + LEAD + 1)
                        hidT_high(0, e, base)
                    if n == 11:
                        silu(1, e, base)
                    if n == 14:
                        hidT_high(1, e, base)
                    if n == 17:
                        silu(2, e, base)

            act.wait_ge(x2_mm, 2 * TT)
            act_body(0, 0, True)
            with act.Fori(1, E) as e:
                act_body(e, e * NB - SKIPPED, False)
            base = E * NB - SKIPPED
            for q in range(SKIPPED):
                count = base + q
                act.wait_ge(e_landed[count % RAWS], 16 * (count // RAWS + 1))
                act.wait_ge(e_used, count - SPLITS + 1)
                tiles = FC[2][1] // P
                high(ES[count % SPLITS][:, 0:tiles, :], EW[count % RAWS][:, 0:tiles, :], e_hi)
            hidT_high(2, E - 1, base)
            gate_out(E - 1, base + 1)

            act.wait_ge(root_table, 1)
            nc.scalar.activation(EPS[:, 2:3], EPS[:, 0:1], ACT.Sqrt).then_inc(root_table, 1)

            def final_root(t):
                act.wait_ge(var_ready, 2 * TT + t + 1)
                nc.scalar.activation(RSTDF[:, t:t + 1], RSTDF[:, t:t + 1], ACT.Sqrt).then_inc(roots, 1)

            for t in range(TT):
                act.wait_ge(x_in[t], 32)
                act.wait_ge(squares, TT + t)
                nc.scalar.activation(YE[:], XF[t][:], ACT.Square, accum_out=SUMSQF[:, t:t + 1]).then_inc(squares, 1)
                if t:
                    final_root(t - 1)
            final_root(TT - 1)

        @block.vector
        def _(dve):
            steps = Steps(dve, v_step)
            V = nc.vector

            def low(out, src, high_part, s):
                V.tensor_tensor(out, src, high_part.bitcast(F32), ALU.subtract).then_inc(s, 1)

            def scale_rows(t):
                dve.wait_ge(roots, t + 1)
                steps.then(V.reciprocal(RSTD[:, t:t + 1], RSTD[:, t:t + 1]))
                V.tensor_scalar(X[:, t, :], X[:, t, :], RSTD[:, t:t + 1], None, ALU.mult).then_inc(scaled, 1)

            def hT_low(g):
                s, k = g // KD, g % KD
                part = slice(s * L, (s + 1) * L)
                dve.wait_ge(hT_hi, g + 1)
                V.scalar_tensor_tensor(HT[1][:, k, part], PS[:, g % 4, :], col("norm1", k), HT[0][:, k, part].bitcast(F32),
                                       ALU.mult, ALU.subtract).then_inc(hT_lo, 1)

            dve.wait_ge(small_in, 16)
            for t in range(TT):
                dve.wait_ge(squares, t + 1)
                V.tensor_scalar(RSTD[:, t:t + 1], SUMSQ[:, t:t + 1], 1.0 / D, 1e-6, ALU.mult, ALU.add).then_inc(var_ready, 1)
                if t:
                    scale_rows(t - 1)
                if t > LT:
                    hT_low(2 * (t - LT - 1))
                    hT_low(2 * (t - LT - 1) + 1)
            scale_rows(TT - 1)

            def split_w(s, i, j):
                dve.wait_ge(w_hi, split_count((s, i, j)))
                low(SPLIT[j][1][:], RAW[j][:], SPLIT[j][0][:], w_lo)

            def conv_taps(ct, taps):
                for tap in taps:
                    src = APAD[:, ct, :, tap:tap + L]
                    w = col("dw_w", ct * TAPS + tap)
                    if tap == 0:
                        ins = V.tensor_scalar(CONV[:, ct, :, :], src, w, col("dw_b", ct), ALU.mult, ALU.add)
                    else:
                        ins = V.scalar_tensor_tensor(CONV[:, ct, :, :], src, w, CONV[:, ct, :, :], ALU.mult, ALU.add)
                    if tap == TAPS - 1:
                        ins.then_inc(conv_done, 1)
                    else:
                        steps.then(ins)

            for g in range(2 * (LT - 1), 2 * KD):
                hT_low(g)
                if g == 2 * KD - 5:
                    split_w(0, 0, 0)
            for j in range(1, 4):
                split_w(0, 0, j)

            def mlp_argument(layer):
                dve.wait_ge(ffn_in, 16)
                dve.wait_ge(mlp_mm, layer + 1)
                steps.then(V.tensor_scalar(FARG[:], PS[0:FFN, 6, :], FF[:, 3 * FFN + layer:3 * FFN + layer + 1],
                                           FF[:, 3 * FFN + 3:3 * FFN + 4], ALU.add, ALU.mult))
                steps.then(V.tensor_scalar(FK[:], FARG[:], 1.0 / (2.0 * math.pi), ROUNDER, ALU.mult, ALU.add))
                steps.then(V.tensor_scalar(FK[:], FK[:], ROUNDER, None, ALU.subtract))
                steps.then(V.scalar_tensor_tensor(FARG[:], FK[:], -TWO_PI_HEAD, FARG[:], ALU.mult, ALU.add))
                steps.then(V.scalar_tensor_tensor(FARG[:], FK[:], -TWO_PI_TAIL, FARG[:], ALU.mult, ALU.add))
                V.tensor_scalar(FARG[:], FARG[:], 3.1415925, -3.1415925, ALU.min, ALU.max).then_inc(mlp_arg, 1)

            mlp_argument(0)
            for s, i, j in UNITS:
                c = SECTIONS[s][2](i, j)
                if s == 0 and j % 2 == 1:
                    ct = 2 * i + j // 2
                    dve.wait_ge(w_used, used_count((s, i, j)))
                    dve.wait_ge(z_free, ct + 1)
                    dve.wait_ge(pads_set, 1)
                    V.scalar_tensor_tensor(APAD[:, ct, :, PAD:PAD + L], PS[:, 2 * j:2 * j + 2, :], col("b_in", c),
                                           SIG[ct % 2][:], ALU.add, ALU.mult).then_inc(a_ready, 1)
                if s == 1:
                    cc = c - 2 * KC
                    r = SHORTS[j % 2]
                    dve.wait_ge(short_mid, 3 * i + j + 1)
                    steps.then(V.scalar_tensor_tensor(r[:], ZPAD[j][:, :, 0:L], col("short_w", cc * SHORT), r[:],
                                                      ALU.mult, ALU.add))
                    V.scalar_tensor_tensor(r[:], ZPAD[j][:, :, 2:L + 2], col("short_w", cc * SHORT + 2), r[:],
                                           ALU.mult, ALU.add).then_inc(short_done, 1)
                    dve.wait_ge(short_done, 3 * i + j + 1)
                    if j == 1:
                        V.tensor_tensor(r[:], r[:], SHORTS[0][:], ALU.mult).then_inc(v_ready, 1)
                after = unit_after(s, i, j)
                if after:
                    split_w(*after)
                if s == 0 and i == 0 and j < 2:
                    mlp_argument(j + 1)
                if s == 1 and j == 2:
                    for q in range(2):
                        dve.wait_ge(vT_hi, 2 * i + q + 1)
                        low(VT[1][:, q * LT:(q + 1) * LT, i * P:(i + 1) * P],
                            PS[:, 6 + q, :].rearrange("p (t n) -> p t n", n=P),
                            VT[0][:, q * LT:(q + 1) * LT, i * P:(i + 1) * P], vT_lo)
                if s == 1:
                    dve.wait_ge(a_ready, KC)
                    conv_taps(i, range(4 * j, 4 * j + 4))
                if s == 2:
                    conv_taps(i, range(12 + 5 * j, min(12 + 5 * j + 5, TAPS)))

            dve.wait_ge(table_hi, 1)
            low(COS[1][:], TABLE_RAW[0][:], COS[0][:], cos_lo)
            dve.wait_ge(decay_in, 16)

            def eo_low(lt):
                dve.wait_ge(eo_hi, lt + 1)
                low(EO[1][:, lt, :, :], HSUM[:].rearrange("p (s n) -> p s n", s=2), EO[0][:, lt, :, :], eo_lo)

            for lt in range(LT):
                dve.wait_ge(taps_mm, lt + 1)
                ge(dve, abs_ready, lt - 1)
                for q in range(2):
                    out = V.tensor_tensor(HF[lt % 2][:, q * DC:(q + 1) * DC], PS[:, 4 + q, :], DECAY[:, lt, :], ALU.mult)
                out.then_inc(taps_ready, 1)
                if lt:
                    eo_low(lt - 1)
                    dve.wait_ge(eo_lo, lt)
                dve.wait_ge(taps_ready, lt + 1)
                h = HF[lt % 2]
                V.tensor_tensor(HSUM[:, 0:DC], h[:, 0:DC], h[:, DC:2 * DC], ALU.add).then_inc(eo_sum, 1)
                V.tensor_tensor(HSUM[:, DC:2 * DC], h[:, DC:2 * DC], h[:, 0:DC], ALU.subtract).then_inc(eo_sum, 1)
            eo_low(LT - 1)
            dve.wait_ge(norm_mm, LT)
            dve.wait_ge(norm_row, 1)
            dve.wait_ge(skip_in, 16)
            V.scalar_tensor_tensor(SKIPN[:], PS[:, 6, :], float(DC), SKIP[:], ALU.mult, ALU.mult).then_inc(skip_norm, 1)

            dve.wait_ge(ln_mm, 1)
            for ct in range(KC):
                V.tensor_tensor(CONV[:, ct, :, :], CONV[:, ct, :, :], PS[:, 0:2, :], ALU.subtract).then_inc(ln_x, 1)
            dve.wait_ge(norm_col, 1)
            steps.then(V.reciprocal(NORMC[:], PS[:, 7, 0:KC]))
            V.tensor_scalar(NORMC[:], NORMC[:], 1.0 / DC / DC, None, ALU.mult).then_inc(norm_col, 1)
            dve.wait_ge(norm_col, 2)

            def spectrum(f):
                re, im = (PS[:, 4, :], PS[:, 5, :]) if f % 2 == 0 else (PS[:, 6, :], PS[:, 7, :])
                cos_h, sin_h = col("cos_half", f), col("sin_half", f)
                dve.wait_ge(k_mm, f + 1)
                dve.wait_ge(skip_norm, 1)
                steps.did(V.scalar_tensor_tensor(KTMP[0][:], im, sin_h, SKIPN[:], ALU.mult, ALU.subtract))
                steps.then(V.tensor_scalar(KTMP[1][:], re, sin_h, None, ALU.mult))
                V.scalar_tensor_tensor(KR[:, f, :], re, cos_h, KTMP[0][:], ALU.mult, ALU.subtract).then_inc(k_ready, 1)
                V.scalar_tensor_tensor(KI[:, f, :], im, cos_h, KTMP[1][:], ALU.mult, ALU.add).then_inc(k_ready, 1)
                dve.wait_ge(k_ready, 2 * f + 2)

            spectrum(0)
            spectrum(1)
            dve.wait_ge(ln_root, 1)
            V.reciprocal(LNRS[:], LNRS[:]).then_inc(ln_root, 1)
            spectrum(2)
            spectrum(3)

            def products(s, f):
                n = s * LT + f
                uc, us = PS[:, 2 * (f % 2), :], PS[:, 2 * (f % 2) + 1, :]
                dve.wait_ge(u_mm, n + 1)
                for tmp, (u, k) in zip(YT, ((uc, KR), (us, KI), (us, KR), (uc, KI))):
                    out = V.tensor_tensor(tmp[:], u, k[:, f, :], ALU.mult)
                out.then_inc(u_used, 1)
                dve.wait_ge(u_used, n + 1)
                for part, op in enumerate((ALU.add, ALU.subtract)):
                    ge(dve, y_lo, 2 * n - 1 + part)
                    V.tensor_tensor(YV[part][:], YT[2 * part][:], YT[2 * part + 1][:], op).then_inc(y_val, 1)
                dve.wait_ge(y_val, 2 * n + 2)

            def hyena_out(s):
                dve.wait_ge(x0_in, 16 * (s + 1))
                dve.wait_ge(y_mm, LT * (s + 1))
                for ct in range(KC):
                    V.scalar_tensor_tensor(X0[:, ct, :], PS[:, 4 + ct, :], NORMC[:, ct:ct + 1], X0[:, ct, :],
                                           ALU.mult, ALU.mult).then_inc(uy_ready, 1)
                for ct in range(KC):
                    dve.wait_ge(ub_hi, s * KC + ct + 1)
                    low(UB[1][:, ct, s, :], X0[:, ct, :], UB[0][:, ct, s, :], ub_lo)

            def split_out(n):
                j = n % 4
                dve.wait_ge(o_hi, n + 1)
                low(OUT_SPLIT[j][1][:], OUT_RAW[j][:], OUT_SPLIT[j][0][:], o_lo)

            dve.wait_ge(ln_mm, 2)
            for f in range(LT):
                products(0, f)
            products(1, 0)
            products(1, 1)
            hyena_out(0)
            products(1, 2)
            products(1, 3)
            for n in range(4):
                split_out(n)
            hyena_out(1)

            def split_wo(n):
                dve.wait_ge(o_hi, 2 * KD + n + 1)
                slot = WO_SPLIT[wo_slot(n)]
                low(slot[1][:], WO_RAW[n % 4][:], slot[0][:], o_lo)

            for dt in range(KD):
                for q in range(2):
                    n = 2 * dt + q
                    j = n % 4
                    dve.wait_ge(o_used, n + 1)
                    dve.wait_ge(gin_in[j], 16 * (n // 4 + 1))
                    V.scalar_tensor_tensor(GIN[j][:], PS[:, 2 * j:2 * j + 2, :], col(("conv_b", "hy_b")[q], dt), GIN[j][:],
                                           ALU.add, ALU.mult).then_inc(m_free, 1)
                j = 2 * dt % 4
                dve.wait_ge(m_free, 2 * dt + 2)
                V.tensor_tensor(GIN[j][:], GIN[j][:], GIN[j + 1][:], ALU.add).then_inc(m_val, 1)
                for n in (2 * dt + 4, 2 * dt + 5):
                    if n < 2 * KD:
                        split_out(n)
                dve.wait_ge(m_hi, dt + 1)
                low(MT[1][:, dt, :, :], GIN[j][:], MT[0][:, dt, :, :], m_lo)
                for n in (2 * dt + 4 - 2 * KD, 2 * dt + 5 - 2 * KD):
                    if n >= 0:
                        split_wo(n)

            def add_residual(h, t):
                n = h * TT + t
                dve.wait_ge(x2_mm, n + 1)
                dve.wait_ge(gin_in[n % 4], 16 * (KD // 2 + n // 4 + 1))
                V.tensor_tensor(X2[:, t, h * 512:(h + 1) * 512], PS[:, t if h == 0 else t % 2, :], XRES[n % 4][:],
                                ALU.add).then_inc(x2_ready, 1)

            V.tensor_tensor(ROUTER, ROUTER, col("norm2", 0, KD)[:, :, None].to_broadcast([P, KD, E]),
                            ALU.mult).then_inc(router_ready, 1)
            for n in range(4, 2 * KD - 1):
                split_wo(n)
            add_residual(0, 0)
            split_wo(2 * KD - 1)
            for t in range(1, TT):
                add_residual(0, t)
            dve.wait_ge(ng2_in, 16)
            def row_scale(t):
                dve.wait_ge(x2_sq, TT + t + 1)
                V.tensor_scalar(RSTD2[:, t:t + 1], SUMSQ2[:, t, 0:1], SUMSQ2[:, t, 1:2], 1.0 / D,
                                ALU.add, ALU.mult).then_inc(var_ready, 1)
                dve.wait_ge(roots, TT + t + 1)
                steps.then(V.reciprocal(RSTD2[:, t:t + 1], RSTD2[:, t:t + 1]))

            def norm_rows(t):
                ge(dve, tok_stored[t % 2], 16 * (t // 2))
                V.scalar_tensor_tensor(TOK[t % 2][:], X2[:, t, :], RSTD2[:, t:t + 1], NG2[:], ALU.mult, ALU.mult).then_inc(tok_ready, 1)

            for t in range(TT + 1):
                if t < TT:
                    add_residual(1, t)
                if t:
                    row_scale(t - 1)
                if 1 <= t < TT:
                    norm_rows(t - 1)

            logits = PS[:, 2, 0:TT * E].rearrange("p (t e) -> p t e", e=E)
            dve.wait_ge(logits_mm, TT)
            steps.then(V.tensor_tensor(AFF[:], logits, RSTD2[:, :, None].to_broadcast([P, TT, E]), ALU.mult))
            steps.then(V.reduce_max(RMAX[:], AFF[:], AX_X))
            V.tensor_tensor(AFF[:], AFF[:], RMAX[:, :, None].to_broadcast([P, TT, E]), ALU.subtract).then_inc(exp_in, 1)
            dve.wait_ge(exp_out, 1)
            steps.then(V.reduce_sum(RSUM[:], AFF[:], AX_X))
            steps.then(V.reciprocal(RSUM[:], RSUM[:]))
            for q in range(2):
                part = slice(q * LT, (q + 1) * LT)
                V.tensor_tensor(AFFW[:, :, 32 * q:32 * q + E], AFF[:, part, :], RSUM[:, part, None].to_broadcast([P, LT, E]),
                                ALU.mult).then_inc(aff_ready, 1)
            norm_rows(TT - 1)

            dve.wait_ge(rows_ready, 1)
            rows = ROWS[0]
            for r in range(CAP // 8):
                part = slice(8 * r, 8 * r + 8)
                steps.then(V.max(TOPV[:, part], rows[:]))
                steps.then(V.max_index(TOPI[:, part], TOPV[:, part], rows[:]))
                left = ROWS[1 + r % 2]
                if r + 1 < CAP // 8:
                    steps.then(V.match_replace(left[:], TOPV[:, part], rows[:], -1.0))
                rows = left
            steps.then(V.tensor_copy(TOPF[:], TOPI[:]))
            for q in range(2):
                rows_of, slots_of = slice(32 * q, 32 * q + E), slice(CAP * q, CAP * (q + 1))
                steps.then(V.tensor_copy(PAIR[:, 0, slots_of], TOPV[rows_of, :]))
                V.tensor_scalar(PAIR[:, 1, slots_of], TOPF[rows_of, :], float(L * q), None, ALU.add).then_inc(pair_ready, 1)
            dve.wait_ge(slots_mm, 2)
            V.tensor_copy(GATES[:], PS[:, 0, 0:E]).then_inc(slots_ready, 1)
            V.tensor_copy(SLOTS[:], PS[:, 1, 0:E]).then_inc(slots_ready, 1)

            def split_e(n, e, base):
                r, (tiles, width) = slot_of(n, e), place_of(*BODY[n][:2], 0)
                dve.wait_ge(e_hi, base + pos(n, e) + 1)
                q = pos_mod(n, e, SPLITS)
                low(EL[r][:, 0:tiles, 0:width], EW[r][:, 0:tiles, 0:width], ES[q][:, 0:tiles, 0:width], e_lo)

            def hidden(c, e, base):
                last_up = pos(BODY.index(("up", c, 1)), e)
                dve.wait_ge(e_used, base + last_up + 1)
                dve.wait_ge(silu_ready, NF * e + c + 1)
                ge(dve, hidT_mm, NF * e + c)
                w = FC[c][1]
                V.tensor_tensor(HID[:, 0:w], SG[:, 0:w], PS[:, 1, 0:w], ALU.mult).then_inc(hid_ready, 1)

            def hidT_low(c, e):
                dve.wait_ge(hidT_hi, NF * e + c + 1)
                tiles = FC[c][1] // P
                low(HIDT[1][:, 0:tiles, :].rearrange("p t n -> p (t n)"), PS[:, 6, 0:tiles * P],
                    HIDT[0][:, 0:tiles, :].rearrange("p t n -> p (t n)"), hidT_lo)

            def xsT_low(e):
                dve.wait_ge(xsT_hi, e + 1)
                low(XST[1][:].rearrange("p k n -> p (k n)"), PS[:, 6:8, :].rearrange("p a n -> p (a n)"),
                    XST[0][:].rearrange("p k n -> p (k n)"), xsT_lo)

            def dve_body(e, base, first):
                for n in range(NB):
                    if not (first and LEAD <= n < LEAD + SKIPPED):
                        split_e(n, e, base)
                    if n == (1 if first else 0):
                        xsT_low(e)
                    if n == 2 and not first:
                        hidT_low(2, e - 1)
                    if n == 5:
                        hidden(0, e, base)
                    if n == 8:
                        hidT_low(0, e)
                    if n == 11:
                        hidden(1, e, base)
                    if n == 14:
                        hidT_low(1, e)
                    if n == 17:
                        hidden(2, e, base)

            dve_body(0, 0, True)
            with dve.Fori(1, E) as e:
                dve_body(e, e * NB - SKIPPED, False)
            base = E * NB - SKIPPED
            for q in range(SKIPPED):
                count = base + q
                tiles = FC[2][1] // P
                dve.wait_ge(e_hi, count + 1)
                low(EL[count % RAWS][:, 0:tiles, :], EW[count % RAWS][:, 0:tiles, :],
                    ES[count % SPLITS][:, 0:tiles, :], e_lo)
            hidT_low(2, E - 1)

            def final_rows(t):
                dve.wait_ge(roots, 2 * TT + t + 1)
                steps.then(V.reciprocal(RSTDF[:, t:t + 1], RSTDF[:, t:t + 1]))
                V.scalar_tensor_tensor(XF[t][:], XF[t][:], RSTDF[:, t:t + 1], NGF[:], ALU.mult, ALU.mult).then_inc(fin_out, 1)

            dve.wait_ge(ngf_in, 16)
            for t in range(TT):
                dve.wait_ge(squares, TT + t + 1)
                V.tensor_scalar(RSTDF[:, t:t + 1], SUMSQF[:, t:t + 1], 1.0 / D, 1e-6, ALU.mult, ALU.add).then_inc(var_ready, 1)
                if t:
                    final_rows(t - 1)
            final_rows(TT - 1)

        @block.tensor
        def _(pe):
            def product(out, a, b, first, last):
                nc.tensor.matmul(out, a[0], b[0], start=first, stop=False)
                nc.tensor.matmul(out, a[0], b[1], start=False, stop=False)
                return nc.tensor.matmul(out, a[1], b[0], start=False, stop=last)

            pe.wait_ge(small_in, 16)
            for g in range(2 * KD):
                s, k = g // KD, g % KD
                pe.wait_ge(scaled, (s + 1) * LT)
                ge(pe, hT_lo, g - 3)
                for t in range(LT):
                    mm = nc.tensor.transpose(PS[:, g % 4, t * P:(t + 1) * P], X[:, s * LT + t, k * P:(k + 1) * P], IDENT)
                mm.then_inc(xT_ready, 1)

            def filter_layer(layer):
                pe.wait_ge(ffn_in, 16)
                pe.wait_ge(zpos_in, 16)
                ge(pe, mlp_sin, layer)
                rows = zpos.shape[0] if layer == 0 else FFN
                src = ZP[:] if layer == 0 else FH[layer - 1][:]
                nc.tensor.matmul(PS[0:FFN, 6, :], FF[0:rows, layer * FFN:(layer + 1) * FFN], src,
                                 start=True, stop=True).then_inc(mlp_mm, 1)

            filter_layer(0)
            for s, i, j in UNITS:
                pe.wait_ge(w_lo, split_count((s, i, j)))
                before = unit_before((s, i, j))
                if before:
                    bs, bi, bj = before
                    if bs == 0 and bj % 2 == 0:
                        pe.wait_ge(z_free, 2 * bi + bj // 2 + 1)
                    elif bs == 0:
                        pe.wait_ge(a_ready, 2 * bi + bj // 2 + 1)
                    elif bs == 1:
                        pe.wait_ge(z_free, KC + 3 * bi + bj + 1)
                    else:
                        pe.wait_ge(g_ready, 4 * bi + bj + 1)
                if s == 2 and i == 0 and j == 3:
                    pe.wait_ge(vT_lo, 2 * KC)
                if (s, i, j) == (0, 0, 3):
                    pe.wait_ge(mlp_arg, 3)
                for k in range(KD):
                    if (s, i, j) == (0, 0, 0):
                        pe.wait_ge(hT_lo, max(2 * KD - 2, KD + k + 1))
                    for q in range(2):
                        mm = product(PS[:, 2 * j + q, :], (SPLIT[j][0][:, k, :], SPLIT[j][1][:, k, :]),
                                     (HT[0][:, k, q * L:(q + 1) * L], HT[1][:, k, q * L:(q + 1) * L]), k == 0, k == KD - 1)
                mm.then_inc(w_used, 1)
                if s == 0 and i == 0 and j < 2:
                    filter_layer(j + 1)
                if s == 1 and j == 2:
                    pe.wait_ge(v_ready, i + 1)
                    if i == 0:
                        pe.wait_ge(a_ready, KC)
                    for q in range(2):
                        ge(pe, vT_lo, 2 * (i - 1) + q + 1)
                        for t in range(LT):
                            mm = nc.tensor.transpose(PS[:, 6 + q, t * P:(t + 1) * P], SHORTS[1][:, q, t * P:(t + 1) * P], IDENT)
                        mm.then_inc(vT_mm, 1)

            pe.wait_ge(conv_done, KC)
            pe.wait_ge(ones_set, 4)
            pe.wait_ge(g_ready, 4 * SECTIONS[2][0] - 3)

            def channel_sums(ct):
                for q in range(2):
                    mm = nc.tensor.matmul(PS[:, q, :], ONES[:], CONV[:, ct, q, :], start=ct == 0, stop=ct == KC - 1)
                return mm

            for ct in range(KC // 2):
                channel_sums(ct)

            pe.wait_ge(g_ready, 4 * SECTIONS[2][0])
            pe.wait_ge(w4_in, 16)

            def taps(lt):
                ge(pe, taps_ready, lt)
                for q in range(2):
                    mm = nc.tensor.matmul(PS[:, 4 + q, :], FH[2][:, lt * P:(lt + 1) * P], W4[:, q * DC:(q + 1) * DC],
                                          start=True, stop=True)
                mm.then_inc(taps_mm, 1)

            def norm(lt):
                pe.wait_ge(abs_ready, lt + 1)
                for q in range(2):
                    mm = nc.tensor.matmul(PS[:, 6, :], ONES[:], HABS[:, q * DC:(q + 1) * DC],
                                          start=lt == 0 and q == 0, stop=lt == LT - 1 and q == 1)
                mm.then_inc(norm_mm, 1)

            for lt in range(LT):
                taps(lt)
                if lt:
                    norm(lt - 1)
            norm(LT - 1)
            for ct in range(KC // 2, KC):
                mm = channel_sums(ct)
            mm.then_inc(ln_mm, 1)
            pe.wait_ge(norm_row, 1)
            for ct in range(KC):
                mm = nc.tensor.matmul(PS[:, 7, ct:ct + 1], NROW[:, ct * P:(ct + 1) * P], IDENT[0:1, 0:1], start=True, stop=True)
            mm.then_inc(norm_col, 1)

            def table_tile(table, n, f):
                return table[0][:, n, f * P:(f + 1) * P], table[1][:, n, f * P:(f + 1) * P]

            def spectrum(f):
                if f == 0:
                    pe.wait_ge(cos_lo, 1)
                    pe.wait_ge(sin_lo, 1)
                    pe.wait_ge(eo_lo, LT)
                elif f == 1:
                    pe.wait_ge(skip_norm, 1)
                    pe.wait_ge(norm_col, 2)
                else:
                    pe.wait_ge(k_ready, 2 * (f - 1))
                for q, table in enumerate((COS, SIN)):
                    bank = 4 + 2 * (f % 2) + q
                    for n in range(LT):
                        mm = product(PS[:, bank, :], table_tile(table, n, f), (EO[0][:, n, q, :], EO[1][:, n, q, :]),
                                     n == 0, n == LT - 1)
                mm.then_inc(k_mm, 1)

            spectrum(0)
            spectrum(1)
            for ct in range(KC):
                pe.wait_ge(ln_sq, ct + 1)
                for q in range(2):
                    mm = nc.tensor.matmul(PS[:, 2 + q, :], ONES[:], LNSQ[ct % 2][:, q, :], start=ct == 0, stop=ct == KC - 1)
                if ct < KC - 1:
                    mm.then_inc(ln_used, 1)
            mm.then_inc(ln_mm, 1)
            spectrum(2)
            spectrum(3)

            def transform(s, f):
                n = s * LT + f
                if n < 2:
                    pe.wait_ge(ln_root, 1)
                    pe.wait_ge(ln_x, KC)
                else:
                    pe.wait_ge(u_used, n - 1)
                for q, table in enumerate((COS, SIN)):
                    for m in range(LT):
                        mm = product(PS[:, 2 * (f % 2) + q, :], table_tile(table, m, f),
                                     (VT[0][:, s * LT + m, :], VT[1][:, s * LT + m, :]), m == 0, m == LT - 1)
                mm.then_inc(u_mm, 1)

            def back(s, f):
                if f == 0:
                    ge(pe, uy_ready, s * KC)
                    pe.wait_ge(k_ready, 2 * LT)
                for q, (y, table) in enumerate(((YRE, COS), (YIM, SIN))):
                    pe.wait_ge(y_lo, 2 * (s * LT + f) + q + 1)
                    for ct in range(KC):
                        part = slice(ct * P, (ct + 1) * P)
                        mm = product(PS[:, 4 + ct, :], (y[0][:, f, part], y[1][:, f, part]),
                                     (table[0][:, f, :], table[1][:, f, :]), f == 0 and q == 0, f == LT - 1 and q == 1)
                mm.then_inc(y_mm, 1)

            pe.wait_ge(vT_lo, 2 * KC)
            for f in range(LT):
                transform(0, f)
            transform(1, 0)
            back(0, 0)
            back(0, 1)
            back(0, 2)
            transform(1, 1)
            back(0, 3)
            transform(1, 2)
            transform(1, 3)
            for f in range(LT):
                back(1, f)

            pe.wait_ge(at_lo, KC)
            pe.wait_ge(u_used, 2 * LT)
            for n in range(2 * KD):
                j = n % 4
                pe.wait_ge(o_lo, n + 1)
                if n == 2:
                    pe.wait_ge(uy_ready, 2 * KC)
                ge(pe, m_free, n - 3)
                src = (AT, UB)[n % 2]
                if n == 1:
                    pe.wait_ge(ub_lo, 2 * KC)
                for k in range(KC):
                    for q in range(2):
                        mm = product(PS[:, 2 * j + q, :], (OUT_SPLIT[j][0][:, k, :], OUT_SPLIT[j][1][:, k, :]),
                                     (src[0][:, k, q, :], src[1][:, k, q, :]), k == 0, k == KC - 1)
                mm.then_inc(o_used, 1)

            def mixed(k, t):
                part = slice((t % LT) * P, (t % LT + 1) * P)
                return MT[0][:, k, t // LT, part], MT[1][:, k, t // LT, part]

            for k in range(KD):
                pe.wait_ge(o_lo, 2 * KD + k + 1)
                pe.wait_ge(m_lo, k + 1)
                for t in range(TT):
                    if k == 0:
                        pe.wait_ge(m_free, 2 * KD - 2 + max(t // 2 - 1, 0))
                    mm = product(PS[:, t, :], mixed(k, t), (WO_SPLIT[wo_slot(k)][0][:], WO_SPLIT[wo_slot(k)][1][:]),
                                 k == 0, k == KD - 1)
                    if k == KD - 1:
                        mm.then_inc(x2_mm, 1)
                    elif t == TT - 1:
                        mm.then_inc(o_used, 1)

            def logits(t):
                pe.wait_ge(x2T_ready, x2T_count(1, t))
                if t == 0:
                    pe.wait_ge(router_ready, 1)
                for k in range(KD):
                    mm = nc.tensor.matmul(PS[:, 2, t * E:(t + 1) * E], X2T[t % 2][:, k, :], ROUTER[:, k, :],
                                          start=k == 0, stop=k == KD - 1)
                mm.then_inc(logits_mm, 1)

            def second_half(t):
                pe.wait_ge(x2_ready, t + 1 if t < 2 else TT + t - 1)
                for k in range(KD):
                    if t == 0:
                        pe.wait_ge(o_lo, 3 * KD + k + 1)
                    if k == KD // 2 and t >= 2:
                        logits(t - 2)
                    slot = WO_SPLIT[wo_slot(KD + k)]
                    mm = product(PS[:, t % 2, :], mixed(k, t), (slot[0][:], slot[1][:]), k == 0, k == KD - 1)
                mm.then_inc(x2_mm, 1)

            def x2_T(h, t):
                pe.wait_ge(x2_ready, TT + h * (t + 1))
                if t >= 2:
                    pe.wait_ge(x2T_ready, x2T_count(h, t - 2))
                for k in range(4):
                    mm = nc.tensor.transpose(PS[:, 4 + 2 * (t % 2) + h, k * P:(k + 1) * P],
                                             X2[:, t, (4 * h + k) * P:(4 * h + k + 1) * P], IDENT)
                mm.then_inc(x2T_mm, 1)

            for t in range(TT + 1):
                if t < TT:
                    second_half(t)
                    x2_T(0, t)
                if t:
                    x2_T(1, t - 1)
            logits(TT - 2)
            logits(TT - 1)
            pe.wait_ge(aff_ready, 2)
            for t in range(LT):
                mm = nc.tensor.transpose(PS[0:48, 3, t * P:(t + 1) * P], AFFW[:, t, :], IDENT)
            mm.then_inc(affT_mm, 1)
            pe.wait_ge(pair_ready, 2)
            for q in range(2):
                nc.tensor.transpose(PS[:, q, 0:E], PAIR[:, q, :], IDENT[0:E, 0:E]).then_inc(slots_mm, 1)

            def tokens_of(e):
                pe.wait_ge(xs_in, (e + 1) * 16)
                for k in range(KD):
                    mm = nc.tensor.transpose(PS[:, 6 + k // 4, (k % 4) * P:(k % 4 + 1) * P], XS[:, k * P:(k + 1) * P], IDENT)
                mm.then_inc(xsT_mm, 1)

            def hidden_T(c, e):
                pe.wait_ge(hid_ready, NF * e + c + 1)
                for t in range(FC[c][1] // P):
                    mm = nc.tensor.transpose(PS[:, 6, t * P:(t + 1) * P], HID[:, t * P:(t + 1) * P], IDENT)
                mm.then_inc(hidT_mm, 1)

            def gate_up(c, e, base):
                for n, (kind, cc, kh) in enumerate(BODY):
                    if kind == "down" or cc != c:
                        continue
                    w = FC[c][1]
                    q, r = pos_mod(n, e, SPLITS), slot_of(n, e)
                    pe.wait_ge(e_lo, base + pos(n, e) + 1)
                    bank = 0 if kind == "gate" else 1
                    if kh == 0 and kind == "gate":
                        ge(pe, hid_ready, NF * e + c)
                    for t in range(4):
                        k = 4 * kh + t
                        mm = product(PS[:, bank, 0:w], (XST[0][:, k, :], XST[1][:, k, :]),
                                     (ES[q][:, t, 0:w], EL[r][:, t, 0:w]), k == 0, k == KD - 1)
                    mm.then_inc(e_used, 1)

            def down(c, e, counts):
                tiles = FC[c][1] // P
                pe.wait_ge(hidT_lo, NF * e + c + 1)
                if c == 0:
                    ge(pe, ye_ready, e)
                for dh in range(2):
                    count, q, r = counts[dh]
                    pe.wait_ge(e_lo, count + 1)
                    for t in range(tiles):
                        mm = product(PS[:, 4 + dh, :], (HIDT[0][:, t, :], HIDT[1][:, t, :]),
                                     (ES[q][:, t, :], EL[r][:, t, :]), c == 0 and t == 0, c == NF - 1 and t == tiles - 1)
                    mm.then_inc(e_used, 1)

            def down_counts(c, e, base):
                ns = [BODY.index(("down", c, dh)) for dh in range(2)]
                return [(base + pos(n, e), pos_mod(n, e, SPLITS), slot_of(n, e)) for n in ns]

            def pe_body(e, base, first, last):
                gate_up(0, e, base)
                if not first:
                    down(2, e - 1, down_counts(2, e, base))
                hidden_T(0, e)
                gate_up(1, e, base)
                down(0, e, down_counts(0, e, base))
                hidden_T(1, e)
                gate_up(2, e, base)
                pe.wait_ge(hidT_lo, NF * e + 2)
                if not last:
                    tokens_of(e + 1)
                down(1, e, down_counts(1, e, base))
                if not last:
                    pe.wait_ge(xsT_lo, e + 2)
                hidden_T(2, e)

            tokens_of(0)
            pe.wait_ge(xsT_lo, 1)
            pe_body(0, 0, True, False)
            with pe.Fori(1, E - 1) as e:
                pe_body(e, e * NB - SKIPPED, False, False)
            pe_body(E - 1, (E - 1) * NB - SKIPPED, False, True)
            base = E * NB - SKIPPED
            down(2, E - 1, [(base + dh, (base + dh) % SPLITS, (base + dh) % RAWS) for dh in range(2)])


def kernel(**inputs):
    import numpy as np
    import concourse.bacc as bacc
    from concourse.bass_utils import run_bass_kernel_spmd

    def w(name):
        return np.asarray(inputs[name])[0]

    f32 = np.float32
    xp, xs = np.asarray(inputs["x_prompt"])[0], np.asarray(inputs["x_sample"])[0]
    L, D = xp.shape
    DC = w("conv_w_out").shape[0]
    PROJ = w("w_in").shape[1]
    E = w("router_w").shape[1]
    TAPS, SHORT = w("conv_dw_w").shape[0], w("hy_short_w").shape[0]

    def columns(a):
        return a.reshape(-1, P).T

    def columns_taps(a):
        return a.reshape(a.shape[0], -1, P).transpose(2, 1, 0).reshape(P, -1)

    f = np.arange(L)
    half = np.pi * (2 * f + 1) / (4 * L)
    angle = np.pi * np.outer(2 * f + 1, 2 * f + 1) / (4 * L)
    parts = {
        "b_in": columns(w("b_in")), "dw_w": columns_taps(w("conv_dw_w")), "dw_b": columns(w("conv_dw_b")),
        "ln_g": columns(w("conv_ln_g")), "ln_b": columns(w("conv_ln_b")), "conv_b": columns(w("conv_b_out")),
        "short_w": columns_taps(w("hy_short_w")), "short_b": columns(w("hy_short_b")), "hy_b": columns(w("hy_b_out")),
        "norm1": columns(w("norm1_g")), "norm2": columns(w("norm2_g")), "cos_half": columns(np.cos(half).astype(f32)),
        "sin_half": columns(np.sin(half).astype(f32)),
        "router": w("router_w").reshape(-1, P, E).transpose(1, 0, 2).reshape(P, -1), "ident": np.eye(P, dtype=f32),
    }
    where, _ = small_columns(D, DC, PROJ, TAPS, SHORT, E)
    small = np.concatenate([parts[name] for name in where], axis=1)
    w1 = w("hy_f_w1")
    N = w1.shape[1]
    ffn = np.concatenate([np.concatenate([w1, np.zeros((N - w1.shape[0], N), f32)]), w("hy_f_w2"), w("hy_f_w3"),
                          np.stack([w("hy_f_b1"), w("hy_f_b2"), w("hy_f_b3"), w("hy_f_freq")], axis=1)], axis=1)
    bands_n = (w1.shape[0] - 1) // 2
    time = np.linspace(0.0, 1.0, L, dtype=f32)[:, None]
    turn = (f32(2.0 * math.pi) * np.arange(L, dtype=f32)[:, None] / f32(L)).astype(f32)
    bands = np.linspace(1e-4, bands_n - 1, bands_n, dtype=f32)[None, :]
    zpos = np.concatenate([time, np.cos(bands * turn), -np.sin(bands * turn)], axis=1).astype(f32).T
    deltas = np.linspace(math.log(1e-2) / 1.5, math.log(1e-2) / 0.3, DC, dtype=f32)
    decay = np.exp(-time * np.abs(deltas)[None, :]).astype(f32)
    arrays = {
        "x_prompt": xp, "x_sample": xs, "small": small, "ffn": ffn, "ffn_w4": w("hy_f_w4"), "zpos": zpos, "decay": decay,
        "cosine": np.cos(angle).astype(f32), "sine": np.sin(angle).astype(f32),
        "w_in": w("w_in"), "conv_w_out": w("conv_w_out"), "hy_w_out": w("hy_w_out"), "w_o": w("w_o"),
        "hy_skip": np.asarray(inputs["hy_skip"]), "norm2_g": np.asarray(inputs["norm2_g"]),
        "norm_f_g": np.asarray(inputs["norm_f_g"]).reshape(1, D),
        "w_gate": w("exp_w_gate"), "w_up": w("exp_w_up"), "w_down": w("exp_w_down"),
    }
    arrays = {f"in_{k}": np.ascontiguousarray(v) for k, v in arrays.items()}
    nc = bacc.Bacc("TRN2", target_bir_lowering=False, num_devices=1)
    args = [nc.dram_tensor(k, a.shape, mybir.dt.from_np(a.dtype), kind="ExternalInput").ap() for k, a in arrays.items()]
    args += [nc.dram_tensor(k, (L, D), F32, kind="ExternalOutput").ap() for k in ("out_prompt", "out_sample")]
    hybrid_encoder_kernel(nc, *args)
    result = run_bass_kernel_spmd(nc, [arrays], core_ids=[0]).results[0]
    return result["out_prompt"].reshape(1, L, D), result["out_sample"].reshape(1, L, D)
```
